# Optimizing a Trainium2 kernel written in Bass

```python
import jax, jax.numpy as jnp
from jax import lax
import numpy as np

D_MODEL = 1024
BATCH = 1
SEQ = 2048
DEPTH = 1
DEC_BATCH = 8
DEC_SEQ = 8
PAST_LEN = 4096
PAGE_SIZE = 128

HD = 64
N_ATT_HEADS = D_MODEL // 128
ATT_WIDTH = N_ATT_HEADS * HD
MLSTM_HEADS = 4
MLSTM_WIDTH = D_MODEL - ATT_WIDTH
MLSTM_HD = MLSTM_WIDTH // MLSTM_HEADS
ROT_DIM = HD // 4
ROPE_THETA = 500000.0
DILATED = ((128, 1), (512, 4), (2048, 16))
MAX_WINDOW = 2048
BLOCK = 128
CONV_W = 4
CHUNK = 128
D_FF = 4 * D_MODEL
EPS = 1e-6
IN_SIZES = (ATT_WIDTH, ATT_WIDTH, ATT_WIDTH, 2 * MLSTM_WIDTH, MLSTM_WIDTH, MLSTM_WIDTH, 2 * MLSTM_HEADS)
IN_COLS = sum(IN_SIZES)
IN_SPLITS = tuple(int(s) for s in np.cumsum(IN_SIZES)[:-1])

kernel_name = 'dilated_swa_mlstm_hybrid_step'

def rms_norm(x, g):
    xf = x.astype(jnp.float32)
    y = xf * lax.rsqrt(jnp.mean(xf * xf, axis=-1, keepdims=True) + EPS)
    return (y * g.astype(jnp.float32)).astype(x.dtype)

def rotary(x, pos):
    half = ROT_DIM // 2
    inv_freq = ROPE_THETA ** (-jnp.arange(half, dtype=jnp.float32) / half)
    ang = pos.astype(jnp.float32)[:, None] * inv_freq[None, :]
    cos = jnp.cos(ang)[None, :, None, :]
    sin = jnp.sin(ang)[None, :, None, :]
    x1 = x[..., :half].astype(jnp.float32)
    x2 = x[..., half:ROT_DIM].astype(jnp.float32)
    rot = jnp.concatenate([x1 * cos - x2 * sin, x2 * cos + x1 * sin], axis=-1).astype(x.dtype)
    return jnp.concatenate([rot, x[..., ROT_DIM:]], axis=-1)

def from_blocks(x, B, S, dil):
    L = S // dil
    rest = x.shape[3:]
    x = x.reshape((B, dil, -1) + rest)[:, :, :L]
    perm = (0, 2, 1) + tuple(range(3, x.ndim))
    return x.transpose(perm).reshape((B, S) + rest)

def banded_residue_attention(q, k, v, window, dil):
    B, S, H, Dh = q.shape
    L = S // dil
    nb = -(-L // BLOCK)
    Lp = nb * BLOCK
    sub_w = window // dil

    def to_blocks(x):
        x = x.reshape(B, L, dil, H, Dh).transpose(0, 2, 1, 3, 4).reshape(B * dil, L, H, Dh)
        x = jnp.pad(x, ((0, 0), (0, Lp - L), (0, 0), (0, 0)))
        return x.reshape(B * dil, nb, BLOCK, H, Dh)

    def with_prev(x):
        prev = jnp.pad(x[:, :-1], ((0, 0), (1, 0), (0, 0), (0, 0), (0, 0)))
        return jnp.concatenate([prev, x], axis=2)

    qb = to_blocks(q)
    kk = with_prev(to_blocks(k))
    vv = with_prev(to_blocks(v))
    s = jnp.einsum('bnqhd,bnkhd->bnhqk', qb, kk, preferred_element_type=jnp.float32)
    qi = jnp.arange(BLOCK)
    ki = jnp.arange(2 * BLOCK) - BLOCK
    rel = qi[:, None] - ki[None, :]
    start = jnp.arange(nb) * BLOCK
    valid = ((rel >= 0) & (rel <= sub_w))[None] & ((start[:, None, None] + ki[None, None, :]) >= 0)
    s = jnp.where(valid[None, :, None], s, -jnp.inf)
    mx = jnp.max(s, axis=-1, keepdims=True)
    p = jnp.exp(s - mx)
    den = jnp.sum(p, axis=-1)
    o = jnp.einsum('bnhqk,bnkhd->bnqhd', p.astype(v.dtype), vv, preferred_element_type=jnp.float32)
    o = o / jnp.swapaxes(den, 2, 3)[..., None]
    lse = jnp.swapaxes(mx[..., 0] + jnp.log(den), 2, 3)
    return from_blocks(o, B, S, dil), from_blocks(lse, B, S, dil)

def combine_by_denominator(outs, lses):
    w = jax.nn.softmax(jnp.stack(lses, 0), axis=0)
    return jnp.einsum('gbth,gbthd->bthd', w, jnp.stack(outs, 0))

def dilated_attention_prompt(q, k, v):
    outs, lses = [], []
    for window, dil in DILATED:
        o, lse = banded_residue_attention(q, k, v, window, dil)
        outs.append(o)
        lses.append(lse)
    return combine_by_denominator(outs, lses)

def dilated_attention_sample(q, kc, vc):
    B, T, H, Dh = q.shape
    W = kc.shape[1] - T
    ti = jnp.arange(T)
    outs, lses = [], []
    for window, dil in DILATED:
        j = jnp.arange(window // dil + 1)
        idx = W + ti[:, None] - dil * j[None, :]
        valid = idx >= 0
        idx = jnp.maximum(idx, 0)
        kg = kc[:, idx]
        vg = vc[:, idx]
        s = jnp.einsum('bthd,btjhd->bthj', q, kg, preferred_element_type=jnp.float32)
        s = jnp.where(valid[None, :, None, :], s, -jnp.inf)
        mx = jnp.max(s, axis=-1, keepdims=True)
        p = jnp.exp(s - mx)
        den = jnp.sum(p, axis=-1)
        o = jnp.einsum('bthj,btjhd->bthd', p.astype(vc.dtype), vg, preferred_element_type=jnp.float32)
        outs.append(o / den[..., None])
        lses.append(mx[..., 0] + jnp.log(den))
    return combine_by_denominator(outs, lses)

def mlstm_chunkwise(q, k, v, ig, lf, C0, n0, m0, chunk):
    B, T, H, D = q.shape
    nc = T // chunk
    to_c4 = lambda x: x.reshape(B, nc, chunk, H, D).transpose(1, 0, 3, 2, 4)
    to_c3 = lambda x: x.reshape(B, nc, chunk, H).transpose(1, 0, 3, 2)
    causal = jnp.tril(jnp.ones((chunk, chunk), dtype=bool))

    def step(carry, inp):
        C, n, m = carry
        qc, kc, vc, igc, lfc = inp
        b = jnp.cumsum(lfc, axis=-1)
        a = b + m[..., None]
        Dm = b[..., :, None] - b[..., None, :] + igc[..., None, :]
        Dm = jnp.where(causal, Dm, -jnp.inf)
        mt = jnp.maximum(a, jnp.max(Dm, axis=-1))
        w_inter = jnp.exp(a - mt)
        Wm = jnp.exp(Dm - mt[..., None])
        sc = jnp.einsum('bhtd,bhsd->bhts', qc, kc) * Wm
        num = w_inter[..., None] * jnp.einsum('bhtd,bhde->bhte', qc, C) + jnp.einsum('bhts,bhse->bhte', sc, vc)
        den = w_inter * jnp.einsum('bhtd,bhd->bht', qc, n) + jnp.sum(sc, axis=-1)
        h = num / jnp.maximum(jnp.abs(den), jnp.exp(-mt))[..., None]
        mT = mt[..., -1]
        wT_inter = jnp.exp(a[..., -1] - mT)
        wT = jnp.exp(b[..., -1:] - b + igc - mT[..., None])
        C_new = wT_inter[..., None, None] * C + jnp.einsum('bhs,bhsd,bhse->bhde', wT, kc, vc)
        n_new = wT_inter[..., None] * n + jnp.einsum('bhs,bhsd->bhd', wT, kc)
        return (C_new, n_new, mT), h

    (C1, n1, m1), hs = lax.scan(step, (C0, n0, m0), (to_c4(q), to_c4(k), to_c4(v), to_c3(ig), to_c3(lf)))
    h = hs.transpose(1, 0, 3, 2, 4).reshape(B, T, H, D)
    return h, C1, n1, m1

def mixer_block(h, pos, past, w_in, b_gate, w_conv, b_conv, mh_norm_g, w_out):
    B, T, _ = h.shape
    f32 = jnp.float32
    proj = jnp.einsum('btd,dc->btc', h, w_in)
    qa, ka, va, qk_raw, vb, ob, gates = jnp.split(proj, IN_SPLITS, axis=-1)
    qa = rotary(qa.reshape(B, T, N_ATT_HEADS, HD), pos) * (HD ** -0.5)
    ka = rotary(ka.reshape(B, T, N_ATT_HEADS, HD), pos)
    va = va.reshape(B, T, N_ATT_HEADS, HD)
    if past is None:
        att = dilated_attention_prompt(qa, ka, va)
        n_keep = min(MAX_WINDOW, T)
        new_k, new_v = ka[:, T - n_keep:], va[:, T - n_keep:]
        conv_buf = jnp.zeros((B, CONV_W - 1, 2 * MLSTM_WIDTH), h.dtype)
        C0 = jnp.zeros((B, MLSTM_HEADS, MLSTM_HD, MLSTM_HD), f32)
        n0 = jnp.zeros((B, MLSTM_HEADS, MLSTM_HD), f32)
        m0 = jnp.zeros((B, MLSTM_HEADS), f32)
        chunk = CHUNK if T % CHUNK == 0 else T
    else:
        win_k, win_v, conv_buf, C0, n0, m0 = past
        kc = jnp.concatenate([win_k.astype(ka.dtype), ka], axis=1)
        vc = jnp.concatenate([win_v.astype(va.dtype), va], axis=1)
        att = dilated_attention_sample(qa, kc, vc)
        n_keep = win_k.shape[1]
        new_k, new_v = kc[:, -n_keep:], vc[:, -n_keep:]
        C0, n0, m0 = C0.astype(f32), n0.astype(f32), m0.astype(f32)
        chunk = T
    xp = jnp.concatenate([conv_buf.astype(h.dtype), qk_raw], axis=1)
    conv = b_conv + sum(xp[:, w:w + T] * w_conv[w] for w in range(CONV_W))
    new_conv = xp[:, T:]
    qb, kb = jnp.split(jax.nn.silu(conv), 2, axis=-1)
    qb = qb.reshape(B, T, MLSTM_HEADS, MLSTM_HD).astype(f32)
    kb = kb.reshape(B, T, MLSTM_HEADS, MLSTM_HD).astype(f32) * (MLSTM_HD ** -0.5)
    vb = vb.reshape(B, T, MLSTM_HEADS, MLSTM_HD).astype(f32)
    ig, fg = jnp.split((gates + b_gate).astype(f32), 2, axis=-1)
    lf = jax.nn.log_sigmoid(fg)
    hb, C1, n1, m1 = mlstm_chunkwise(qb, kb, vb, ig, lf, C0, n0, m0, chunk)
    hb = hb * lax.rsqrt(jnp.mean(hb * hb, axis=-1, keepdims=True) + EPS)
    hb = hb * mh_norm_g.reshape(MLSTM_HEADS, MLSTM_HD).astype(f32)
    hb = hb * jax.nn.sigmoid(ob.reshape(B, T, MLSTM_HEADS, MLSTM_HD).astype(f32))
    mix = jnp.concatenate([att.reshape(B, T, ATT_WIDTH).astype(h.dtype), hb.reshape(B, T, MLSTM_WIDTH).astype(h.dtype)], axis=-1)
    out = jnp.einsum('btc,cd->btd', mix, w_out)
    dt = h.dtype
    return out, (new_k, new_v, new_conv, C1.astype(dt), n1.astype(dt), m1.astype(dt))

def sqrelu_mlp(h, w_up, w_down):
    u = jnp.einsum('btd,df->btf', h, w_up)
    return jnp.einsum('btf,fd->btd', jnp.square(jax.nn.relu(u)), w_down)

def setup_inputs(seed: int = 0) -> dict:
    key = jax.random.key(seed)
    ks = jax.random.split(key, 20)
    nrm = jax.random.normal
    wb = min(MAX_WINDOW, PAST_LEN)
    f_bias = jnp.linspace(3.0, 6.0, MLSTM_HEADS, dtype=jnp.float32)[None, :] + 0.1 * nrm(ks[9], (DEPTH, MLSTM_HEADS))
    i_bias = 0.1 * nrm(ks[10], (DEPTH, MLSTM_HEADS))
    return {
        'x_prompt': nrm(ks[0], (BATCH, SEQ, D_MODEL), jnp.float32),
        'x_sample': nrm(ks[1], (DEC_BATCH, DEC_SEQ, D_MODEL), jnp.float32),
        'cache_win_k': nrm(ks[2], (DEPTH, DEC_BATCH, wb, N_ATT_HEADS, HD), jnp.float32),
        'cache_win_v': nrm(ks[3], (DEPTH, DEC_BATCH, wb, N_ATT_HEADS, HD), jnp.float32),
        'state_conv': nrm(ks[4], (DEPTH, DEC_BATCH, CONV_W - 1, 2 * MLSTM_WIDTH), jnp.float32),
        'state_C': 0.2 * nrm(ks[5], (DEPTH, DEC_BATCH, MLSTM_HEADS, MLSTM_HD, MLSTM_HD), jnp.float32),
        'state_n': 0.2 * nrm(ks[6], (DEPTH, DEC_BATCH, MLSTM_HEADS, MLSTM_HD), jnp.float32),
        'state_m': jax.random.uniform(ks[7], (DEPTH, DEC_BATCH, MLSTM_HEADS), jnp.float32, 0.0, 4.0),
        'norm1_g': 1.0 + 0.01 * nrm(ks[8], (DEPTH, D_MODEL)),
        'w_in': nrm(ks[11], (DEPTH, D_MODEL, IN_COLS)) * D_MODEL ** -0.5,
        'b_gate': jnp.concatenate([i_bias, f_bias], axis=-1),
        'w_conv': nrm(ks[12], (DEPTH, CONV_W, 2 * MLSTM_WIDTH)) * CONV_W ** -0.5,
        'b_conv': 0.01 * nrm(ks[13], (DEPTH, 2 * MLSTM_WIDTH)),
        'mh_norm_g': 1.0 + 0.01 * nrm(ks[14], (DEPTH, MLSTM_WIDTH)),
        'w_out': nrm(ks[15], (DEPTH, D_MODEL, D_MODEL)) * D_MODEL ** -0.5,
        'norm2_g': 1.0 + 0.01 * nrm(ks[16], (DEPTH, D_MODEL)),
        'w_up': nrm(ks[17], (DEPTH, D_MODEL, D_FF)) * D_MODEL ** -0.5,
        'w_down': nrm(ks[18], (DEPTH, D_FF, D_MODEL)) * D_FF ** -0.5,
        'norm_f_g': 1.0 + 0.01 * nrm(ks[19], (D_MODEL,)),
    }

def reference(x_prompt, x_sample, cache_win_k, cache_win_v, state_conv, state_C, state_n, state_m,
              norm1_g, w_in, b_gate, w_conv, b_conv, mh_norm_g, w_out, norm2_g, w_up, w_down, norm_f_g):
    pos_p = jnp.arange(x_prompt.shape[1])
    pos_s = PAST_LEN + jnp.arange(x_sample.shape[1])
    hp, hs = x_prompt, x_sample
    st_p, st_s = [], []
    for l in range(DEPTH):
        params = (w_in[l], b_gate[l], w_conv[l], b_conv[l], mh_norm_g[l], w_out[l])
        a_p, sp = mixer_block(rms_norm(hp, norm1_g[l]), pos_p, None, *params)
        past = (cache_win_k[l], cache_win_v[l], state_conv[l], state_C[l], state_n[l], state_m[l])
        a_s, ss = mixer_block(rms_norm(hs, norm1_g[l]), pos_s, past, *params)
        hp = hp + a_p
        hs = hs + a_s
        hp = hp + sqrelu_mlp(rms_norm(hp, norm2_g[l]), w_up[l], w_down[l])
        hs = hs + sqrelu_mlp(rms_norm(hs, norm2_g[l]), w_up[l], w_down[l])
        st_p.append(sp)
        st_s.append(ss)
    y_prompt = rms_norm(hp, norm_f_g)
    y_sample = rms_norm(hs, norm_f_g)
    pk, pv, pconv, pC, pn, pm = (jnp.stack([s[i] for s in st_p], 0) for i in range(6))
    sk, sv, sconv, sC, sn, sm = (jnp.stack([s[i] for s in st_s], 0) for i in range(6))
    return (y_prompt, y_sample, pk, pv, pconv, pC, pn, pm, sk, sv, sconv, sC, sn, sm)


_drawn_inputs = setup_inputs


def setup_inputs(seed=0):
    import zlib

    import numpy as np

    out = dict(_drawn_inputs(seed))
    spreads = {}
    factors = {'norm1_g': 2.942,
     'mh_norm_g': 45.689,
     'norm2_g': 32.355,
     'norm_f_g': 32.677,
     'b_conv': 8.0}
    for name, (base, spread) in spreads.items():
        noise = np.random.default_rng([zlib.crc32(name.encode()), seed]).standard_normal(out[name].shape)
        drawn = base * np.exp(spread * noise) if base else spread * noise
        out[name] = __import__('jax').numpy.asarray(drawn.astype(out[name].dtype))
    for name, factor in factors.items():
        out[name] = (out[name] * factor).astype(out[name].dtype)
    return out
```

```python
import numpy as np
import concourse.bass as bass
from concourse import mybir
from contextlib import ExitStack

F32 = mybir.dt.float32
F32R = mybir.dt.float32r
BF16 = mybir.dt.bfloat16
ALU = mybir.AluOpType
ACT = mybir.ActivationFunctionType
AX = mybir.AxisListType

P = 128
D = 1024
KC = D // P
SEQ = 2048
DEC_B, DEC_T = 8, 8
NS = DEC_B * DEC_T
NT = SEQ + NS
TILES = SEQ // P + 1
ROWS = TILES * P
H, HD = 8, 64
AW = H * HD
ROT = HD // 4
MH, MD = 4, 128
MW = MH * MD
DFF = 4 * D
WB = 2048
EPS = 1e-6
NEG = -1.0e30
NCH = SEQ // P
QK, KK, VK, VB, OB = range(5)
CONVW = 4
LN_EXP = "natural_log_exp_and_others"


class Chain:

    def __init__(self, eng, sem):
        self.eng, self.sem, self.n, self.moved = eng, sem, 0, 0

    def mark(self, ins):
        ins.then_inc(self.sem, 1)
        self.n += 1

    def wait(self):
        self.eng.wait_ge(self.sem, self.n + self.moved)

    def link(self, ins):
        self.mark(ins)
        self.wait()

    def loop(self, trips, per):
        return _ChainLoop(self, trips, per)


class _ChainLoop:
    def __init__(self, chain, trips, per):
        self.chain, self.trips, self.per = chain, trips, per

    def __enter__(self):
        self.fori = self.chain.eng.Fori(0, self.trips)
        i = self.fori.__enter__()
        self.start = self.chain.n
        self.chain.moved = i * self.per
        return i

    def __exit__(self, *e):
        if e[0] is None:
            assert self.chain.n - self.start == self.per, (self.chain.n - self.start, self.per)
        self.chain.n = self.start + self.trips * self.per
        self.chain.moved = 0
        return self.fori.__exit__(*e)


class Norm:

    def __init__(self, nc, sem, tag, rows_of, xb, xn, small, gain, hi, lo, tr, ident, free=None):
        self.nc, self.rows_of, self.xb, self.xn, self.small, self.gain = nc, rows_of, xb, xn, small, gain
        self.hi, self.lo, self.tr, self.ident = hi, lo, tr, ident
        self.free = free
        self.x_in = [sem(f"{tag}_x_in{s}") for s in range(2)]
        self.ssq, self.var, self.root, self.xn_ready, self.turned, self.hi_ready, self.lo_ready = (
            sem(f"{tag}_{n}") for n in ("ssq", "var", "root", "xn", "turned", "hi", "lo"))

    def load(self, sp, T, s, first):
        if not first:
            sp.wait_ge(self.xn_ready, T - 1)
        sp.dma_start(self.xb[:, s], self.rows_of(T)).then_inc(self.x_in[s], 16)

    def act_stats(self, act, T, s, half, first):
        act.wait_ge(self.x_in[s], 16 * half + 16)
        if not first:
            act.wait_ge(self.turned, T - 1)
        q = self.small
        self.nc.scalar.activation(self.xn[:, s], self.xb[:, s], ACT.Square,
                                  accum_out=q[:, s, 0:1]).then_inc(self.ssq, 1)
        act.wait_ge(self.var, T + 1)
        self.nc.scalar.activation(q[:, s, 2:3], q[:, s, 1:2], ACT.Ln).then_inc(self.root, 1)
        act.wait_ge(self.root, 2 * T + 1)
        self.nc.scalar.activation(q[:, s, 3:4], q[:, s, 2:3], ACT.Exp, scale=-0.5).then_inc(self.root, 1)

    def dve_scale(self, dve, chain, T, s):
        v, q = self.nc.vector, self.small
        dve.wait_ge(self.ssq, T + 1)
        v.tensor_scalar(q[:, s, 1:2], q[:, s, 0:1], 1.0 / D, EPS, ALU.mult, ALU.add).then_inc(self.var, 1)
        dve.wait_ge(self.root, 2 * T + 2)
        chain.link(v.tensor_tensor(q[:, s, 4:5], q[:, s, 3:4], q[:, s, 3:4], ALU.mult))
        chain.link(v.tensor_tensor(q[:, s, 5:6], q[:, s, 4:5], q[:, s, 1:2], ALU.mult))
        chain.link(v.tensor_scalar(q[:, s, 6:7], q[:, s, 5:6], -0.5, 1.5, ALU.mult, ALU.add))
        chain.link(v.tensor_tensor(q[:, s, 7:8], q[:, s, 6:7], q[:, s, 3:4], ALU.mult))
        v.scalar_tensor_tensor(self.xn[:, s], self.xb[:, s], q[:, s, 7:8], self.gain[:],
                               ALU.mult, ALU.mult).then_inc(self.xn_ready, 1)

    def pe_turn(self, pe, T, s, first):
        pe.wait_ge(self.xn_ready, T + 1)
        if not first:
            pe.wait_ge(self.lo_ready, T - 1)
        for k in range(KC):
            last = self.nc.tensor.transpose(self.tr[2 * s + k // 4][:, (k % 4) * P:(k % 4 + 1) * P],
                                            self.xn[:, s, k * P:(k + 1) * P], self.ident[:])
        last.then_inc(self.turned, 1)

    def act_hi(self, act, T, s, col):
        act.wait_ge(self.turned, T + 1)
        if self.free:
            self.free(act)
        for half in range(2):
            last = self.nc.scalar.activation(self.hi[:, 4 * half:4 * half + 4, bass.ds(col, P)],
                                             self.tr[2 * s + half][:].rearrange("p (k c) -> p k c", k=4), ACT.Copy)
        last.then_inc(self.hi_ready, 1)

    def dve_lo(self, dve, T, s, col):
        dve.wait_ge(self.hi_ready, T + 1)
        for half in range(2):
            last = self.nc.vector.tensor_tensor(
                self.lo[:, 4 * half:4 * half + 4, bass.ds(col, P)],
                self.tr[2 * s + half][:].rearrange("p (k c) -> p k c", k=4),
                self.hi[:, 4 * half:4 * half + 4, bass.ds(col, P)].bitcast(F32), ALU.subtract)
        last.then_inc(self.lo_ready, 1)


    def sync_group(self, sp, T0, n):
        full = n // 2
        start = 0
        if T0 == 0:
            for t in range(2):
                self.load(sp, t, t, True)
            start = 1
        with sp.Fori(start, full) as i:
            for j in range(2):
                self.load(sp, T0 + 2 * i + j, j, False)
        if n % 2:
            self.load(sp, T0 + n - 1, 0, False)

    def act_group(self, act, T0, n):
        if T0 == 0:
            self.act_stats(act, 0, 0, 0, True)
            self.act_stats(act, 1, 1, 0, True)
            self.act_hi(act, 0, 0, 0)
            self.act_stats(act, 2, 0, 1, False)
            self.act_hi(act, 1, 1, P)
            T, left = 2, n - 2
        else:
            self.act_stats(act, T0, 0, T0 // 2, False)
            T, left = T0, n
        full = (left - 1) // 2
        with act.Fori(0, full) as i:
            for j in range(2):
                self.act_stats(act, T + 2 * i + j + 1, (j + 1) % 2, T // 2 + i + (j + 1) // 2, False)
                self.act_hi(act, T + 2 * i + j, j, (T - T0 + 2 * i + j) * P)
        for t in range(T + 2 * full, T0 + n):
            if t + 1 < T0 + n:
                self.act_stats(act, t + 1, (t + 1) % 2, (t + 1) // 2, False)
            self.act_hi(act, t, t % 2, (t - T0) * P)

    def dve_group(self, dve, chain, T0, n):
        self.dve_scale(dve, chain, T0, 0)
        full = (n - 1) // 2
        with chain.loop(full, 8) as i:
            for j in range(2):
                self.dve_scale(dve, chain, T0 + 2 * i + j + 1, (j + 1) % 2)
                self.dve_lo(dve, T0 + 2 * i + j, j, (2 * i + j) * P)
        for t in range(2 * full, n):
            if t + 1 < n:
                self.dve_scale(dve, chain, T0 + t + 1, (t + 1) % 2)
            self.dve_lo(dve, T0 + t, t % 2, t * P)

    def pe_group(self, pe, T0, n):
        start = 0
        if T0 == 0:
            for t in range(2):
                self.pe_turn(pe, t, t, True)
            start = 1
        with pe.Fori(start, n // 2) as i:
            for j in range(2):
                self.pe_turn(pe, T0 + 2 * i + j, j, False)
        if n % 2:
            self.pe_turn(pe, T0 + n - 1, 0, False)


def split_products(nc, out, pairs, last_inc=None):
    n = len(pairs)
    for k, (ah, al, bh, bl) in enumerate(pairs):
        nc.tensor.matmul(out, ah, bh, start=(k == 0), stop=False)
        nc.tensor.matmul(out, ah, bl, start=False, stop=False)
        ins = nc.tensor.matmul(out, al, bh, start=False, stop=(k == n - 1))
    if last_inc is not None:
        ins.then_inc(last_inc, 1)
    return ins


def project(K):
    nc, sem = K.nc, K.sem
    GT0, GN = (0, 8), (8, 9)
    SPLIT = 8 * P
    with ExitStack() as ctx:
        def sb(name, shape, dt=F32):
            return ctx.enter_context(nc.sbuf_tensor("p1_" + name, shape, dt))

        hT_hi = sb("hT_hi", [P, KC, 9 * P], F32R)
        hT_lo = sb("hT_lo", [P, KC, 9 * P], F32R)
        w_raw = sb("w_raw", [P, KC, 512])
        w_hi = [sb(f"w_hi{s}", [P, KC, 512], F32R) for s in range(2)]
        w_lo = [sb(f"w_lo{s}", [P, KC, 512], F32R) for s in range(2)]
        wq_raw = w_raw[:].rearrange("p k c -> p (k c)")[:, 0:KC * P]
        wq_hi = [w[:].rearrange("p k c -> p (k c)")[:, 0:KC * P].rearrange("p (k c) -> p k c", k=KC) for w in w_hi]
        wq_lo = [w[:].rearrange("p k c -> p (k c)")[:, 0:KC * P].rearrange("p (k c) -> p k c", k=KC) for w in w_lo]
        xb = sb("xb", [P, 2, D])
        xn = sb("xn", [P, 2, D])
        small = sb("small", [P, 2, 8])
        gain = sb("gain", [P, D])
        stage = sb("stage", [P, 3, AW])
        rot_a = sb("rot_a", [P, 2, H, ROT])
        rot_b = sb("rot_b", [P, 2, H, ROT])
        rot = sb("rot", [P, 2, TILES, 2 * ROT])
        wg_raw = sb("wg_raw", [P, KC, 8])
        wg_hi = sb("wg_hi", [P, KC, 8], F32R)
        wg_lo = sb("wg_lo", [P, KC, 8], F32R)
        bg = sb("bg", [P, 8])
        raw = sb("raw", [P, 2, 3 + SPLIT])
        sraw = sb("sraw", [P, 2, DEC_B, 3 + DEC_T])
        acc = sb("acc", [P, 2, SPLIT + NS])
        sig = xn[:].rearrange("p s d -> p (s d)")[:, 0:SPLIT + NS]
        wcv = sb("wcv", [P, 8, CONVW])
        bcv = sb("bcv", [P, 8])
        ksc = sb("ksc", [P, 8])
        ct = sb("ct", [P, 8, 27])
        stT = sb("stT", [P, 8, 24])
        st24, lastrows = sig[0:24, 0:8 * P], sig[0:27, 0:8 * P]
        bank = [ctx.enter_context(nc.psum_tensor(f"p1_bank{i}", [P, 512], F32)) for i in range(8)]
        ident = K.ident

        const_in, w_in, hi_ready, lo_ready = sem("p1_const_in"), sem("p1_w_in"), sem("p1_w_hi"), sem("p1_w_lo")
        wg_hi_ready, wg_lo_ready = sem("p1_wg_hi"), sem("p1_wg_lo")
        qk_mm, qk_out = sem("p1_qk_mm"), sem("p1_qk_evac")
        tok_mm, tok_ready, gate_mm, gate_ready = sem("p1_tok_mm"), sem("p1_tok_ready"), sem("p1_gate_mm"), sem("p1_gate_ready")
        conv_done, sig_done, conv_out = sem("p1_conv_done"), sem("p1_sig_done"), sem("p1_conv_out")
        stage_out = [sem(f"p1_stage_out{s}") for s in range(3)]
        acc_out = [sem(f"p1_acc_out{s}") for s in range(2)]
        gated, dve_own, pe_state, act_state = sem("p1_gated"), sem("p1_dve_own"), sem("p1_pe_state"), sem("p1_act_state")
        tail_zero, tail_mm, tail_ev, tail_out = sem("p1_tail_zero"), sem("p1_tail_mm"), sem("p1_tail_ev"), sem("p1_tail_out")
        xv = K.x.rearrange("(t p) d -> t p d", p=P)

        def hT_free(eng, g):
            if g:
                eng.wait_ge(tok_mm, 40)

        norm = Norm(nc, sem, "p1", lambda T: xv[T], xb, xn, small, gain, hT_hi, hT_lo,
                    [bank[4], bank[5], bank[6], bank[7]], ident)

        NPC = (2, 3)
        QB = (0, 16)

        block = ctx.enter_context(nc.Block(no_gpsimd_drain=True))

        @block.sync
        def _(sp):
            for dst, src in ((gain[:], K.norm1_g.partition_broadcast(P)), (rot[:], K.rot), (wg_raw[:], K.w_gate),
                             (bg[:], K.b_gate.partition_broadcast(P)), (wcv[:], K.w_conv), (bcv[:], K.b_conv),
                             (ksc[:], K.k_scale), (st24, K.state_conv)):
                sp.dma_start(dst, src).then_inc(const_in, 16)
            for g in range(2):
                norm.sync_group(sp, GT0[g], GN[g])
                base = 13 * g
                if g == 0:
                    sp.dma_start(wq_raw, K.w_qk[0]).then_inc(w_in, 16)
                with sp.Fori(1 - g, 8) as c:
                    sp.wait_ge(lo_ready, c + base)
                    sp.dma_start(wq_raw, K.w_qk[c]).then_inc(w_in, 16)
                with sp.Fori(0, 5) as b:
                    sp.wait_ge(lo_ready, b + (base + 8))
                    sp.dma_start(w_raw[:], K.w_tok[b]).then_inc(w_in, 16)

        @block.gpsimd
        def _(pool):
            nc.gpsimd.memset(ct[:], 0.0).then_inc(tail_zero, 1)
            pool.wait_ge(wg_hi_ready, 1)
            nc.gpsimd.tensor_tensor(wg_lo[:], wg_raw[:], wg_hi[:].bitcast(F32), ALU.subtract).then_inc(wg_lo_ready, 1)

            def lo(E, dst, hi, src):
                pool.wait_ge(hi_ready, E + 1)
                nc.gpsimd.tensor_tensor(dst, src, hi.bitcast(F32), ALU.subtract).then_inc(lo_ready, 1)

            qr = wq_raw.rearrange("p (k c) -> p k c", k=KC)
            for g in range(2):
                base = 13 * g
                with pool.Fori(0, 4) as i:
                    for j in range(2):
                        lo(base + 2 * i + j, wq_lo[j], wq_hi[j], qr)
                with pool.Fori(0, 2) as i:
                    for j in range(2):
                        lo(base + 8 + 2 * i + j, w_lo[j][:], w_hi[j][:], w_raw[:])
                lo(base + 12, w_lo[0][:], w_hi[0][:], w_raw[:])

        @block.scalar
        def _(act):
            act.wait_ge(const_in, 16 * 8)
            act.wait_ge(tail_zero, 1)
            nc.scalar.activation(wg_hi[:], wg_raw[:], ACT.Copy).then_inc(wg_hi_ready, 1)
            act.wait_ge(pe_state, 1)
            nc.scalar.activation(stT[:], bank[0][:, 0:8 * 24].rearrange("p (k c) -> p k c", k=8),
                                 ACT.Copy).then_inc(act_state, 1)
            act.wait_ge(act_state, 1)

            def w_round(E, dst, src, free=None):
                act.wait_ge(w_in, 16 * (E + 1))
                if free:
                    act.wait_ge(*free)
                nc.scalar.activation(dst, src, ACT.Copy).then_inc(hi_ready, 1)

            qr = wq_raw.rearrange("p (k c) -> p k c", k=KC)

            def evac(g, c, j, slot_used=True):
                n, qb = NPC[g], QB[g]
                if slot_used:
                    act.wait_ge(conv_out, 8 * g + c - 1)
                nc.scalar.activation(raw[:, j, 0:3], ct[:, bass.ds(c, 1), 0:3].rearrange("p a b -> p (a b)"), ACT.Copy)
                if g == 1:
                    nc.scalar.activation(sraw[:, j, :, 0:3],
                                         stT[:, bass.ds(c, 1), :].rearrange("p a (b w) -> p (a b) w", w=3), ACT.Copy)
                for q in range(2):
                    act.wait_ge(qk_mm, qb + n * c + q + 1)
                    nc.scalar.activation(raw[:, j, 3 + 512 * q:3 + 512 * (q + 1)], bank[q][:], ACT.Copy).then_inc(qk_out, 1)
                if g == 1:
                    act.wait_ge(qk_mm, qb + n * c + 3)
                    nc.scalar.activation(sraw[:, j, :, 3:3 + DEC_T],
                                         bank[2][:, 0:NS].rearrange("p (b t) -> p b t", b=DEC_B), ACT.Copy).then_inc(qk_out, 1)

            def squash(g, c, j):
                w = SPLIT + (NS if g else 0)
                act.wait_ge(conv_done, 8 * g + c + 1)
                nc.scalar.activation(sig[:, 0:w], acc[:, j, 0:w], ACT.Sigmoid).then_inc(sig_done, 1)

            def store(g, c, j):
                w = SPLIT + (NS if g else 0)
                act.wait_ge(conv_out, 8 * g + c + 1)
                act.dma_start(K.qkt[c, :, SPLIT * g:SPLIT * g + w], acc[:, j, 0:w]).then_inc(acc_out[j], 16)

            def keep(g, b, t, slot):
                T = GT0[g] + t
                act.wait_ge(tok_ready, 40 * g + b * GN[g] + t + 1)
                if b == OB:
                    nc.scalar.activation(stage[:, slot], stage[:, slot], ACT.Sigmoid).then_inc(gated, 1)
                    act.wait_ge(gated, T + 1)
                act.dma_start(K.proj[b, T * P:(T + 1) * P, :], stage[:, slot]).then_inc(stage_out[slot], 16)

            for g in range(2):
                n, base, nn = NPC[g], 13 * g, GN[g]
                norm.free = lambda e, g=g: hT_free(e, g)
                nc.scalar.preload_act_table_set(LN_EXP)
                norm.act_group(act, GT0[g], nn)
                w_round(base, wq_hi[0], qr, (tok_mm, 40) if g else None)
                w_round(base + 1, wq_hi[1], qr, (tok_mm, 32) if g else None)
                evac(g, 0, 0, g > 0)
                squash(g, 0, 0)
                w_round(base + 2, wq_hi[0], qr, (qk_mm, QB[g] + n))
                evac(g, 1, 1, g > 0)
                store(g, 0, 0)
                squash(g, 1, 1)
                with act.Fori(1, 3) as i:
                    for j in range(2):
                        w_round(base + 2 * i + j + 1, wq_hi[1 - j], qr, (qk_mm, QB[g] + n * (2 * i + j)))
                        evac(g, 2 * i + j, j)
                        store(g, 2 * i + j - 1, 1 - j)
                        squash(g, 2 * i + j, j)
                w_round(base + 7, wq_hi[1], qr, (qk_mm, QB[g] + n * 6))
                evac(g, 6, 0)
                store(g, 5, 1)
                squash(g, 6, 0)
                w_round(base + 8, w_hi[0][:], w_raw[:], (qk_mm, QB[g] + n * 7))
                evac(g, 7, 1)
                store(g, 6, 0)
                squash(g, 7, 1)
                store(g, 7, 1)
                R = 2 if g == 0 else 3
                w_round(base + 9, w_hi[1][:], w_raw[:], (qk_mm, QB[g] + n * 8))
                for t in range(nn):
                    keep(g, 0, t, t % R)
                w_round(base + 10, w_hi[0][:], w_raw[:], (tok_mm, 40 * g + nn))
                for t in range(nn):
                    keep(g, 1, t, t % R)
                w_round(base + 11, w_hi[1][:], w_raw[:], (tok_mm, 40 * g + 2 * nn))
                for t in range(nn):
                    keep(g, 2, t, t % R)
                w_round(base + 12, w_hi[0][:], w_raw[:], (tok_mm, 40 * g + 3 * nn))
                for t in range(nn):
                    keep(g, 3, t, t % R)
                for t in range(nn):
                    keep(g, 4, t, t % R)
            act.wait_ge(tail_mm, 1)
            for half in range(2):
                nc.scalar.activation(lastrows[:, 512 * half:512 * half + 512], bank[half][0:27, :],
                                     ACT.Copy).then_inc(tail_ev, 1)
            act.wait_ge(tail_ev, 2)
            act.dma_start(K.new_conv_prompt, lastrows[0:3, :]).then_inc(tail_out, 16)
            act.dma_start(K.new_conv_sample, lastrows[3:27, :]).then_inc(tail_out, 16)
            act.wait_ge(tail_out, 32)
            for s in range(3):
                act.wait_ge(stage_out[s], 16 * (15 + (20 if s < 2 else 0)))
            for s in range(2):
                act.wait_ge(acc_out[s], 16 * 8)

        @block.vector
        def _(dve):
            chain = Chain(dve, dve_own)
            v = nc.vector
            dve.wait_ge(const_in, 16 * 8)

            def conv(g, c, j, stored):
                dve.wait_ge(qk_out, QB[g] + NPC[g] * (c + 1))
                if stored is not None:
                    dve.wait_ge(acc_out[j], 16 * stored)
                views = [(raw[:, j, :], acc[:, j, 0:SPLIT], lambda a, w: a[:, w:w + SPLIT])]
                if g:
                    views.append((sraw[:, j], acc[:, j, SPLIT:SPLIT + NS].rearrange("p (b t) -> p b t", b=DEC_B),
                                  lambda a, w: a[:, :, w:w + DEC_T]))
                cw = [wcv[:, bass.ds(c, 1), w:w + 1].rearrange("p a b -> p (a b)") for w in range(CONVW)]
                cb = bcv[:, bass.ds(c, 1)]
                for src, dst, cut in views:
                    ins = v.tensor_scalar(dst, cut(src, 0), cw[0], cb, ALU.mult, ALU.add)
                chain.link(ins)
                for w in (1, 2, 3):
                    for src, dst, cut in views:
                        ins = v.scalar_tensor_tensor(dst, cut(src, w), cw[w], dst, ALU.mult, ALU.add)
                    if w < 3:
                        chain.link(ins)
                ins.then_inc(conv_done, 1)
                v.tensor_copy(ct[:, bass.ds(c, 1), 0:3].rearrange("p a b -> p (a b)"), raw[:, j, SPLIT:SPLIT + 3])
                if g:
                    v.tensor_copy(ct[:, bass.ds(c, 1), 3:27].rearrange("p a (b w) -> p (a b) w", w=3),
                                  sraw[:, j, :, DEC_T:DEC_T + 3])
                w = SPLIT + (NS if g else 0)
                dve.wait_ge(sig_done, 8 * g + c + 1)
                v.scalar_tensor_tensor(acc[:, j, 0:w], sig[:, 0:w], ksc[:, bass.ds(c, 1)], acc[:, j, 0:w],
                                       ALU.mult, ALU.mult).then_inc(conv_out, 1)

            def tile_out(g, b, t, kind):
                R = 2 if g == 0 else 3
                n = GN[g]
                slot, s, T = t % R, t % 2, GT0[g] + t
                ev = 40 * g + b * n + t
                dve.wait_ge(tok_mm, ev + 1)
                uses = (20 if g and slot < 2 else 0) + b * (n // R) + t // R
                if not (isinstance(uses, int) and uses == 0):
                    dve.wait_ge(stage_out[slot], 16 * uses)
                ps = bank[2 + s][:].rearrange("p (h d) -> p h d", h=H)
                st = stage[:, slot].rearrange("p (h d) -> p h d", h=H)
                half = ROT // 2

                def tab(lo, hi):
                    a = rot[:, bass.ds(kind, 1), T, lo:hi]
                    return a.broadcast_to([P, H, hi - lo])

                v.tensor_tensor(rot_a[:, s], ps[:, :, 0:ROT], tab(0, ROT), ALU.mult)
                v.tensor_tensor(rot_b[:, s, :, 0:half], ps[:, :, half:ROT], tab(ROT, ROT + half), ALU.mult)
                v.tensor_tensor(rot_b[:, s, :, half:ROT], ps[:, :, 0:half], tab(ROT + half, 2 * ROT), ALU.mult)
                chain.link(v.tensor_copy(stage[:, slot], bank[2 + s][:]))
                v.tensor_tensor(st[:, :, 0:ROT], rot_a[:, s], rot_b[:, s], ALU.add).then_inc(tok_ready, 1)

            for g in range(2):
                n = GN[g]
                norm.dve_group(dve, chain, GT0[g], n)
                dve.wait_ge(gate_mm, g + 1)
                v.tensor_tensor(K.gates[:, GT0[g]:GT0[g] + n, :],
                                bank[4][:, 0:8 * n].rearrange("p (t e) -> p t e", e=8),
                                bg[:].rearrange("p (a e) -> p a e", a=1).broadcast_to([P, n, 8]), ALU.add).then_inc(gate_ready, 1)
                if g == 0:
                    dve.wait_ge(tail_zero, 1)
                for c in range(2):
                    conv(g, c, c, 4 if g else None)
                with chain.loop(3, 6) as i:
                    for j in range(2):
                        conv(g, 2 * i + 2 + j, j, i + (4 * g + 1))
                with chain.loop(2, 2 * n) as i:
                    for j in range(2):
                        for t in range(n):
                            tile_out(g, 2 * i + j, t, i)
                for t in range(n):
                    tile_out(g, 4, t, 1)

        @block.tensor
        def _(pe):
            pe.wait_ge(const_in, 16 * 8)
            pe.wait_ge(K.ident_ready, K.ident_value)
            for k in range(8):
                last = nc.tensor.transpose(bank[0][:, 24 * k:24 * k + 24], st24[:, k * P:(k + 1) * P], ident[0:24, 0:24])
            last.then_inc(pe_state, 1)
            pe.wait_ge(act_state, 1)

            def chunk(g, c, j, opening=False):
                n = NPC[g]
                pe.wait_ge(lo_ready, c + (13 * g + 1))
                for q in range(n):
                    w = 512 if q < 2 else NS
                    if not opening:
                        pe.wait_ge(qk_out, n * c + (QB[g] - n + q + 1))
                    elif g:
                        pe.wait_ge(qk_out, QB[1])
                        pe.wait_ge(tok_ready, 40)
                    split_products(nc, bank[q][:, 0:w],
                                   [(wq_hi[j][:, k], wq_lo[j][:, k], hT_hi[:, k, 512 * q:512 * q + w],
                                     hT_lo[:, k, 512 * q:512 * q + w]) for k in range(KC)], qk_mm)

            def tokens(g, b, j):
                n = GN[g]
                pe.wait_ge(lo_ready, b + (13 * g + 9))
                for t in range(n):
                    ev = n * b + (40 * g + t)
                    pe.wait_ge(tok_ready, ev if t == 0 else ev - 1)
                    split_products(nc, bank[2 + t % 2][:],
                                   [(hT_hi[:, k, t * P:(t + 1) * P], hT_lo[:, k, t * P:(t + 1) * P],
                                     w_hi[j][:, k], w_lo[j][:, k]) for k in range(KC)], tok_mm)

            for g in range(2):
                n = GN[g]
                if g:
                    pe.wait_ge(gate_ready, 1)
                norm.pe_group(pe, GT0[g], n)
                pe.wait_ge(norm.lo_ready, GT0[g] + n)
                pe.wait_ge(wg_lo_ready, 1)
                for t in range(n):
                    ins = split_products(nc, bank[4][:, 8 * t:8 * t + 8],
                                         [(hT_hi[:, k, t * P:(t + 1) * P], hT_lo[:, k, t * P:(t + 1) * P],
                                           wg_hi[:, k], wg_lo[:, k]) for k in range(KC)])
                ins.then_inc(gate_mm, 1)
                chunk(g, 0, 0, True)
                chunk(g, 1, 1)
                with pe.Fori(1, 4) as i:
                    for j in range(2):
                        chunk(g, 2 * i + j, j)
                pe.wait_ge(qk_out, QB[g] + 8 * NPC[g])
                with pe.Fori(0, 2) as i:
                    for j in range(2):
                        tokens(g, 2 * i + j, j)
                tokens(g, 4, 0)
            pe.wait_ge(conv_out, 16)
            pe.wait_ge(qk_out, 16 + 24)
            for k in range(8):
                last = nc.tensor.transpose(bank[k // 4][0:27, (k % 4) * P:(k % 4 + 1) * P], ct[:, k, :], ident[:])
            last.then_inc(tail_mm, 1)


def gate_tables(K):
    nc, sem = K.nc, K.sem
    RP, RS = NCH * MH, DEC_B * MH
    R = RP + RS
    with ExitStack() as ctx:
        def sb(name, shape, dt=F32):
            return ctx.enter_context(nc.sbuf_tensor("gt_" + name, shape, dt))

        gT = sb("gT", [8, ROWS])
        t = {n: sb(n, [R, P]) for n in ("ig", "fg", "mag", "soft", "lf", "b", "u", "U", "g", "ng", "mt",
                                         "w_in", "e_mt", "w_T", "ones")}
        col = sb("col", [R, 8])
        BT, MP, NGT, WTI, MN = (col[:, k:k + 1] for k in range(5))
        ends = sb("ends", [MH, 2, NCH])
        msc = sb("msc", [MH, NCH + 1])
        bank = [ctx.enter_context(nc.psum_tensor(f"gt_bank{i}", [P, 512], F32)) for i in range(6)]
        names = ("turned", "evac", "own", "aown", "pad", "rows_in", "ends_out", "ends_in", "m_out", "m_in",
                 "tabs_out", "small_in", "fin", "pe_tab", "tab_ready", "act_step")
        s = {n: sem("gt_" + n) for n in names}
        g_dram = K.dram("gate_rows", (8, ROWS))
        ends_dram = K.dram("gate_ends", (2, RP))
        mprev_dram = K.dram("gate_mprev", (RP,))
        tab_dram = K.dram("gate_tab", (4, RS, DEC_T))
        wti_dram = K.dram("gate_wti", (R,))
        block = ctx.enter_context(nc.Block(no_gpsimd_drain=True))

        @block.tensor
        def _(pe):
            for k in range(TILES):
                last = nc.tensor.transpose(bank[k // 4][0:8, (k % 4) * P:(k % 4 + 1) * P], K.gates[:, k, :], K.ident[:])
            last.then_inc(s["turned"], 1)
            pe.wait_ge(s["act_step"], 7)
            for k, n in enumerate(("u", "w_in", "e_mt", "w_T")):
                last = nc.tensor.transpose(bank[5][:, RP * k:RP * (k + 1)], t[n][0:RP, :], K.ident[0:RP, 0:RP])
            last.then_inc(s["pe_tab"], 1)

        @block.gpsimd
        def _(pool):
            nc.gpsimd.memset(t["ig"][:], NEG).then_inc(s["pad"], 1)
            nc.gpsimd.memset(t["fg"][:], 1.0e30).then_inc(s["pad"], 1)
            nc.gpsimd.memset(t["ones"][:], 1.0).then_inc(s["pad"], 1)
            nc.gpsimd.memset(msc[:], 0.0).then_inc(s["pad"], 1)

        @block.sync
        def _(sp):
            sp.wait_ge(s["evac"], 5)
            sp.dma_start(g_dram, gT[:]).then_inc(s["rows_in"], 16)
            sp.wait_ge(s["rows_in"], 16)
            sp.wait_ge(s["pad"], 4)
            n = 1
            for row, name in ((0, "ig"), (MH, "fg")):
                for c in range(NCH):
                    sp.dma_start(t[name][MH * c:MH * (c + 1), :], g_dram[row:row + MH, c * P:(c + 1) * P]).then_inc(s["rows_in"], 16)
                for b in range(DEC_B):
                    sp.dma_start(t[name][RP + MH * b:RP + MH * (b + 1), 0:DEC_T],
                                 g_dram[row:row + MH, SEQ + DEC_T * b:SEQ + DEC_T * (b + 1)]).then_inc(s["rows_in"], 16)
                n += NCH + DEC_B
            sp.dma_start(MP[RP:R, :], K.ins["state_m"]).then_inc(s["small_in"], 16)
            with nc.allow_non_contiguous_dma(reason="a few words"):
                sp.wait_ge(s["own"], K.gt_own_scan)
                sp.dma_start(ends_dram[0].rearrange("(r a) -> r a", a=1), t["U"][0:RP, P - 1:P]).then_inc(s["ends_out"], 16)
                sp.dma_start(ends_dram[1].rearrange("(r a) -> r a", a=1), t["b"][0:RP, P - 1:P]).then_inc(s["ends_out"], 16)
                sp.wait_ge(s["ends_out"], 32)
                sp.dma_start(ends[:], ends_dram.rearrange("k (c h) -> h k c", h=MH)).then_inc(s["ends_in"], 16)
                sp.wait_ge(s["own"], K.gt_own_m)
                sp.dma_start(mprev_dram.rearrange("(c h) -> h c", h=MH), msc[:, 0:NCH]).then_inc(s["m_out"], 16)
                sp.dma_start(K.o["m_prompt"].rearrange("a b (h c) -> (a b h) c", c=1), msc[:, NCH:NCH + 1]).then_inc(s["fin"], 16)
                sp.wait_ge(s["m_out"], 16)
                sp.dma_start(MP[0:RP, :], mprev_dram.rearrange("(r a) -> r a", a=1)).then_inc(s["m_in"], 16)
                sp.wait_ge(s["own"], K.gt_own_g)
                sp.dma_start(K.ng_rows, t["ng"][0:RP, :]).then_inc(s["fin"], 16)
                sp.dma_start(K.ng_sample, t["ng"][RP:R, 0:DEC_T]).then_inc(s["fin"], 16)
                sp.wait_ge(s["own"], K.gt_own_mn)
                sp.dma_start(K.o["m_sample"].rearrange("a b (h c) -> (a b h) c", c=1), MN[RP:R, :]).then_inc(s["fin"], 16)
                sp.wait_ge(s["act_step"], 7)
                for k, n in enumerate(("u", "w_in", "e_mt", "w_T")):
                    sp.dma_start(tab_dram[k], t[n][RP:R, 0:DEC_T]).then_inc(s["tabs_out"], 16)
                sp.dma_start(wti_dram.rearrange("(r a) -> r a", a=1), WTI).then_inc(s["tabs_out"], 16)
                sp.wait_ge(s["tabs_out"], 80)
                sp.dma_start(K.wti[:], wti_dram.partition_broadcast(P)).then_inc(s["fin"], 16)
                for k in range(4):
                    for b in range(DEC_B):
                        sp.dma_start(K.tab_s[DEC_T * b:DEC_T * (b + 1), k, :],
                                     tab_dram[k, MH * b:MH * (b + 1), :].rearrange("h t -> t h")).then_inc(s["fin"], 16)
            sp.wait_ge(s["fin"], 16 * (5 + 4 * DEC_B))

        @block.scalar
        def _(act):
            nc.scalar.preload_act_table_set(LN_EXP)
            act.wait_ge(s["turned"], 1)
            for k in range(5):
                w = min(512, ROWS - 512 * k)
                nc.scalar.activation(gT[:, 512 * k:512 * k + w], bank[k][0:8, 0:w], ACT.Copy).then_inc(s["evac"], 1)
            act.wait_ge(s["rows_in"], 16 * (1 + 2 * (NCH + DEC_B)))
            act.wait_ge(s["pad"], 4)
            A = nc.scalar.activation
            own = Chain(act, s["act_step"])
            own.link(A(t["mag"][:], t["fg"][:], ACT.Abs))
            own.link(A(t["soft"][:], t["mag"][:], ACT.Exp, scale=-1.0))
            own.link(A(t["lf"][:], t["soft"][:], ACT.Ln, bias=1.0))
            act.wait_ge(s["own"], K.gt_own_g)
            act.wait_ge(s["m_in"], 16)
            act.wait_ge(s["small_in"], 16)
            own.mark(A(t["w_in"][:], t["g"][:], ACT.Exp, bias=MP, scale=-1.0))
            own.mark(A(t["e_mt"][:], t["mt"][:], ACT.Exp, scale=-1.0))
            own.mark(A(t["w_T"][:], t["u"][:], ACT.Exp, bias=NGT))
            own.mark(A(WTI, MP, ACT.Exp, bias=NGT))

        @block.vector
        def _(dve):
            v = nc.vector
            chain = Chain(dve, s["own"])
            dve.wait_ge(s["act_step"], 3)
            chain.link(v.scalar_tensor_tensor(t["lf"][:], t["fg"][:], 0.0, t["lf"][:], ALU.min, ALU.subtract))
            chain.link(v.tensor_tensor_scan(t["b"][:], t["ones"][:], t["lf"][:], 0.0, ALU.mult, ALU.add))
            chain.link(v.tensor_tensor(t["u"][:], t["ig"][:], t["b"][:], ALU.subtract))
            chain.link(v.tensor_tensor_scan(t["U"][:], t["u"][:], t["u"][:], -3.0e38, ALU.max, ALU.max))
            assert chain.n == K.gt_own_scan
            dve.wait_ge(s["ends_in"], 16)
            chain.link(v.tensor_tensor_scan(msc[:, 1:NCH + 1], ends[:, 0, :], ends[:, 1, :], 0.0, ALU.max, ALU.add))
            assert chain.n == K.gt_own_m
            dve.wait_ge(s["m_in"], 16)
            dve.wait_ge(s["small_in"], 16)
            chain.link(v.tensor_scalar(t["g"][:], t["U"][:], MP, None, ALU.max))
            chain.mark(v.tensor_scalar(t["ng"][:], t["g"][:], -1.0, None, ALU.mult))
            chain.link(v.tensor_tensor(t["mt"][:], t["b"][:], t["g"][:], ALU.add))
            chain.link(v.tensor_copy(NGT, t["ng"][:, P - 1:P]))
            assert chain.n == K.gt_own_g
            chain.link(v.tensor_copy(MN, t["mt"][:, P - 1:P]))
            assert chain.n == K.gt_own_mn
            dve.wait_ge(s["pe_tab"], 1)
            v.tensor_copy(K.tab_p[:], bank[5][:, 0:4 * RP].rearrange("p (k r) -> p k r", k=4)).then_inc(s["tab_ready"], 1)


def mix_prompt(K):
    nc, sem = K.nc, K.sem
    HW = HD + 2
    VW = MD + 1
    STEPS = 4
    NZ = 10
    ZERO = 9
    UNIT = [0] * 4 + [1] * 4 + [2] * 2
    FIRSTZ = (0, 4, 8)
    LASTZ = (3, 7, 9)
    with ExitStack() as ctx:
        def sb(name, shape, dt=F32):
            return ctx.enter_context(nc.sbuf_tensor("mx_" + name, shape, dt))

        q_in = [sb(f"q_in{a}", [P, AW]) for a in range(3)]
        k_in = [sb(f"k_in{a}", [P, AW]) for a in range(3)]
        v_in = [sb(f"v_in{a}", [P, 2, AW]) for a in range(3)]
        qz = [sb(f"qz{a}", [P, H, P]) for a in range(3)]
        kT = [sb(f"kT{a}", [P, 2, H // 2, P]) for a in range(3)]
        probs = sb("probs", [P, 2, 512])
        probsT = sb("probsT", [P, 2, 512])
        part = [sb(f"part{a}", [P, 2, H, HW]) for a in range(3)]
        mk = sb("mk", [P, 2, 2, P], BF16)
        mk1 = sb("mk1", [P, 4, 2, P], BF16)
        identb = sb("identb", [P, P], BF16)
        maskT = sb("maskT", [P, P])
        mq = sb("mq", [P, 2, MH, P])
        mkk = sb("mkk", [P, 2, MH, P])
        vx = sb("vx", [P, 2, MH, VW])
        gb = sb("gb", [P, 2, MH, P])
        ob = sb("ob", [P, 2, MW])
        mhg = sb("mhg", [P, MW])
        tb = sb("tb", [P, 4, MH])
        wt = sb("wt", [P, MH])
        arg = sb("arg", [P, MH, P])
        wm = sb("wm", [P, MH, P])
        scT = sb("scT", [P, MH, P])
        kw = sb("kw", [P, MH, P])
        num = sb("num", [P, MH, VW])
        C = sb("C", [P, MH, VW])
        hh = sb("hh", [P, MH, MD])
        sq = sb("sq", [P, MH, MD])
        hg = sb("hg", [P, MH, MD])
        gs = sb("gs", [P, MW])
        hb = sb("hb", [P, 2, MH, MD])
        sm = sb("sm", [P, 10, MH])
        bank = [ctx.enter_context(nc.psum_tensor(f"mx_bank{i}", [P, 512], F32)) for i in range(8)]

        s = {n: sem("mx_" + n) for n in (
            "turned", "scores", "probs_turned", "summed", "ml_scores", "ml_num", "ml_inter", "ml_dC",
            "turned_out", "exps", "ml_w", "ml_num_out", "ml_rms",
            "maxes", "probsT_out", "unit_out", "ml_arg", "ml_sc", "ml_kw", "ml_num_done", "ml_h", "ml_C", "ml_hb",
            "own", "pool_own", "gs", "sq", "hg", "consts", "zeros", "fin", "ml_ms", "gain_in")}
        unit_in = [sem(f"mx_unit_in{a}") for a in range(3)]
        ml_in = [sem(f"mx_ml_in{p}") for p in range(2)]
        part_out = [[sem(f"mx_part_out{a}{p}") for p in range(2)] for a in range(3)]
        hb_out = [sem(f"mx_hb_out{p}") for p in range(2)]

        qkt = K.qkt

        def view(t, a, i, j):
            if a == 0:
                return t[0:SEQ].rearrange("(n p) c -> n p c", p=P)[4 * i + j]
            if a == 1:
                return t[0:SEQ].rearrange("(b p r) c -> r b p c", p=P, r=4)[i, j]
            return t[0:SEQ].rearrange("(p r) c -> r p c", r=16)[4 * i + j]

        block = ctx.enter_context(nc.Block(no_gpsimd_drain=True))

        @block.sync
        def _(sp):
            def load_unit(a, i, j):
                sp.dma_start(q_in[a][:], view(K.proj[QK], a, i, j)).then_inc(unit_in[a], 16)
                sp.dma_start(k_in[a][:], view(K.proj[KK], a, i, j)).then_inc(unit_in[a], 16)
                sp.dma_start(v_in[a][:, j % 2 if a < 2 else 0], view(K.proj[VK], a, i, j)).then_inc(unit_in[a], 16)

            def load_ml(n, p):
                x = ml_in[p]
                sp.dma_start(mq[:, p], qkt[0:MH, :, bass.ds(n * P, P)].rearrange("h p t -> p h t")).then_inc(x, 16)
                sp.dma_start(mkk[:, p], qkt[MH:2 * MH, :, bass.ds(n * P, P)].rearrange("h p t -> p h t")).then_inc(x, 16)
                sp.dma_start(vx[:, p, :, 0:MD], K.proj[VB, bass.ds(n * P, P), :].rearrange("p (h d) -> p h d", h=MH)).then_inc(x, 16)
                sp.dma_start(gb[:, p], K.ng_rows[bass.ds(MH * n, MH), :].partition_broadcast(P)).then_inc(x, 16)
                sp.dma_start(ob[:, p], K.proj[OB, bass.ds(n * P, P), :]).then_inc(x, 16)

            def turn(i, j, more, more_ml):
                n = 4 * i + j
                for a in range(3):
                    sp.wait_ge(s["unit_out"], 3 * n + a + 1)
                    sp.dma_start(view(K.parts[a], a, i, j), part[a][:, j % 2].rearrange("p h c -> p (h c)"))\
                        .then_inc(part_out[a][j % 2], 16)
                    if more:
                        load_unit(a, i + (j + 1) // 4, (j + 1) % 4)
                sp.wait_ge(s["ml_hb"], n + 1)
                sp.dma_start(K.mix[bass.ds(n * P, P), AW:D], hb[:, j % 2].rearrange("p h d -> p (h d)"))\
                    .then_inc(hb_out[j % 2], 16)
                sp.wait_ge(s["ml_C"], n + 1)
                if more_ml:
                    load_ml(n + 2, j % 2)

            sp.dma_start(mhg[:], K.ins["mh_norm_g"].partition_broadcast(P)).then_inc(s["gain_in"], 16)
            sp.wait_ge(s["zeros"], ZERO)
            for a in range(3):
                load_unit(a, 0, 0)
            load_ml(0, 0)
            load_ml(1, 1)
            with sp.Fori(0, 3) as i:
                for j in range(STEPS):
                    turn(i, j, True, True)
            for j in range(STEPS):
                turn(3, j, j < 3, j < 2)
            sp.dma_start(K.o["C_prompt"][0, 0].rearrange("h d e -> d h e"), C[:, :, 0:MD]).then_inc(s["fin"], 16)
            with nc.allow_non_contiguous_dma(reason="the normaliser column"):
                sp.dma_start(K.o["n_prompt"][0, 0].rearrange("h (d e) -> d h e", e=1), C[:, :, MD:VW]).then_inc(s["fin"], 16)
            sp.wait_ge(s["fin"], 32)
            for a in range(3):
                for p in range(2):
                    sp.wait_ge(part_out[a][p], 16 * 8)
            for p in range(2):
                sp.wait_ge(hb_out[p], 16 * 8)

        @block.gpsimd
        def _(pool):
            g = nc.gpsimd
            own = Chain(pool, s["pool_own"])
            for a in range(3):
                g.memset(qz[a][:], 0.0).then_inc(s["zeros"], 1)
            for a in range(2):
                g.memset(kT[a][:], 0.0).then_inc(s["zeros"], 1)
                g.memset(v_in[a][:], 0.0).then_inc(s["zeros"], 1)
            g.memset(vx[:], 1.0).then_inc(s["zeros"], 1)
            g.memset(C[:], 0.0).then_inc(s["zeros"], 1)
            own.mark(g.memset(mk[:], 0.0))
            own.mark(g.memset(mk1[:], 0.0))
            own.mark(g.memset(maskT[:], 0.0))
            own.mark(g.tensor_copy(identb[:], K.ident[:]))
            own.wait()

            def keep_where(t, step, mult):
                own.mark(g.affine_select(out=t, in_=t, compare_op=ALU.is_ge, fill=NEG, base=0,
                                         pattern=[[step, P]], channel_multiplier=mult))

            for p in range(2):
                keep_where(mk[:, p, p], -1, 1)
                keep_where(mk[:, p, 1 - p], 1, -1)
            for i in range(4):
                keep_where(mk1[:, i, 0], -1, 1)
                if i:
                    keep_where(mk1[:, i, 1], 1, -1)
            own.mark(g.memset(mk1[:, 0, 1], NEG))
            keep_where(maskT[:], 1, -1)
            own.wait()
            g.memset(sm[:, 9], 0.0).then_inc(s["consts"], 1)
            pool.wait_ge(s["gain_in"], 16)
            with pool.Fori(0, 4) as i:
                for j in range(STEPS):
                    n, p = 4 * i + j, j % 2
                    pool.wait_ge(ml_in[p], 80 * (2 * i + j // 2 + 1))
                    pool.wait_ge(s["hg"], n)
                    g.tensor_tensor(gs[:], ob[:, p], mhg[:], ALU.mult).then_inc(s["gs"], 1)
                    pool.wait_ge(s["ml_h"], n + 1)
                    g.tensor_tensor(sq[:], hh[:], hh[:], ALU.mult).then_inc(s["sq"], 1)
                    pool.wait_ge(s["gs"], n + 1)
                    g.tensor_tensor(hg[:].rearrange("p h d -> p (h d)"), hh[:].rearrange("p h d -> p (h d)"), gs[:],
                                    ALU.mult).then_inc(s["hg"], 1)

        @block.scalar
        def _(act):
            A = nc.scalar.activation
            nc.scalar.preload_act_table_set(LN_EXP)
            act.wait_ge(s["zeros"], ZERO)

            def q_out(a, n):
                act.wait_ge(s["turned"], 6 * n + (2 * a + 1))
                t = bank[4][:].rearrange("p (h c) -> p h c", h=4)
                for e in range(2):
                    r = slice(64 * e, 64 * e + 64)
                    ins = A(qz[a][r].rearrange("p (h e) c -> p h e c", e=2)[:, :, e], t[r], ACT.Copy, scale=HD ** -0.5)
                ins.then_inc(s["turned_out"], 1)

            def k_out(a, n, p):
                act.wait_ge(s["turned"], 6 * n + (2 * a + 2))
                A(kT[a][:, p if a < 2 else 0], bank[4][:].rearrange("p (h c) -> p h c", h=4), ACT.Copy).then_inc(s["turned_out"], 1)

            def exps(z, n, p):
                a = UNIT[z]
                w = 256 if a < 2 else P
                h0 = 2 * (z - FIRSTZ[a]) if a < 2 else 4 * (z - 8)
                act.wait_ge(s["maxes"], NZ * n + (z + 1))
                act.wait_ge(s["probs_turned"], NZ * n + max(z - 1, 0))
                for k in range(512 // w):
                    ins = A(probs[:, z % 2, w * k:w * (k + 1)], bank[z % 2][:, w * k:w * (k + 1)], ACT.Exp,
                            bias=part[a][:, p, h0 + k, HD:HD + 1], accum_out=part[a][:, p, h0 + k, HD + 1:HW])
                ins.then_inc(s["exps"], 1)

            with act.Fori(0, 4) as i:
                for j in range(STEPS):
                    n, p = 4 * i + j, j % 2
                    q_out(0, n)
                    k_out(0, n, p)
                    act.wait_ge(s["ml_arg"], n + 1)
                    for h in range(MH):
                        ins = A(wm[:, h], arg[:, h], ACT.Exp, bias=tb[:, 0, h:h + 1])
                    ins.then_inc(s["ml_w"], 1)
                    exps(0, n, p)
                    exps(1, n, p)
                    q_out(1, n)
                    exps(2, n, p)
                    k_out(1, n, p)
                    exps(3, n, p)
                    act.wait_ge(s["ml_num"], n + 1)
                    for e in range(2):
                        ins = A(num[:, 2 * e:2 * e + 2], bank[6 + e][:, 0:2 * VW].rearrange("p (h c) -> p h c", h=2), ACT.Copy)
                    ins.then_inc(s["ml_num_out"], 1)
                    exps(4, n, p)
                    q_out(2, n)
                    exps(5, n, p)
                    k_out(2, n, p)
                    for z in (6, 7, 8, 9):
                        exps(z, n, p)
                    act.wait_ge(s["ml_ms"], n + 1)
                    A(sm[:, 3], sm[:, 2], ACT.Ln).then_inc(s["ml_rms"], 1)
                    act.wait_ge(s["ml_rms"], 2 * n + 1)
                    A(sm[:, 4], sm[:, 3], ACT.Exp, scale=-0.5).then_inc(s["ml_rms"], 1)

        @block.vector
        def _(dve):
            v = nc.vector
            chain = Chain(dve, s["own"])
            dve.wait_ge(s["zeros"], ZERO)
            dve.wait_ge(s["consts"], 1)

            def bc(ap, w):
                return ap.rearrange("p (h a) -> p h a", a=1).broadcast_to([P, MH, w])

            def maxes(z, n, p, i, j):
                a = UNIT[z]
                w = 256 if a < 2 else P
                h0 = 2 * (z - FIRSTZ[a]) if a < 2 else 4 * (z - 8)
                if z in FIRSTZ:
                    dve.wait_ge(part_out[a][p], 16 * (2 * i + j // 2))
                dve.wait_ge(s["scores"], NZ * n + (z + 1))
                v.reduce_max(part[a][:, p, h0:h0 + 512 // w, HD:HD + 1], bank[z % 2][:].rearrange("p (h k) -> p h k", k=w),
                             AX.X, negate=True).then_inc(s["maxes"], 1)

            def pt_out(z, n):
                dve.wait_ge(s["probs_turned"], NZ * n + (z + 1))
                dve.wait_ge(s["summed"], NZ * n + max(z - 1, 0))
                v.tensor_copy(probsT[:, z % 2], bank[2 + z % 2][:]).then_inc(s["probsT_out"], 1)

            def unit_out(a, n, p):
                dve.wait_ge(s["summed"], NZ * n + (LASTZ[a] + 1))
                v.tensor_copy(part[a][:, p, :, 0:HD], bank[5][:].rearrange("p (h d) -> p h d", h=H)).then_inc(s["unit_out"], 1)

            with chain.loop(4, 4 * 9) as i:
                for j in range(STEPS):
                    n, p = 4 * i + j, j % 2
                    v.tensor_copy(tb[:], K.tab_p[:, :, bass.ds(MH * n, MH)])
                    v.tensor_copy(wt[:], K.wti[:, bass.ds(MH * n, MH)])
                    dve.wait_ge(ml_in[p], 80 * (2 * i + j // 2 + 1))
                    v.tensor_tensor(arg[:], gb[:, p], maskT[:].rearrange("p (a t) -> p a t", a=1).broadcast_to([P, MH, P]),
                                    ALU.add).then_inc(s["ml_arg"], 1)
                    dve.wait_ge(s["ml_arg"], n + 1)
                    maxes(0, n, p, i, j)
                    dve.wait_ge(s["ml_scores"], 2 * n + 2)
                    v.tensor_tensor(kw[:], bank[7][:].rearrange("p (h d) -> p h d", h=MH), bc(tb[:, 3], MD), ALU.mult).then_inc(s["ml_kw"], 1)
                    dve.wait_ge(s["ml_w"], n + 1)
                    v.tensor_tensor(scT[:], bank[6][:].rearrange("p (h t) -> p h t", h=MH), wm[:], ALU.mult).then_inc(s["ml_sc"], 1)
                    maxes(1, n, p, i, j)
                    pt_out(0, n)
                    maxes(2, n, p, i, j)
                    pt_out(1, n)
                    maxes(3, n, p, i, j)
                    pt_out(2, n)
                    maxes(4, n, p, i, j)
                    pt_out(3, n)
                    maxes(5, n, p, i, j)
                    pt_out(4, n)
                    unit_out(0, n, p)
                    maxes(6, n, p, i, j)
                    pt_out(5, n)
                    dve.wait_ge(s["ml_inter"], n + 1)
                    dve.wait_ge(s["ml_num_out"], n + 1)
                    for h in range(MH):
                        ins = v.scalar_tensor_tensor(num[:, h], bank[6 + h // 2][:, VW * (h % 2):VW * (h % 2 + 1)],
                                                     tb[:, 1, h:h + 1], num[:, h], ALU.mult, ALU.add)
                    ins.then_inc(s["ml_num_done"], 1)
                    maxes(7, n, p, i, j)
                    pt_out(6, n)
                    dve.wait_ge(s["ml_num_done"], n + 1)
                    chain.link(v.tensor_scalar(sm[:, 5], num[:, :, MD:VW].rearrange("p h a -> p (h a)"), -1.0, None, ALU.mult))
                    chain.link(v.tensor_tensor(sm[:, 6], sm[:, 5], num[:, :, MD:VW].rearrange("p h a -> p (h a)"), ALU.max))
                    chain.link(v.tensor_tensor(sm[:, 0], sm[:, 6], tb[:, 2], ALU.max))
                    chain.link(v.reciprocal(sm[:, 1], sm[:, 0]))
                    v.tensor_tensor(hh[:], num[:, :, 0:MD], bc(sm[:, 1], MD), ALU.mult).then_inc(s["ml_h"], 1)
                    maxes(8, n, p, i, j)
                    pt_out(7, n)
                    maxes(9, n, p, i, j)
                    pt_out(8, n)
                    unit_out(1, n, p)
                    dve.wait_ge(s["sq"], n + 1)
                    chain.link(v.reduce_sum(sm[:, 7], sq[:], AX.X))
                    v.tensor_scalar(sm[:, 2], sm[:, 7], 1.0 / MD, EPS, ALU.mult, ALU.add).then_inc(s["ml_ms"], 1)
                    pt_out(9, n)
                    dve.wait_ge(s["ml_dC"], n + 1)
                    for h in range(MH):
                        ins = v.scalar_tensor_tensor(C[:, h], C[:, h], wt[:, h:h + 1],
                                                     bank[6 + h // 2][:, VW * (h % 2):VW * (h % 2 + 1)], ALU.mult, ALU.add)
                    ins.then_inc(s["ml_C"], 1)
                    unit_out(2, n, p)
                    dve.wait_ge(s["ml_rms"], 2 * n + 2)
                    chain.link(v.tensor_tensor(sm[:, 5], sm[:, 4], sm[:, 4], ALU.mult))
                    chain.link(v.tensor_tensor(sm[:, 6], sm[:, 5], sm[:, 2], ALU.mult))
                    chain.link(v.tensor_scalar(sm[:, 7], sm[:, 6], -0.5, 1.5, ALU.mult, ALU.add))
                    chain.link(v.tensor_tensor(sm[:, 8], sm[:, 7], sm[:, 4], ALU.mult))
                    dve.wait_ge(s["hg"], n + 1)
                    dve.wait_ge(hb_out[p], 16 * (2 * i + j // 2))
                    v.tensor_tensor(hb[:, p], hg[:], bc(sm[:, 8], MD), ALU.mult).then_inc(s["ml_hb"], 1)

        @block.tensor
        def _(pe):
            mm, tp = nc.tensor.matmul, nc.tensor.transpose
            pe.wait_ge(s["zeros"], ZERO)
            pe.wait_ge(s["consts"], 1)

            def turn(a, which, n):
                k = 2 * a + which
                pe.wait_ge(unit_in[a], 48 * (n + 1))
                pe.wait_ge(s["turned_out"], 6 * n + k)
                src = (q_in, k_in)[which][a]
                for c in range(4):
                    ins = tp(bank[4][:, c * P:(c + 1) * P], src[:, c * P:(c + 1) * P], K.ident[:])
                ins.then_inc(s["turned"], 1)

            def scores(z, n, i, j):
                a, p = UNIT[z], j % 2
                out = bank[z % 2]
                pe.wait_ge(s["turned_out"], 6 * n + 2 * (a + 1))
                pe.wait_ge(s["exps"], NZ * n + max(z - 1, 0))
                if a < 2:
                    if j:
                        m = mk[:, p]
                    else:
                        m = mk1[:, bass.ds(i, 1)].rearrange("p a s k -> p (a s) k") if a == 0 else mk1[:, 0]
                    m = m.rearrange("p s k -> p (s k)").rearrange("p (a c) -> p a c", a=1).broadcast_to([P, 2, 256])
                    h0, w = 2 * (z - FIRSTZ[a]), 256
                    ks = lambda h: kT[a][:, :, h // 2, :]
                else:
                    m = mk[:, 0, 0].rearrange("p (a c) -> p a c", a=1).broadcast_to([P, 4, P])
                    h0, w = 4 * (z - 8), P
                    ks = lambda h: kT[a][:, 0, h // 2, :]
                mm(out[:], identb[:], m, start=True, stop=False, skip_group_check=True)
                for k in range(512 // w):
                    ins = mm(out[:, w * k:w * (k + 1)], qz[a][:, h0 + k], ks(h0 + k), start=False, stop=(k == 512 // w - 1),
                             skip_group_check=True)
                ins.then_inc(s["scores"], 1)

            def turn_probs(z, n):
                pe.wait_ge(s["exps"], NZ * n + (z + 1))
                pe.wait_ge(s["probsT_out"], NZ * n + max(z - 1, 0))
                for c in range(4):
                    ins = tp(bank[2 + z % 2][:, c * P:(c + 1) * P], probs[:, z % 2, c * P:(c + 1) * P], K.ident[:])
                ins.then_inc(s["probs_turned"], 1)

            def values(z, n):
                a = UNIT[z]
                pe.wait_ge(s["probsT_out"], NZ * n + (z + 1))
                if z in FIRSTZ:
                    pe.wait_ge(s["unit_out"], 3 * n + a)
                if a < 2:
                    for k in range(2):
                        h = 2 * (z - FIRSTZ[a]) + k
                        for b in range(2):
                            ins = mm(bank[5][:, HD * h:HD * (h + 1)], probsT[:, z % 2, (2 * k + b) * P:(2 * k + b + 1) * P],
                                     v_in[a][:, b, HD * h:HD * (h + 1)], start=(b == 0), stop=(b == 1))
                else:
                    for k in range(4):
                        h = 4 * (z - 8) + k
                        ins = mm(bank[5][:, HD * h:HD * (h + 1)], probsT[:, z % 2, k * P:(k + 1) * P],
                                 v_in[a][:, 0, HD * h:HD * (h + 1)], start=True, stop=True)
                ins.then_inc(s["summed"], 1)

            def pair(h):
                return bank[6 + h // 2][:, VW * (h % 2):VW * (h % 2 + 1)]

            with pe.Fori(0, 4) as i:
                for j in range(STEPS):
                    n, p = 4 * i + j, j % 2
                    turn(0, 0, n)
                    pe.wait_ge(ml_in[p], 80 * (2 * i + j // 2 + 1))
                    pe.wait_ge(s["ml_C"], n)
                    for h in range(MH):
                        ins = mm(bank[6][:, P * h:P * (h + 1)], mkk[:, p, h], mq[:, p, h], start=True, stop=True)
                    ins.then_inc(s["ml_scores"], 1)
                    turn(0, 1, n)
                    for h in range(MH):
                        ins = tp(bank[7][:, P * h:P * (h + 1)], mkk[:, p, h], K.ident[:])
                    ins.then_inc(s["ml_scores"], 1)
                    scores(0, n, i, j)
                    scores(1, n, i, j); turn_probs(0, n); turn(1, 0, n)
                    scores(2, n, i, j); turn_probs(1, n); values(0, n); turn(1, 1, n)
                    scores(3, n, i, j); turn_probs(2, n); values(1, n)
                    pe.wait_ge(s["ml_sc"], n + 1)
                    pe.wait_ge(s["ml_kw"], n + 1)
                    for h in range(MH):
                        ins = mm(pair(h), scT[:, h], vx[:, p, h], start=True, stop=True)
                    ins.then_inc(s["ml_num"], 1)
                    scores(4, n, i, j); turn_probs(3, n); values(2, n); turn(2, 0, n)
                    scores(5, n, i, j); turn_probs(4, n); values(3, n); turn(2, 1, n)
                    scores(6, n, i, j); turn_probs(5, n); values(4, n)
                    pe.wait_ge(s["ml_num_out"], n + 1)
                    for h in range(MH):
                        ins = mm(pair(h), mq[:, p, h], C[:, h], start=True, stop=True)
                    ins.then_inc(s["ml_inter"], 1)
                    scores(7, n, i, j); turn_probs(6, n); values(5, n)
                    scores(8, n, i, j); turn_probs(7, n); values(6, n)
                    scores(9, n, i, j); turn_probs(8, n); values(7, n)
                    turn_probs(9, n); values(8, n)
                    pe.wait_ge(s["ml_num_done"], n + 1)
                    for h in range(MH):
                        ins = mm(pair(h), kw[:, h], vx[:, p, h], start=True, stop=True)
                    ins.then_inc(s["ml_dC"], 1)
                    values(9, n)


KT = 13
KEYS = 12 * P + DEC_T
RT = H * DEC_T


def sample_tables():
    t = np.arange(DEC_T)[:, None]
    p = np.arange(P)
    pos = np.concatenate([16 * p + r for r in range(8)] + [WB - 512 + 4 * p + c for c in range(4)]
                         + [WB + np.arange(DEC_T)])[None, :]
    back = WB + t - pos
    part16 = np.zeros(KEYS, bool)
    part16[0:8 * P] = True
    new = np.zeros(KEYS, bool)
    new[12 * P:] = True
    d16 = (back >= 0) & (back % 16 == 0) & (back <= 2048) & (part16 | new)
    d4 = (back >= 0) & (back % 4 == 0) & (back <= 512) & ~part16
    d1 = (back >= 0) & (back <= 128) & ~part16
    count = d16.astype(np.float32) + d4 + d1
    assert (d1.sum(1) == 129).all() and (d4.sum(1) == 129).all() and (d16.sum(1) == 129).all()
    mask = np.where(count > 0, 0.0, NEG).astype(np.float32)
    return np.tile(mask, (H, 1)), np.tile(count.astype(np.float32), (H, 1))


def sample_chunk_tables():
    tok = np.arange(NS)
    b = tok // DEC_T
    ok = (b[:, None] == b[None, :]) & (tok[:, None] <= tok[None, :])
    return np.where(ok, 0.0, NEG).astype(np.float32), (b[:, None] == np.arange(DEC_B)[None, :]).astype(np.float32)


def mix_sample(K):
    nc, sem = K.nc, K.sem
    VW = MD + 1
    BH = DEC_B * MH
    S0 = SEQ
    with ExitStack() as ctx:
        def sb(name, shape, dt=F32):
            return ctx.enter_context(nc.sbuf_tensor("sm_" + name, shape, dt))

        kin = sb("kin", [P, 2, 12, AW])
        vin = sb("vin", [P, 2, 12, AW])
        knew = sb("knew", [DEC_T, 2, AW])
        vnew = sb("vnew", [DEC_T, 2, AW])
        kT = sb("kT", [P, H // 2, KEYS])
        mask = sb("mask", [RT, KEYS])
        count = sb("count", [RT, KEYS])
        pr = sb("pr", [RT, 2, KEYS])
        pT = sb("pT", [P, KT, RT])
        qs = kT[0:NS, 0, 0:AW]
        qT = sb("qT", [P, H // 2, NS])
        qbd = sb("qbd", [P, 2, H // 2, RT])
        osb = sb("osb", [RT, 2, AW])
        st = sb("st", [RT, 2, 4])
        free = {"k": [kin, 0], "v": [vin, 0]}

        def carve(which, parts, cols):
            t, at = free[which]
            flat = t[:].rearrange("p a b c -> p (a b c)")
            free[which][1] = at + cols
            assert at + cols <= 24 * AW
            return flat[0:parts, at:at + cols]

        Cs = carve("v", P, BH * VW).rearrange("p (e c) -> p e c", c=VW)
        mq = carve("k", P, MH * NS).rearrange("p (h t) -> p h t", h=MH)
        mkk = carve("k", P, MH * NS).rearrange("p (h t) -> p h t", h=MH)
        vx = carve("k", NS, MH * VW).rearrange("p (h c) -> p h c", h=MH)
        ngs = carve("k", NS, MH * NS).rearrange("p (h t) -> p h t", h=MH)
        arg = carve("k", NS, MH * NS).rearrange("p (h t) -> p h t", h=MH)
        wm = carve("k", NS, MH * NS).rearrange("p (h t) -> p h t", h=MH)
        scT = carve("k", NS, MH * NS).rearrange("p (h t) -> p h t", h=MH)
        qm = carve("k", P, MH * 576).rearrange("p (h x) -> p h x", h=MH)
        kwm = carve("v", NS, MH * DEC_B * MD).rearrange("p (h b d) -> p h b d", h=MH, b=DEC_B)
        kw = carve("k", NS, MW).rearrange("p (h d) -> p h d", h=MH)
        num = carve("k", NS, MH * VW).rearrange("p (h c) -> p h c", h=MH)
        obs = carve("k", NS, MW)
        mhg = carve("k", NS, MW)
        hh = carve("k", NS, MW).rearrange("p (h d) -> p h d", h=MH)
        sq = carve("k", NS, MW).rearrange("p (h d) -> p h d", h=MH)
        hb = osb[:, 0].rearrange("p (h d) -> p h d", h=MH)
        n32 = carve("v", BH, MD)
        maskS = carve("k", NS, NS)
        seq1 = carve("k", NS, DEC_B)
        sm = carve("k", NS, 10 * MH).rearrange("p (k h) -> p k h", h=MH)
        bank = [ctx.enter_context(nc.psum_tensor(f"sm_bank{i}", [P, 512], F32)) for i in range(8)]

        s = {n: sem("sm_" + n) for n in (
            "ml_in", "tab_in", "clear", "pe_ml", "act_ml", "own", "pool_own", "dC", "C_new", "hb_ready", "fin",
            "rows_out", "k_turned", "k_out_a", "k_out_d", "scores", "masked", "maxed", "exps", "counted",
            "p_turned", "pT_out", "summed", "o_ready", "q_ready", "ml_done")}
        k_in = [sem(f"sm_k_in{p}") for p in range(2)]
        v_in = [sem(f"sm_v_in{p}") for p in range(2)]
        o_out = [sem(f"sm_o_out{p}") for p in range(2)]
        block = ctx.enter_context(nc.Block(no_gpsimd_drain=True))
        NML = 9 + 2 * MH

        @block.sync
        def _(sp):
            x = s["ml_in"]
            sp.wait_ge(s["clear"], 3)
            sp.dma_start(mq, K.qkt[0:MH, :, SEQ:NT].rearrange("h p t -> p h t")).then_inc(x, 16)
            sp.dma_start(mkk, K.qkt[MH:2 * MH, :, SEQ:NT].rearrange("h p t -> p h t")).then_inc(x, 16)
            sp.dma_start(vx[:, :, 0:MD], K.proj[VB, S0:S0 + NS, :].rearrange("p (h d) -> p h d", h=MH)).then_inc(x, 16)
            for h in range(MH):
                sp.dma_start(ngs[:, h].rearrange("p (b t) -> p b t", b=DEC_B),
                             K.ng_sample.rearrange("(b h) t -> h b t", h=MH)[h].partition_broadcast(NS)).then_inc(x, 16)
            sp.dma_start(obs, K.proj[OB, S0:S0 + NS, :]).then_inc(x, 16)
            sp.dma_start(mhg, K.ins["mh_norm_g"].partition_broadcast(NS)).then_inc(x, 16)
            sp.dma_start(maskS, K.ins["chunk_mask"]).then_inc(x, 16)
            sp.dma_start(seq1, K.ins["token_seq"]).then_inc(x, 16)
            sp.dma_start(n32, K.ins["state_n"].rearrange("b h d -> (b h) d")).then_inc(x, 16)
            sp.dma_start(qs, K.proj[QK, S0:S0 + NS, :]).then_inc(x, 16)
            for h in range(MH):
                sp.dma_start(Cs.rearrange("p (b h) c -> p b h c", h=MH)[:, :, h, 0:MD],
                             K.ins["state_C"][:, h].rearrange("b d e -> d b e")).then_inc(x, 16)
            sp.dma_start(mask[:], K.ins["sample_mask"]).then_inc(s["tab_in"], 16)
            sp.dma_start(count[:], K.ins["sample_count"]).then_inc(s["tab_in"], 16)
            for kind, name in ((KK, "k"), (VK, "v")):
                sp.dma_start(K.o[f"win_{name}_prompt"].rearrange("a b s h d -> (a b s) (h d)"), K.proj[kind, 0:SEQ, :]).then_inc(s["rows_out"], 16)
                sp.dma_start(K.o[f"win_{name}_sample"][0].rearrange("b s h d -> b s (h d)")[:, WB - DEC_T:WB, :],
                             K.proj[kind, S0:S0 + NS, :].rearrange("(b t) c -> b t c", b=DEC_B)).then_inc(s["rows_out"], 16)
            sp.wait_ge(s["C_new"], BH)
            for h in range(MH):
                sp.dma_start(K.o["C_sample"][0, :, h].rearrange("b d e -> d b e"),
                             Cs.rearrange("p (b h) c -> p b h c", h=MH)[:, :, h, 0:MD]).then_inc(s["fin"], 16)
            with nc.allow_non_contiguous_dma(reason="the normaliser column"):
                for h in range(MH):
                    sp.dma_start(K.o["n_sample"][0, :, h].rearrange("b (d a) -> d b a", a=1),
                                 Cs.rearrange("p (b h) c -> p b h c", h=MH)[:, :, h, MD:VW]).then_inc(s["fin"], 16)
            sp.wait_ge(s["hb_ready"], 1)
            sp.dma_start(K.mix[S0:S0 + NS, AW:D], osb[:, 0]).then_inc(s["fin"], 16)
            sp.wait_ge(s["fin"], 16 * (2 * MH + 1))
            sp.wait_ge(s["ml_done"], 1)

            def load(t, new, cache, kind, b, p, x):
                sp.dma_start(t[:, p, 0:8], cache[b].rearrange("(i r) c -> i r c", r=16)[:, 0:8]).then_inc(x[p], 16)
                sp.dma_start(t[:, p, 8:12], cache[b, WB - 512:WB, :].rearrange("(i r) c -> i r c", r=4)).then_inc(x[p], 16)
                sp.dma_start(new[:, p], K.proj[kind, bass.ds(DEC_T * b + S0, DEC_T), :]).then_inc(x[p], 16)

            def load_k(b, p):
                load(kin, knew, K.ins["cache_k"], KK, b, p, k_in)

            def load_v(b, p):
                load(vin, vnew, K.ins["cache_v"], VK, b, p, v_in)

            for b in range(2):
                load_k(b, b)
                load_v(b, b)

            def turn(b, p, more):
                sp.wait_ge(s["k_turned"], KT * (b + 1))
                if more:
                    load_k(b + 2, p)
                sp.wait_ge(s["summed"], b + 1)
                if more:
                    load_v(b + 2, p)
                sp.wait_ge(s["o_ready"], b + 1)
                for h in range(H):
                    sp.dma_start(K.mix[bass.ds(DEC_T * b + S0, DEC_T), HD * h:HD * (h + 1)],
                                 osb[DEC_T * h:DEC_T * (h + 1), p, HD * h:HD * (h + 1)]).then_inc(o_out[p], 16)

            with sp.Fori(0, 3) as i:
                for j in range(2):
                    turn(2 * i + j, j, True)
            turn(6, 0, False)
            turn(7, 1, False)
            for p in range(2):
                sp.wait_ge(o_out[p], 16 * H * 4)
            sp.wait_ge(s["rows_out"], 64)

        @block.gpsimd
        def _(pool):
            g = nc.gpsimd
            own = Chain(pool, s["pool_own"])
            g.memset(vx, 1.0).then_inc(s["clear"], 1)
            g.memset(qm, 0.0).then_inc(s["clear"], 1)
            g.memset(qbd[:], 0.0).then_inc(s["clear"], 1)
            pool.wait_ge(s["ml_in"], 16 * NML)
            own.mark(g.tensor_tensor(arg, ngs, maskS.rearrange("p (a t) -> p a t", a=1).broadcast_to([NS, MH, NS]), ALU.add))
            own.mark(g.tensor_tensor(obs, obs, mhg, ALU.mult))
            pool.wait_ge(s["clear"], 3)
            for h in range(MH):
                own.mark(g.tensor_copy(qm[:, h].rearrange("p (b x) -> p b x", x=72)[:, :, 0:DEC_T],
                                       mq[:, h].rearrange("p (b t) -> p b t", b=DEC_B)))

            def put(b, p):
                for h in range(H):
                    e = h % 2
                    ins = g.tensor_copy(qbd[64 * e:64 * e + 64, p, h // 2, DEC_T * h:DEC_T * (h + 1)],
                                        qT[64 * e:64 * e + 64, h // 2, bass.ds(DEC_T * b, DEC_T)])
                ins.then_inc(s["q_ready"], 1)

            own.wait()
            pool.wait_ge(s["act_ml"], 1)
            put(0, 0)
            put(1, 1)
            with pool.Fori(1, 4) as i:
                for j in range(2):
                    pool.wait_ge(s["scores"], 4 * (2 * i + j - 1))
                    put(2 * i + j, j)

        def kcols(x):
            return slice(x * P, x * P + (P if x < 12 else DEC_T))

        @block.scalar
        def _(act):
            A = nc.scalar.activation
            nc.scalar.preload_act_table_set(LN_EXP)
            own = Chain(act, s["act_ml"])
            act.wait_ge(s["pe_ml"], 1)
            own.mark(A(qT[:], bank[0][:, 0:4 * NS].rearrange("p (h t) -> p h t", h=4), ACT.Copy, scale=HD ** -0.5))
            ins = A(Cs[:, :, MD:VW].rearrange("p e a -> p (e a)"), bank[1][:, 0:BH], ACT.Copy)
            own.link(ins)
            act.wait_ge(s["pool_own"], 1)
            for h in range(MH):
                ins = A(wm[:, h], arg[:, h], ACT.Exp, bias=K.tab_s[:, 0, h:h + 1])
            own.link(ins)
            act.wait_ge(s["pe_ml"], 3)
            for e in range(2):
                ins = A(num[:, 2 * e:2 * e + 2], bank[4 + e][0:NS, 0:2 * VW].rearrange("p (h c) -> p h c", h=2), ACT.Copy)
            own.link(ins)
            act.wait_ge(s["own"], K.sm_own_ms)
            own.link(A(sm[:, 3], sm[:, 2], ACT.Ln))
            own.link(A(sm[:, 4], sm[:, 3], ACT.Exp, scale=-0.5))

            def keys(b, p, xs):
                for x in xs:
                    act.wait_ge(s["k_turned"], KT * b + x + 1)
                    w = P if x < 12 else DEC_T
                    A(kT[:, :, kcols(x)], bank[0][:, 0:4 * w].rearrange("p (h c) -> p h c", h=4), ACT.Copy).then_inc(s["k_out_a"], 1)

            def exps(b, p):
                act.wait_ge(s["maxed"], b + 1)
                A(pr[:, p], pr[:, p], ACT.Exp, bias=st[:, p, 0:1]).then_inc(s["exps"], 1)

            def turned(b, p):
                act.wait_ge(s["p_turned"], 2 * b + 1)
                act.wait_ge(s["summed"], b)
                A(pT[:, 0:8], bank[4][:].rearrange("p (x r) -> p x r", x=8), ACT.Copy)
                act.wait_ge(s["p_turned"], 2 * b + 2)
                A(pT[:, 8:12], bank[5][:, 0:4 * RT].rearrange("p (x r) -> p x r", x=4), ACT.Copy)
                A(pT[0:DEC_T, 12], bank[5][0:DEC_T, 4 * RT:5 * RT], ACT.Copy).then_inc(s["pT_out"], 1)

            keys(0, 0, range(0, 13, 2))

            def step(b, j):
                keys(b + 1, 1 - j, (0, 2, 4))
                exps(b, j)
                keys(b + 1, 1 - j, (6, 8, 10, 12))
                turned(b, j)

            with act.Fori(0, 3) as i:
                for j in range(2):
                    step(2 * i + j, j)
            step(6, 0)
            exps(7, 1)
            turned(7, 1)

        @block.vector
        def _(dve):
            v = nc.vector
            chain = Chain(dve, s["own"])

            def bc(ap, w):
                return ap.rearrange("p (h a) -> p h a", a=1).broadcast_to([NS, MH, w])

            dve.wait_ge(s["pe_ml"], 2)
            chain.link(v.tensor_tensor(kw, bank[6][0:NS, :].rearrange("p (h d) -> p h d", h=MH), bc(K.tab_s[:, 3], MD), ALU.mult))
            dve.wait_ge(s["act_ml"], 3)
            chain.mark(v.tensor_tensor(scT, bank[7][0:NS, 0:MH * NS].rearrange("p (h t) -> p h t", h=MH), wm, ALU.mult))
            dve.wait_ge(s["ml_in"], 16 * NML)
            for h in range(MH):
                chain.mark(v.tensor_tensor(kwm[:, h], kw[:, h].rearrange("p (b d) -> p b d", b=1).broadcast_to([NS, DEC_B, MD]),
                                           seq1.rearrange("p (b d) -> p b d", d=1).broadcast_to([NS, DEC_B, MD]), ALU.mult))
            assert chain.n == K.sm_own_kwm
            dve.wait_ge(s["pe_ml"], 4)
            dve.wait_ge(s["act_ml"], 4)
            for h in range(MH):
                ins = v.scalar_tensor_tensor(num[:, h], bank[2 + h // 2][0:NS, VW * (h % 2):VW * (h % 2 + 1)],
                                             K.tab_s[:, 1, h:h + 1], num[:, h], ALU.mult, ALU.add)
            chain.link(ins)
            den = num[:, :, MD:VW].rearrange("p h a -> p (h a)")
            chain.link(v.tensor_scalar(sm[:, 5], den, -1.0, None, ALU.mult))
            chain.link(v.tensor_tensor(sm[:, 6], sm[:, 5], den, ALU.max))
            chain.link(v.tensor_tensor(sm[:, 0], sm[:, 6], K.tab_s[:, 2], ALU.max))
            chain.link(v.reciprocal(sm[:, 1], sm[:, 0]))
            chain.link(v.tensor_tensor(hh, num[:, :, 0:MD], bc(sm[:, 1], MD), ALU.mult))
            chain.link(v.tensor_tensor(sq, hh, hh, ALU.mult))
            chain.link(v.reduce_sum(sm[:, 7], sq, AX.X))
            chain.link(v.tensor_scalar(sm[:, 2], sm[:, 7], 1.0 / MD, EPS, ALU.mult, ALU.add))
            assert chain.n == K.sm_own_ms
            dve.wait_ge(s["act_ml"], 6)
            chain.link(v.tensor_tensor(sm[:, 5], sm[:, 4], sm[:, 4], ALU.mult))
            chain.link(v.tensor_tensor(sm[:, 6], sm[:, 5], sm[:, 2], ALU.mult))
            chain.link(v.tensor_scalar(sm[:, 7], sm[:, 6], -0.5, 1.5, ALU.mult, ALU.add))
            chain.link(v.tensor_tensor(sm[:, 8], sm[:, 7], sm[:, 4], ALU.mult))
            chain.link(v.tensor_tensor(hh, hh, bc(sm[:, 8], MD), ALU.mult))
            dve.wait_ge(s["pool_own"], 2)
            v.tensor_tensor(osb[:, 0], hh.rearrange("p h d -> p (h d)"), obs, ALU.mult).then_inc(s["hb_ready"], 1)
            for e in range(BH):
                dve.wait_ge(s["dC"], e + 1)
                v.scalar_tensor_tensor(Cs[:, e], Cs[:, e], K.wti[:, NCH * MH + e:NCH * MH + e + 1], bank[e % 4][:, 0:VW],
                                       ALU.mult, ALU.add).then_inc(s["C_new"], 1)
            dve.wait_ge(s["tab_in"], 32)

            def keys(b, xs):
                for x in xs:
                    dve.wait_ge(s["k_turned"], KT * b + x + 1)
                    v.tensor_copy(kT[:, :, kcols(x)], bank[1][:].rearrange("p (h c) -> p h c", h=4)).then_inc(s["k_out_d"], 1)

            def masked(b, p, cs, first=False):
                for c in cs:
                    w = 512 if c < 3 else DEC_T
                    dve.wait_ge(s["scores"], 4 * b + c + 1)
                    if c == 0 and not first:
                        dve.wait_ge(s["p_turned"], 2 * b - 2)
                    v.tensor_tensor(pr[:, p, 512 * c:512 * c + w], bank[2 + c % 2][0:RT, 0:w], mask[:, 512 * c:512 * c + w],
                                    ALU.add).then_inc(s["masked"], 1)

            def maxed(b, p):
                dve.wait_ge(s["masked"], 4 * b + 4)
                v.reduce_max(st[:, p, 0:1], pr[:, p], AX.X, negate=True).then_inc(s["maxed"], 1)

            def counted(b, p):
                dve.wait_ge(s["exps"], b + 1)
                v.scalar_tensor_tensor(pr[:, p], pr[:, p], 1.0, count[:], ALU.mult, ALU.mult,
                                       accum_out=st[:, p, 1:2]).then_inc(s["counted"], 1)
                dve.wait_ge(s["counted"], b + 1)
                v.reciprocal(st[:, p, 2:3], st[:, p, 1:2]).then_inc(s["own"], 1)
                chain.n += 1

            def out(b, p, used):
                dve.wait_ge(s["summed"], b + 1)
                if used is not None:
                    dve.wait_ge(o_out[p], 16 * H * used)
                chain.wait()
                v.tensor_scalar(osb[:, p], bank[6][0:RT, :], st[:, p, 2:3], None, ALU.mult).then_inc(s["o_ready"], 1)

            keys(0, (1, 3, 5, 7))
            masked(0, 0, (0,), True)
            keys(0, (9, 11))
            masked(0, 0, (1, 2, 3))
            maxed(0, 0)

            def step(b, j, used, first=False):
                keys(b + 1, (1, 3, 5))
                counted(b, j)
                keys(b + 1, (7,))
                masked(b + 1, 1 - j, (0,), first)
                keys(b + 1, (9, 11))
                masked(b + 1, 1 - j, (1, 2, 3))
                maxed(b + 1, 1 - j)
                out(b, j, used)

            step(0, 0, None, True)
            step(1, 1, None)
            with chain.loop(2, 2) as i:
                for j in range(2):
                    step(2 * i + j + 2, j, i + 1)
            step(6, 0, 3)
            counted(7, 1)
            out(7, 1, 3)

        @block.tensor
        def _(pe):
            mm, tp = nc.tensor.matmul, nc.tensor.transpose
            ident = K.ident
            pe.wait_ge(s["ml_in"], 16 * NML)
            for c in range(4):
                tp(bank[0][:, NS * c:NS * (c + 1)], qs[:, c * P:(c + 1) * P], ident[0:NS, 0:NS])
            tp(bank[1][:, 0:BH], n32, ident[0:BH, 0:BH]).then_inc(s["pe_ml"], 1)
            for h in range(MH):
                mm(bank[7][0:NS, NS * h:NS * (h + 1)], mkk[:, h], mq[:, h], start=True, stop=True)
            for h in range(MH):
                ins = tp(bank[6][0:NS, P * h:P * (h + 1)], mkk[:, h], ident[:])
            ins.then_inc(s["pe_ml"], 1)
            pe.wait_ge(s["clear"], 3)
            pe.wait_ge(s["own"], 2)
            for h in range(MH):
                ins = mm(bank[4 + h // 2][0:NS, VW * (h % 2):VW * (h % 2 + 1)], scT[:, h], vx[:, h], start=True, stop=True)
            ins.then_inc(s["pe_ml"], 1)
            pe.wait_ge(s["act_ml"], 2)
            pe.wait_ge(s["pool_own"], 6)
            for h in range(MH):
                for b in range(DEC_B):
                    ins = mm(bank[2 + h // 2][0:NS, VW * (h % 2):VW * (h % 2 + 1)], qm[:, h, NS * b:NS * (b + 1)],
                             Cs[:, MH * b + h], start=(b == 0), stop=(b == DEC_B - 1))
            ins.then_inc(s["pe_ml"], 1)
            pe.wait_ge(s["own"], K.sm_own_kwm + 1)
            for e in range(BH):
                if e >= 4:
                    pe.wait_ge(s["C_new"], e - 3)
                ins = mm(bank[e % 4][:, 0:VW], kwm[:, e % MH, e // MH], vx[:, e % MH], start=True, stop=True)
                ins.then_inc(s["dC"], 1)
            pe.wait_ge(s["C_new"], BH)
            nc.tensor.transpose(bank[7][0:1, 0:P], ident[:, 0:1], ident[:]).then_inc(s["ml_done"], 1)

            def turn(b, p, xs):
                for x in xs:
                    if x % 2 == 0:
                        pe.wait_ge(s["k_out_a"], 7 * b + x // 2)
                    else:
                        pe.wait_ge(s["k_out_d"], 6 * b + x // 2)
                    src = kin[:, p, x] if x < 12 else knew[:, p]
                    w = P if x < 12 else DEC_T
                    for c in range(4):
                        dst, rows = bank[x % 2][:, w * c:w * (c + 1)], src[:, c * P:(c + 1) * P]
                        if x < 12:
                            ins = tp(dst, rows, ident[:])
                        else:
                            ins = mm(dst, rows, ident[0:w, 0:w], start=True, stop=True)
                    ins.then_inc(s["k_turned"], 1)

            def scores(b, p, c):
                w = 512 if c < 3 else DEC_T
                pe.wait_ge(s["k_out_a"], 7 * b + (2 * c + 2 if c < 3 else 7))
                pe.wait_ge(s["k_out_d"], 6 * b + (2 * c + 2 if c < 3 else 6))
                if c < 2:
                    pe.wait_ge(s["masked"], 4 * b)
                else:
                    pe.wait_ge(s["masked"], 4 * b + c - 1)
                for h in range(4):
                    ins = mm(bank[2 + c % 2][0:RT, 0:w], qbd[:, p, h], kT[:, h, 512 * c:512 * c + w], start=(h == 0), stop=(h == 3))
                ins.then_inc(s["scores"], 1)

            def first_half(b, p, use):
                pe.wait_ge(k_in[p], 48 * (use + 1))
                pe.wait_ge(s["q_ready"], b + 1)
                turn(b, p, range(0, 8))
                scores(b, p, 0)
                turn(b, p, range(8, 12))
                scores(b, p, 1)
                turn(b, p, (12,))
                scores(b, p, 2)
                scores(b, p, 3)

            def second_half(b, p, use):
                pe.wait_ge(s["counted"], b + 1)
                pe.wait_ge(s["pT_out"], b)
                for x in range(KT):
                    w = P if x < 12 else DEC_T
                    dst = bank[4 + x // 8][0:w, RT * (x % 8):RT * (x % 8 + 1)]
                    if x:
                        ins = tp(dst, pr[:, p, kcols(x)], ident[0:RT, 0:RT])
                    else:
                        mm(dst, pr[:, p, kcols(x)], ident[0:RT, 0:RT], start=True, stop=True)
                    if x in (7, 12):
                        ins.then_inc(s["p_turned"], 1)
                pe.wait_ge(v_in[p], 48 * (use + 1))
                pe.wait_ge(s["pT_out"], b + 1)
                pe.wait_ge(s["o_ready"], b)
                for x in range(KT):
                    w = P if x < 12 else DEC_T
                    ins = mm(bank[6][0:RT, :], pT[0:w, x], vin[:, p, x] if x < 12 else vnew[:, p], start=(x == 0), stop=(x == KT - 1))
                ins.then_inc(s["summed"], 1)

            first_half(0, 0, 0)
            with pe.Fori(0, 3) as i:
                for j in range(2):
                    first_half(2 * i + j + 1, 1 - j, i + j)
                    second_half(2 * i + j, j, i)
            first_half(7, 1, 3)
            second_half(6, 0, 3)
            second_half(7, 1, 3)


def project_out(K):
    nc, sem = K.nc, K.sem
    HW = HD + 2
    NP = SEQ // P
    with ExitStack() as ctx:
        def sb(name, shape, dt=F32):
            return ctx.enter_context(nc.sbuf_tensor("out_" + name, shape, dt))

        w_raw = sb("w_raw", [P, 2, 2, D])
        w_hi = sb("w_hi", [P, KC, D], F32R)
        w_lo = sb("w_lo", [P, KC, D], F32R)
        xt = sb("xt", [P, 2, D])
        mt = sb("mt", [P, 2, D])
        pt = sb("pt", [P, 2, 3, H, HW])
        prod = sb("prod", [P, 3, H, HD])
        mT_hi = sb("mT_hi", [P, 2, KC, P], F32R)
        mT_lo = sb("mT_lo", [P, 2, KC, P], F32R)
        st = sb("st", [P, 2, 8, 3, H])
        bank = [ctx.enter_context(nc.psum_tensor(f"out_bank{i}", [P, 512], F32)) for i in range(8)]
        w_in = [sem(f"out_w_in{q}") for q in range(2)]
        w_hi_ready, w_lo_ready = sem("out_w_hi"), sem("out_w_lo")
        tile_in = [sem(f"out_tile_in{q}") for q in range(2)]
        x_in = [sem(f"out_x_in{q}") for q in range(2)]
        x2_out = [sem(f"out_x2_out{q}") for q in range(2)]
        shifted, exps, mixed, turned, hi_ready, lo_ready, prod_mm, added, own = (
            sem("out_" + n) for n in ("shifted", "exps", "mixed", "turned", "hi", "lo", "prod_mm", "added", "own"))
        block = ctx.enter_context(nc.Block(no_gpsimd_drain=True))
        IN = 16 * 2
        last_in = IN * (NP // 2) + 16

        xv = K.x.rearrange("(t p) d -> t p d", p=P)

        @block.sync
        def _(sp):
            def load(t, p):
                rows = bass.ds(t * P, P)
                sp.dma_start(pt[:, p], K.parts[:, rows, :].rearrange("a p (h c) -> p a h c", h=H)).then_inc(tile_in[p], 16)
                sp.dma_start(mt[:, p, AW:D], K.mix[rows, AW:D]).then_inc(tile_in[p], 16)

            def load_x(t, p):
                sp.dma_start(xt[:, p], xv[t]).then_inc(x_in[p], 16)

            for t in range(2):
                load(t, t)
                load_x(t, t)
            for q in range(4):
                if q >= 2:
                    sp.wait_ge(w_lo_ready, q - 1)
                sp.dma_start(w_raw[:, q % 2], K.ins["w_out"][:, 2 * q:2 * q + 2, :]).then_inc(w_in[q % 2], 16)

            def reload(t, i, p):
                sp.wait_ge(turned, t + 1)
                load(t + 2, p)
                sp.wait_ge(x2_out[p], 16 * i + 16)
                load_x(t + 2, p)

            with sp.Fori(0, NP // 2 - 1) as i:
                for j in range(2):
                    reload(2 * i + j, i, j)
            sp.wait_ge(turned, NP - 1)
            sp.dma_start(mt[0:NS, 0], K.mix[SEQ:NT, :]).then_inc(tile_in[0], 16)
            sp.wait_ge(x2_out[0], 16 * (NP // 2))
            load_x(NP, 0)

        @block.gpsimd
        def _(pool):
            for q in range(4):
                pool.wait_ge(w_hi_ready, q + 1)
                nc.gpsimd.tensor_tensor(w_lo[:, 2 * q:2 * q + 2], w_raw[:, q % 2], w_hi[:, 2 * q:2 * q + 2].bitcast(F32),
                                        ALU.subtract).then_inc(w_lo_ready, 1)

        @block.scalar
        def _(act):
            A = nc.scalar.activation
            nc.scalar.preload_act_table_set(LN_EXP)

            def exp(t, p):
                act.wait_ge(shifted, t + 1)
                A(st[:, p, 1], st[:, p, 1], ACT.Exp).then_inc(exps, 1)

            def hi(t, p, w=P, used=True):
                act.wait_ge(turned, t + 1)
                if used:
                    act.wait_ge(prod_mm, 2 * t - 2)
                for e in range(2):
                    ins = A(mT_hi[:, p, 4 * e:4 * e + 4, 0:w],
                            bank[2 * p + e][:].rearrange("p (k c) -> p k c", k=4)[:, :, 0:w], ACT.Copy)
                ins.then_inc(hi_ready, 1)

            def store(t, p):
                act.wait_ge(added, 2 * t + 2)
                act.dma_start(K.x2[bass.ds(t * P, P), :], xt[:, p]).then_inc(x2_out[p], 16)

            exp(0, 0)
            exp(1, 1)
            for q in range(4):
                act.wait_ge(w_in[q % 2], 16 * (q // 2 + 1))
                A(w_hi[:, 2 * q:2 * q + 2], w_raw[:, q % 2], ACT.Copy).then_inc(w_hi_ready, 1)
            hi(0, 0, used=False)
            hi(1, 1, used=False)
            exp(2, 0)
            store(0, 0)
            hi(2, 0)
            exp(3, 1)
            store(1, 1)
            with act.Fori(1, NP // 2 - 1) as i:
                for j in range(2):
                    hi(2 * i + j + 1, 1 - j)
                    exp(2 * i + j + 2, j)
                    store(2 * i + j, j)
            hi(NP - 1, 1)
            store(NP - 2, 0)
            hi(NP, 0, NS)
            store(NP - 1, 1)
            store(NP, 0)
            for p in range(2):
                act.wait_ge(x2_out[p], 16 * (NP // 2 + 1 - p))

        @block.vector
        def _(dve):
            v = nc.vector
            chain = Chain(dve, own)

            def wide(a):
                return a.rearrange("p h (d a) -> p h d a", a=1)

            def combine(t, i, p):
                q = pt[:, p]
                neg, den = q[:, :, :, HD], q[:, :, :, HD + 1]
                S = st[:, p]
                dve.wait_ge(tile_in[p], IN * i + IN)
                chain.link(v.tensor_tensor(S[:, 0, 0], neg[:, 0], neg[:, 1], ALU.min))
                chain.link(v.tensor_tensor(S[:, 0, 1], S[:, 0, 0], neg[:, 2], ALU.min))
                v.tensor_tensor(S[:, 1], S[:, 0, 1:2].broadcast_to([P, 3, H]), neg, ALU.subtract).then_inc(shifted, 1)
                dve.wait_ge(exps, t + 1)
                chain.link(v.tensor_tensor(S[:, 3], S[:, 1], den, ALU.mult))
                chain.link(v.tensor_tensor(S[:, 4, 0], S[:, 3, 0], S[:, 3, 1], ALU.add))
                chain.link(v.tensor_tensor(S[:, 4, 1], S[:, 4, 0], S[:, 3, 2], ALU.add))
                chain.link(v.reciprocal(S[:, 4, 2], S[:, 4, 1]))
                chain.link(v.tensor_tensor(S[:, 2], S[:, 1], S[:, 4, 2:3].broadcast_to([P, 3, H]), ALU.mult))
                for a in range(3):
                    ins = v.tensor_tensor(prod[:, a], q[:, a, :, 0:HD],
                                          S[:, 2, a].rearrange("p (h d) -> p h d", d=1).broadcast_to([P, H, HD]), ALU.mult)
                chain.link(ins)
                chain.link(v.tensor_tensor(prod[:, 0], prod[:, 0], prod[:, 1], ALU.add))
                v.tensor_tensor(mt[:, p, 0:AW].rearrange("p (h d) -> p h d", h=H), prod[:, 0], prod[:, 2],
                                ALU.add).then_inc(mixed, 1)
                dve.wait_ge(mixed, t + 1)

            def lo(t, p, w=P):
                dve.wait_ge(hi_ready, t + 1)
                for e in range(2):
                    ins = v.tensor_tensor(mT_lo[:, p, 4 * e:4 * e + 4, 0:w],
                                          bank[2 * p + e][:].rearrange("p (k c) -> p k c", k=4)[:, :, 0:w],
                                          mT_hi[:, p, 4 * e:4 * e + 4, 0:w].bitcast(F32), ALU.subtract)
                ins.then_inc(lo_ready, 1)

            def add(t, i, p, rows=P):
                dve.wait_ge(x_in[p], 16 * i + 16)
                for e in range(2):
                    dve.wait_ge(prod_mm, 2 * t + e + 1)
                    v.tensor_tensor(xt[0:rows, p, 512 * e:512 * e + 512], xt[0:rows, p, 512 * e:512 * e + 512],
                                    bank[4 + 2 * p + e][0:rows, :], ALU.add).then_inc(added, 1)

            combine(0, 0, 0)
            combine(1, 0, 1)
            lo(0, 0)
            with chain.loop(NP // 2 - 1, 18) as i:
                for j in range(2):
                    lo(2 * i + j + 1, 1 - j)
                    combine(2 * i + j + 2, i + 1, j)
                    add(2 * i + j, i, j)
            lo(NP - 1, 1)
            add(NP - 2, NP // 2 - 1, 0)
            lo(NP, 0, NS)
            add(NP - 1, NP // 2 - 1, 1)
            add(NP, NP // 2, 0, NS)

        @block.tensor
        def _(pe):
            def turn(t, p, used=True):
                pe.wait_ge(mixed, t + 1)
                if used:
                    pe.wait_ge(lo_ready, t - 1)
                for k in range(KC):
                    ins = nc.tensor.transpose(bank[2 * p + k // 4][:, (k % 4) * P:(k % 4 + 1) * P],
                                              mt[:, p, k * P:(k + 1) * P], K.ident[:])
                ins.then_inc(turned, 1)

            def products(t, p, w=P, used=True):
                pe.wait_ge(lo_ready, t + 1)
                for e in range(2):
                    if used:
                        pe.wait_ge(added, 2 * t + e - 3)
                    split_products(nc, bank[4 + 2 * p + e][0:w, :],
                                   [(mT_hi[:, p, k, 0:w], mT_lo[:, p, k, 0:w], w_hi[:, k, 512 * e:512 * e + 512],
                                     w_lo[:, k, 512 * e:512 * e + 512]) for k in range(KC)], prod_mm)

            pe.wait_ge(K.ident_ready, K.ident_value)
            turn(0, 0, False)
            turn(1, 1, False)
            pe.wait_ge(w_lo_ready, 4)
            products(0, 0, used=False)
            turn(2, 0)
            products(1, 1, used=False)
            with pe.Fori(1, NP // 2 - 1) as i:
                for j in range(2):
                    turn(2 * i + j + 1, 1 - j)
                    products(2 * i + j, j)
            turn(NP - 1, 1)
            products(NP - 2, 0)
            pe.wait_ge(lo_ready, NP - 1)
            pe.wait_ge(tile_in[0], last_in)
            for k in range(KC):
                ins = nc.tensor.transpose(bank[k // 4][:, (k % 4) * P:(k % 4) * P + NS],
                                          mt[0:NS, 0, k * P:(k + 1) * P], K.ident[0:NS, 0:NS])
            ins.then_inc(turned, 1)
            products(NP - 1, 1)
            products(NP, 0, NS)


def mlp(K):
    nc, sem = K.nc, K.sem
    GT0, GN = (0, 6, 12), (6, 6, 5)
    PIECE = (3 * P, 3 * P, 2 * P + NS // 2)
    FB = DFF // 256
    G = len(GN)
    with ExitStack() as ctx:
        def sb(name, shape, dt=F32):
            return ctx.enter_context(nc.sbuf_tensor("mlp_" + name, shape, dt))

        hT_hi = sb("hT_hi", [P, KC, 6 * P], F32R)
        hT_lo = sb("hT_lo", [P, KC, 6 * P], F32R)
        xb = sb("xb", [P, 2, D])
        xn = sb("xn", [P, 2, D])
        small = sb("small", [P, 2, 8])
        gain2 = sb("gain2", [P, D])
        gain_f = sb("gain_f", [P, D])
        wu_raw = sb("wu_raw", [P, KC, 256])
        wd_raw = sb("wd_raw", [P, 2, D])
        wu_hi = [sb(f"wu_hi{s}", [P, KC, 256], F32R) for s in range(2)]
        wu_lo = [sb(f"wu_lo{s}", [P, KC, 256], F32R) for s in range(2)]
        wd_hi = [sb(f"wd_hi{s}", [P, 2, D], F32R) for s in range(2)]
        wd_lo = [sb(f"wd_lo{s}", [P, 2, D], F32R) for s in range(2)]
        u2 = xn[:].rearrange("p s d -> p (s d)")[:, 0:2 * 6 * P].rearrange("p (m c) -> p m c", m=2)
        u_hi = [sb(f"u_hi{s}", [P, 2, 6 * P], F32R) for s in range(2)]
        u_lo = [sb(f"u_lo{s}", [P, 2, 6 * P], F32R) for s in range(2)]
        acc = sb("acc", [P, 6, D])
        fin = sb("fin", [P, 8, 6])
        bank = [ctx.enter_context(nc.psum_tensor(f"mlp_bank{i}", [P, 512], F32)) for i in range(8)]

        const_in, acc_in, y_out, copied = sem("mlp_const_in"), sem("mlp_acc_in"), sem("mlp_y_out"), sem("mlp_copied")
        wu_in, wu_hi_ready, wu_lo_ready = sem("mlp_wu_in"), sem("mlp_wu_hi"), sem("mlp_wu_lo")
        wd_in, wd_hi_ready, wd_lo_ready = sem("mlp_wd_in"), sem("mlp_wd_hi"), sem("mlp_wd_lo")
        up_mm, u2_ready, u_hi_ready, u_lo_ready = sem("mlp_up_mm"), sem("mlp_u2"), sem("mlp_u_hi"), sem("mlp_u_lo")
        relu_done = sem("mlp_relu")
        down_mm, summed, own = sem("mlp_down_mm"), sem("mlp_summed"), sem("mlp_own")
        f_ssq, f_var, f_root, y_ready = sem("mlp_f_ssq"), sem("mlp_f_var"), sem("mlp_f_root"), sem("mlp_y_ready")
        DB = tuple(FB * GT0[g] for g in range(G))
        xv = K.x2.rearrange("(t p) d -> t p d", p=P)

        norm = Norm(nc, sem, "mlp", lambda T: xv[T], xb, xn, small, gain2, hT_hi, hT_lo,
                    [bank[4], bank[5], bank[6], bank[7]], K.ident)
        block = ctx.enter_context(nc.Block(no_gpsimd_drain=True))
        @block.sync
        def _(sp):
            CB = (WB - DEC_T) // 6

            def load_up(E, f):
                sp.dma_start(wu_raw[:], K.ins["w_up"][f]).then_inc(wu_in, 16)

            def load_down(E, f):
                sp.dma_start(wd_raw[:], K.ins["w_down"][f]).then_inc(wd_in, 16)

            sp.dma_start(gain2[:], K.ins["norm2_g"].partition_broadcast(P)).then_inc(const_in, 16)
            sp.dma_start(gain_f[:], K.ins["norm_f_g"].partition_broadcast(P)).then_inc(const_in, 16)
            for g in range(G):
                norm.sync_group(sp, GT0[g], GN[g])
                if g:
                    sp.wait_ge(y_out, 16 * GT0[g])
                sp.dma_start(acc[:, 0:GN[g]], K.x2[GT0[g] * P:(GT0[g] + GN[g]) * P, :].rearrange("(t p) d -> p t d", p=P))\
                    .then_inc(acc_in, 16)
                if g == 0:
                    load_up(0, 0)
                    load_down(0, 0)
                    sp.wait_ge(wu_lo_ready, 1)
                    load_up(1, 1)
                    sp.wait_ge(wu_lo_ready, 2)
                    load_up(2, 2)
                    sp.wait_ge(wd_lo_ready, 1)
                    load_down(1, 1)

                def copy(i, j):
                    for name in ("k", "v"):
                        sp.dma_start(K.o[f"win_{name}_sample"][0].rearrange("b s h d -> b s (h d)")[i, CB * (2 * g + j):CB * (2 * g + j + 1), :],
                                     K.ins["cache_" + name][i, DEC_T + CB * (2 * g + j):DEC_T + CB * (2 * g + j + 1), :])\
                            .then_inc(copied, 16)

                def step(i, j, up=None, down=None):
                    f = 2 * i + j
                    copy(i, j)
                    if up is not None:
                        sp.wait_ge(wu_lo_ready, f + (FB * g + 3))
                        load_up(0, up)
                    if down is not None:
                        sp.wait_ge(wd_lo_ready, f + (FB * g + 2))
                        load_down(0, down)

                with sp.Fori(0, 6) as i:
                    for j in range(2):
                        step(i, j, 2 * i + j + 3, 2 * i + j + 2)
                for f in range(12, FB):
                    more = g < G - 1
                    step(f // 2, f % 2, (f + 3) % FB if more or f + 3 < FB else None,
                         (f + 2) % FB if more or f + 2 < FB else None)
            sp.wait_ge(copied, 16 * 2 * G * FB)

        @block.gpsimd
        def _(pool):
            g_ = nc.gpsimd

            def split_up(E, s):
                pool.wait_ge(wu_hi_ready, E + 1)
                g_.tensor_tensor(wu_lo[s][:], wu_raw[:], wu_hi[s][:].bitcast(F32), ALU.subtract).then_inc(wu_lo_ready, 1)

            def split_down(E, s):
                pool.wait_ge(wd_hi_ready, E + 1)
                g_.tensor_tensor(wd_lo[s][:], wd_raw[:], wd_hi[s][:].bitcast(F32), ALU.subtract).then_inc(wd_lo_ready, 1)

            def split_u(g, E, s):
                w = PIECE[g]
                for k in range(4):
                    m, q = k // 2, k % 2
                    pool.wait_ge(u_hi_ready, 4 * E + k + 1)
                    cols = slice(w * q, w * q + w)
                    g_.tensor_tensor(u_lo[s][:, m, cols], u2[:, m, cols], u_hi[s][:, m, cols].bitcast(F32),
                                     ALU.subtract).then_inc(u_lo_ready, 1)

            split_up(0, 0)
            split_down(0, 0)
            split_up(1, 1)
            for g in range(G):
                split_u(g, FB * g, 0)

                def step(f, j, up=True, down=True, u=True):
                    E = f + FB * g
                    if up:
                        split_up(E + 2, j)
                    if down:
                        split_down(E + 1, 1 - j)
                    if u:
                        split_u(g, E + 1, 1 - j)

                with pool.Fori(0, 7) as i:
                    for j in range(2):
                        step(2 * i + j, j)
                more = g < G - 1
                step(14, 0, up=more)
                step(15, 1, up=more, down=more, u=False)

        @block.scalar
        def _(act):
            A = nc.scalar.activation
            nc.scalar.preload_act_table_set(LN_EXP)
            act.wait_ge(const_in, 32)

            def round_up(E, s, used=True):
                act.wait_ge(wu_in, 16 * E + 16)
                if used:
                    act.wait_ge(up_mm, 4 * E - 4)
                A(wu_hi[s][:], wu_raw[:], ACT.Copy).then_inc(wu_hi_ready, 1)

            def round_down(E, s, used=None):
                act.wait_ge(wd_in, 16 * E + 16)
                if used is not None:
                    act.wait_ge(down_mm, used)
                A(wd_hi[s][:], wd_raw[:], ACT.Copy).then_inc(wd_hi_ready, 1)

            def round_u(g, E, s, used=None):
                w = PIECE[g]
                if used is not None:
                    act.wait_ge(down_mm, used)

                def relu(k):
                    m, q = k // 2, k % 2
                    act.wait_ge(up_mm, 4 * E + k + 1)
                    if not (isinstance(E, int) and E == 0):
                        act.wait_ge(u_lo_ready, 4 * E + (k - 3))
                    A(u2[:, m, w * q:w * q + w], bank[k][:, 0:w], ACT.Relu).then_inc(relu_done, 1)

                relu(0)
                for k in range(4):
                    if k < 3:
                        relu(k + 1)
                    m, q = k // 2, k % 2
                    act.wait_ge(u2_ready, 4 * E + k + 1)
                    cols = slice(w * q, w * q + w)
                    A(u_hi[s][:, m, cols], u2[:, m, cols], ACT.Copy).then_inc(u_hi_ready, 1)

            def final(g):
                n = GN[g]
                act.wait_ge(summed, DB[g] + FB * n)
                for t in range(n):
                    if t >= 2:
                        act.wait_ge(f_ssq, GT0[g] + t - 1)
                    A(xn[:, t % 2], acc[:, t], ACT.Square, accum_out=fin[:, 0, t:t + 1]).then_inc(f_ssq, 1)
                act.wait_ge(f_var, g + 1)
                A(fin[:, 2, 0:n], fin[:, 1, 0:n], ACT.Ln).then_inc(f_root, 1)
                act.wait_ge(f_root, 2 * g + 1)
                A(fin[:, 3, 0:n], fin[:, 2, 0:n], ACT.Exp, scale=-0.5).then_inc(f_root, 1)
                for t in range(n):
                    T = GT0[g] + t
                    act.wait_ge(y_ready, T + 1)
                    dst = K.o["y_prompt"][0, T * P:(T + 1) * P, :] if T < TILES - 1 else K.o["y_sample"].rearrange("b t d -> (b t) d")
                    act.dma_start(dst, acc[0:(P if T < TILES - 1 else NS), t]).then_inc(y_out, 16)

            for g in range(G):
                norm.free = (lambda e, g=g: e.wait_ge(up_mm, 4 * FB * g)) if g else None
                if g:
                    act.wait_ge(u_lo_ready, 4 * FB * g)
                norm.act_group(act, GT0[g], GN[g])
                if g == 0:
                    round_up(0, 0, False)
                    round_down(0, 0)
                    round_up(1, 1, False)
                else:
                    final(g - 1)
                    act.wait_ge(f_ssq, GT0[g])
                round_u(g, FB * g, 0)

                def step(f, j, up=True, down=True, u=True):
                    E = f + FB * g
                    past = GN[g] * f + DB[g]
                    if up:
                        round_up(E + 2, j)
                    if down:
                        round_down(E + 1, 1 - j, past)
                    if u:
                        round_u(g, E + 1, 1 - j, past)

                with act.Fori(0, 7) as i:
                    for j in range(2):
                        step(2 * i + j, j)
                more = g < G - 1
                step(14, 0, up=more)
                step(15, 1, up=more, down=more, u=False)
            act.wait_ge(u_lo_ready, 4 * FB * G)
            final(G - 1)
            act.wait_ge(y_out, 16 * TILES)

        @block.vector
        def _(dve):
            v = nc.vector
            chain = Chain(dve, own)
            dve.wait_ge(const_in, 32)

            def square(g, E):
                w = PIECE[g]
                for k in range(4):
                    m, q = k // 2, k % 2
                    dve.wait_ge(relu_done, 4 * E + k + 1)
                    v.tensor_tensor(u2[:, m, w * q:w * q + w], u2[:, m, w * q:w * q + w], u2[:, m, w * q:w * q + w],
                                    ALU.mult).then_inc(u2_ready, 1)

            def add(g, f):
                n = GN[g]
                for t in range(n):
                    rows = P if GT0[g] + t < TILES - 1 else NS
                    done = n * f + (DB[g] + t)
                    dve.wait_ge(down_mm, done + 1)
                    if not (isinstance(f, int) and f == 0):
                        dve.wait_ge(summed, n * f + DB[g])
                    for e in range(2):
                        ins = v.tensor_tensor(acc[0:rows, t, 512 * e:512 * e + 512], acc[0:rows, t, 512 * e:512 * e + 512],
                                              bank[4 + 2 * (t % 2) + e][0:rows, :], ALU.add)
                    ins.then_inc(summed, 1)

            def final(g):
                n = GN[g]
                q = fin[:, :, 0:n]
                dve.wait_ge(f_ssq, GT0[g] + n)
                v.tensor_scalar(q[:, 1], q[:, 0], 1.0 / D, EPS, ALU.mult, ALU.add).then_inc(f_var, 1)
                dve.wait_ge(f_root, 2 * g + 2)
                chain.link(v.tensor_tensor(q[:, 4], q[:, 3], q[:, 3], ALU.mult))
                chain.link(v.tensor_tensor(q[:, 5], q[:, 4], q[:, 1], ALU.mult))
                chain.link(v.tensor_scalar(q[:, 6], q[:, 5], -0.5, 1.5, ALU.mult, ALU.add))
                chain.link(v.tensor_tensor(q[:, 7], q[:, 6], q[:, 3], ALU.mult))
                for t in range(n):
                    v.scalar_tensor_tensor(acc[:, t], acc[:, t], q[:, 7, t:t + 1], gain_f[:], ALU.mult, ALU.mult).then_inc(y_ready, 1)

            for g in range(G):
                norm.dve_group(dve, chain, GT0[g], GN[g])
                if g:
                    final(g - 1)
                square(g, FB * g)
                dve.wait_ge(acc_in, 16 * g + 16)
                square(g, FB * g + 1)
                add(g, 0)
                square(g, FB * g + 2)
                add(g, 1)
                with dve.Fori(1, 7) as i:
                    for j in range(2):
                        square(g, 2 * i + j + (FB * g + 1))
                        add(g, 2 * i + j)
                square(g, FB * g + 15)
                add(g, 14)
                add(g, 15)
            final(G - 1)

        @block.tensor
        def _(pe):
            pe.wait_ge(K.ident_ready, K.ident_value)

            def up(g, E, s):
                w = PIECE[g]
                pe.wait_ge(wu_lo_ready, E + 1)
                for k in range(4):
                    m, q = k // 2, k % 2
                    if not (isinstance(E, int) and E == 0):
                        pe.wait_ge(relu_done, 4 * E + (k - 3))
                    split_products(nc, bank[k][:, 0:w],
                                   [(wu_hi[s][:, c, m * P:(m + 1) * P], wu_lo[s][:, c, m * P:(m + 1) * P],
                                     hT_hi[:, c, w * q:w * q + w], hT_lo[:, c, w * q:w * q + w]) for c in range(KC)], up_mm)

            def down(g, f, s):
                n = GN[g]
                pe.wait_ge(wd_lo_ready, f + (FB * g + 1))
                pe.wait_ge(u_lo_ready, 4 * f + (4 * FB * g + 4))
                for t in range(n):
                    w = P if GT0[g] + t < TILES - 1 else NS
                    done = n * f + (DB[g] + t)
                    if isinstance(f, int) and f == 0 and t < 2:
                        pass
                    else:
                        pe.wait_ge(summed, done - 1 if t else done)
                    for e in range(2):
                        split_products(nc, bank[4 + 2 * (t % 2) + e][0:w, :],
                                       [(u_hi[s][:, m, t * P:t * P + w], u_lo[s][:, m, t * P:t * P + w],
                                         wd_hi[s][:, m, 512 * e:512 * e + 512], wd_lo[s][:, m, 512 * e:512 * e + 512])
                                        for m in range(2)], down_mm if e else None)

            for g in range(G):
                if g:
                    pe.wait_ge(summed, DB[g])
                norm.pe_group(pe, GT0[g], GN[g])
                pe.wait_ge(norm.lo_ready, GT0[g] + GN[g])
                up(g, FB * g, 0)
                up(g, FB * g + 1, 1)
                down(g, 0, 0)
                with pe.Fori(0, 7) as i:
                    for j in range(2):
                        up(g, 2 * i + j + (FB * g + 2), j)
                        down(g, 2 * i + j + 1, 1 - j)
                down(g, 15, 1)


class Kernel:
    pass


STAGES = (project, gate_tables, mix_prompt, mix_sample, project_out, mlp)
INPUTS = [
    ("x", (ROWS, D)), ("norm1_g", (D,)), ("rot", (P, 2, TILES, 2 * ROT)), ("w_gate", (P, KC, 8)), ("b_gate", (8,)),
    ("w_conv", (P, 8, CONVW)), ("b_conv", (P, 8)), ("k_scale", (P, 8)), ("state_conv", (24, 2 * MW)),
    ("w_qk", (8, P, KC * P)), ("w_tok", (5, P, KC, 512)),
    ("cache_k", (DEC_B, WB, AW)), ("cache_v", (DEC_B, WB, AW)),
    ("state_C", (DEC_B, MH, MD, MD)), ("state_n", (DEC_B, MH, MD)), ("state_m", (DEC_B * MH, 1)),
    ("sample_mask", (RT, KEYS)), ("sample_count", (RT, KEYS)), ("chunk_mask", (NS, NS)), ("token_seq", (NS, DEC_B)),
    ("mh_norm_g", (MW,)), ("w_out", (P, KC, D)), ("norm2_g", (D,)),
    ("w_up", (16, P, KC, 256)), ("w_down", (16, P, 2, D)), ("norm_f_g", (D,)),
]
OUTPUTS = [
    ("y_prompt", (1, SEQ, D)), ("y_sample", (DEC_B, DEC_T, D)),
    ("win_k_prompt", (1, 1, WB, H, HD)), ("win_v_prompt", (1, 1, WB, H, HD)),
    ("conv_prompt", (1, 1, CONVW - 1, 2 * MW)), ("C_prompt", (1, 1, MH, MD, MD)),
    ("n_prompt", (1, 1, MH, MD)), ("m_prompt", (1, 1, MH)),
    ("win_k_sample", (1, DEC_B, WB, H, HD)), ("win_v_sample", (1, DEC_B, WB, H, HD)),
    ("conv_sample", (1, DEC_B, CONVW - 1, 2 * MW)), ("C_sample", (1, DEC_B, MH, MD, MD)),
    ("n_sample", (1, DEC_B, MH, MD)), ("m_sample", (1, DEC_B, MH)),
]


def hybrid_step(nc, ins, outs, debug=None):
    K = Kernel()
    K.nc, K.o = nc, outs
    K.x, K.norm1_g, K.rot, K.w_gate, K.b_gate = (ins[n] for n in ("x", "norm1_g", "rot", "w_gate", "b_gate"))
    K.w_conv, K.b_conv, K.k_scale, K.state_conv = (ins[n] for n in ("w_conv", "b_conv", "k_scale", "state_conv"))
    K.w_qk, K.w_tok, K.ins = ins["w_qk"], ins["w_tok"], ins
    K.new_conv_prompt = outs["conv_prompt"].rearrange("a b w c -> (a b w) c")
    K.new_conv_sample = outs["conv_sample"].rearrange("a b w c -> (a b w) c")

    def dram(name, shape):
        kind = "ExternalOutput" if debug and name in debug else "Internal"
        return nc.dram_tensor(name, shape, F32, kind=kind).ap()

    K.proj = dram("proj", (5, ROWS, AW))
    K.qkt = dram("qkt", (8, P, NT))
    K.dram = dram
    K.parts = dram("parts", (3, SEQ, H * (HD + 2)))
    K.mix = dram("mix", (ROWS, D))
    K.x2 = dram("x2", (ROWS, D))
    K.ng_rows = dram("ng_rows", (NCH * MH, P))
    K.ng_sample = dram("ng_sample", (DEC_B * MH, DEC_T))
    K.sm_own_kwm, K.sm_own_ms = 6, 15
    K.gt_own_scan, K.gt_own_m, K.gt_own_g, K.gt_own_mn = 4, 5, 9, 10
    with ExitStack() as ctx:
        stage_sems = []

        def sem(name):
            stage_sems.append(nc.alloc_semaphore(name=name))
            return stage_sems[-1]

        K.sem = sem
        K.ident = ctx.enter_context(nc.sbuf_tensor("ident", [P, P], F32))
        K.gates = ctx.enter_context(nc.sbuf_tensor("gates", [P, TILES, 8], F32))
        K.tab_p = ctx.enter_context(nc.sbuf_tensor("tab_p", [P, 4, NCH * MH], F32))
        K.tab_s = ctx.enter_context(nc.sbuf_tensor("tab_s", [NS, 4, MH], F32))
        K.wti = ctx.enter_context(nc.sbuf_tensor("wti", [P, (NCH + DEC_B) * MH], F32))
        K.ident_ready, K.ident_value = ctx.enter_context(nc.semaphore("ident_ready")), 2
        with nc.Block(no_gpsimd_drain=True) as block:
            @block.gpsimd
            def _(pool):
                nc.gpsimd.memset(K.ident[:], 0.0).then_inc(K.ident_ready, 1)
                pool.wait_ge(K.ident_ready, 1)
                nc.gpsimd.affine_select(out=K.ident[:], in_=K.ident[:], compare_op=ALU.not_equal, fill=1.0, base=0,
                                        pattern=[[-1, P]], channel_multiplier=1).then_inc(K.ident_ready, 1)
        for stage in STAGES:
            stage(K)
            nc.clear_and_free_semaphores(stage_sems)
            stage_sems.clear()
            nc.all_engine_barrier()


def lay_out(i):
    c = np.ascontiguousarray
    w_in = np.asarray(i["w_in"])[0]
    cols = lambda a, n: w_in[:, a:a + n].reshape(KC, P, n).transpose(1, 0, 2)
    qk0 = 3 * AW
    x = np.zeros((ROWS, D), np.float32)
    x[0:SEQ] = np.asarray(i["x_prompt"])[0]
    x[SEQ:NT] = np.asarray(i["x_sample"]).reshape(NS, D)
    half = ROT // 2
    freq = (np.float32(500000.0) ** (-np.arange(half, dtype=np.float32) / half)).astype(np.float32)
    pos = np.zeros(ROWS, np.float32)
    pos[0:SEQ] = np.arange(SEQ)
    pos[SEQ:NT] = np.tile(4096 + np.arange(DEC_T), DEC_B)
    ang = (pos[:, None] * freq[None, :]).astype(np.float32)
    cos, sin = np.cos(ang).astype(np.float32), np.sin(ang).astype(np.float32)
    rot = np.zeros((2, ROWS, 2 * ROT), np.float32)
    rot[0] = np.concatenate([cos, cos, -sin, sin], 1)
    rot[1, :, 0:ROT] = 1.0
    ksc = np.ones((P, 8), np.float32)
    ksc[:, 4:8] = np.float32(MD ** -0.5)
    mask, count = sample_tables()
    chunk_mask, token_seq = sample_chunk_tables()
    return {
        "sample_mask": mask, "sample_count": count, "chunk_mask": chunk_mask, "token_seq": token_seq,
        "x": x, "norm1_g": c(np.asarray(i["norm1_g"])[0]),
        "rot": c(rot.reshape(2, TILES, P, 2 * ROT).transpose(2, 0, 1, 3)),
        "w_gate": c(cols(qk0 + 4 * MW, 8)), "b_gate": c(np.asarray(i["b_gate"])[0]),
        "w_conv": c(np.asarray(i["w_conv"])[0].reshape(CONVW, 8, P).transpose(2, 1, 0)),
        "b_conv": c(np.asarray(i["b_conv"])[0].reshape(8, P).T), "k_scale": ksc,
        "state_conv": c(np.asarray(i["state_conv"]).reshape(24, 2 * MW)),
        "w_qk": c(np.stack([cols(qk0 + P * k, P) for k in range(8)]).reshape(8, P, KC * P)),
        "w_tok": c(np.stack([cols(a, 512) for a in (0, AW, 2 * AW, qk0 + 2 * MW, qk0 + 3 * MW)])),
        "cache_k": c(np.asarray(i["cache_win_k"]).reshape(DEC_B, WB, AW)),
        "cache_v": c(np.asarray(i["cache_win_v"]).reshape(DEC_B, WB, AW)),
        "state_C": c(np.asarray(i["state_C"])[0]), "state_n": c(np.asarray(i["state_n"])[0]),
        "state_m": c(np.asarray(i["state_m"]).reshape(DEC_B * MH, 1)),
        "mh_norm_g": c(np.asarray(i["mh_norm_g"])[0]),
        "w_out": c(np.asarray(i["w_out"])[0].reshape(KC, P, D).transpose(1, 0, 2)),
        "norm2_g": c(np.asarray(i["norm2_g"])[0]),
        "w_up": c(np.asarray(i["w_up"])[0].reshape(KC, P, 16, 256).transpose(2, 1, 0, 3)),
        "w_down": c(np.asarray(i["w_down"])[0].reshape(16, 2, P, D).transpose(0, 2, 1, 3)),
        "norm_f_g": c(np.asarray(i["norm_f_g"])),
    }


def kernel(**inputs):
    import concourse.bacc as _bacc
    from concourse.bass_utils import run_bass_kernel_spmd as _run

    nc = _bacc.Bacc("TRN2", target_bir_lowering=False, num_devices=1)
    arrays = {"in_" + n: a for n, a in lay_out(inputs).items()}
    ins = {n: nc.dram_tensor("in_" + n, s, F32, kind="ExternalInput").ap() for n, s in INPUTS}
    outs = {n: nc.dram_tensor("out_" + n, s, F32, kind="ExternalOutput").ap() for n, s in OUTPUTS}
    hybrid_step(nc, ins, outs)
    r = _run(nc, [arrays], core_ids=[0])
    return tuple(r.results[0]["out_" + n] for n, _ in OUTPUTS)
```

```python
import numpy as np
import concourse.bass as bass
from concourse import mybir
from contextlib import ExitStack

F32 = mybir.dt.float32
F32R = mybir.dt.float32r
BF16 = mybir.dt.bfloat16
ALU = mybir.AluOpType
ACT = mybir.ActivationFunctionType
AX = mybir.AxisListType

P = 128
D = 1024
KC = D // P
SEQ = 2048
DEC_B, DEC_T = 8, 8
NS = DEC_B * DEC_T
NT = SEQ + NS
TILES = SEQ // P + 1
ROWS = TILES * P
H, HD = 8, 64
AW = H * HD
ROT = HD // 4
MH, MD = 4, 128
MW = MH * MD
DFF = 4 * D
WB = 2048
EPS = 1e-6
NEG = -1.0e30
NCH = SEQ // P
QK, KK, VK, OB, VB = range(5)
CONVW = 4
LN_EXP = "natural_log_exp_and_others"


class Chain:

    def __init__(self, eng, sem):
        self.eng, self.sem, self.n, self.moved = eng, sem, 0, 0

    def mark(self, ins):
        ins.then_inc(self.sem, 1)
        self.n += 1

    def wait(self):
        self.eng.wait_ge(self.sem, self.n + self.moved)

    def link(self, ins):
        self.mark(ins)
        self.wait()

    def loop(self, trips, per):
        return _ChainLoop(self, trips, per)


class _ChainLoop:
    def __init__(self, chain, trips, per):
        self.chain, self.trips, self.per = chain, trips, per

    def __enter__(self):
        self.fori = self.chain.eng.Fori(0, self.trips)
        i = self.fori.__enter__()
        self.start = self.chain.n
        self.chain.moved = i * self.per
        return i

    def __exit__(self, *e):
        if e[0] is None:
            assert self.chain.n - self.start == self.per, (self.chain.n - self.start, self.per)
        self.chain.n = self.start + self.trips * self.per
        self.chain.moved = 0
        return self.fori.__exit__(*e)


class Norm:

    def __init__(self, nc, sem, tag, rows_of, xb, xn, small, gain, hi, lo, tr, ident):
        self.nc, self.rows_of, self.xb, self.xn, self.small, self.gain = nc, rows_of, xb, xn, small, gain
        self.hi, self.lo, self.tr, self.ident = hi, lo, tr, ident
        self.x_in = [sem(f"{tag}_x_in{s}") for s in range(2)]
        self.ssq, self.var, self.root, self.xn_ready, self.turned, self.hi_ready, self.lo_ready = (
            sem(f"{tag}_{n}") for n in ("ssq", "var", "root", "xn", "turned", "hi", "lo"))

    def load(self, sp, T, s, first):
        if not first:
            sp.wait_ge(self.xn_ready, T - 1)
        sp.dma_start(self.xb[:, s], self.rows_of(T)).then_inc(self.x_in[s], 16)

    def act_stats(self, act, T, s, half, first):
        act.wait_ge(self.x_in[s], 16 * half + 16)
        if not first:
            act.wait_ge(self.turned, T - 1)
        q = self.small
        self.nc.scalar.activation(self.xn[:, s], self.xb[:, s], ACT.Square,
                                  accum_out=q[:, s, 0:1]).then_inc(self.ssq, 1)
        act.wait_ge(self.var, T + 1)
        self.nc.scalar.activation(q[:, s, 2:3], q[:, s, 1:2], ACT.Ln).then_inc(self.root, 1)
        act.wait_ge(self.root, 2 * T + 1)
        self.nc.scalar.activation(q[:, s, 3:4], q[:, s, 2:3], ACT.Exp, scale=-0.5).then_inc(self.root, 1)

    def dve_scale(self, dve, chain, T, s):
        v, q = self.nc.vector, self.small
        dve.wait_ge(self.ssq, T + 1)
        v.tensor_scalar(q[:, s, 1:2], q[:, s, 0:1], 1.0 / D, EPS, ALU.mult, ALU.add).then_inc(self.var, 1)
        dve.wait_ge(self.root, 2 * T + 2)
        chain.link(v.tensor_tensor(q[:, s, 4:5], q[:, s, 3:4], q[:, s, 3:4], ALU.mult))
        chain.link(v.tensor_tensor(q[:, s, 5:6], q[:, s, 4:5], q[:, s, 1:2], ALU.mult))
        chain.link(v.tensor_scalar(q[:, s, 6:7], q[:, s, 5:6], -0.5, 1.5, ALU.mult, ALU.add))
        chain.link(v.tensor_tensor(q[:, s, 7:8], q[:, s, 6:7], q[:, s, 3:4], ALU.mult))
        v.scalar_tensor_tensor(self.xn[:, s], self.xb[:, s], q[:, s, 7:8], self.gain[:],
                               ALU.mult, ALU.mult).then_inc(self.xn_ready, 1)

    def pe_turn(self, pe, T, s, first):
        pe.wait_ge(self.xn_ready, T + 1)
        if not first:
            pe.wait_ge(self.lo_ready, T - 1)
        for k in range(KC):
            last = self.nc.tensor.transpose(self.tr[2 * s + k // 4][:, (k % 4) * P:(k % 4 + 1) * P],
                                            self.xn[:, s, k * P:(k + 1) * P], self.ident[:])
        last.then_inc(self.turned, 1)

    def act_hi(self, act, T, s, col):
        act.wait_ge(self.turned, T + 1)
        for half in range(2):
            last = self.nc.scalar.activation(self.hi[:, 4 * half:4 * half + 4, bass.ds(col, P)],
                                             self.tr[2 * s + half][:].rearrange("p (k c) -> p k c", k=4), ACT.Copy)
        last.then_inc(self.hi_ready, 1)

    def dve_lo(self, dve, T, s, col):
        dve.wait_ge(self.hi_ready, T + 1)
        for half in range(2):
            last = self.nc.vector.tensor_tensor(
                self.lo[:, 4 * half:4 * half + 4, bass.ds(col, P)],
                self.tr[2 * s + half][:].rearrange("p (k c) -> p k c", k=4),
                self.hi[:, 4 * half:4 * half + 4, bass.ds(col, P)].bitcast(F32), ALU.subtract)
        last.then_inc(self.lo_ready, 1)


    def sync_group(self, sp, n, between=None):
        for t in range(2):
            self.load(sp, t, t, True)
        if between:
            between()
        with sp.Fori(1, n // 2) as i:
            for j in range(2):
                self.load(sp, 2 * i + j, j, False)

    def act_group(self, act, n, between=None):
        self.act_stats(act, 0, 0, 0, True)
        self.act_stats(act, 1, 1, 0, True)
        self.act_hi(act, 0, 0, 0)
        self.act_stats(act, 2, 0, 1, False)
        self.act_hi(act, 1, 1, P)
        if between:
            between()
        full = (n - 3) // 2
        with act.Fori(1, full + 1) as i:
            for j in range(2):
                self.act_stats(act, 2 * i + j + 1, (j + 1) % 2, i + (j + 1) // 2, False)
                self.act_hi(act, 2 * i + j, j, (2 * i + j) * P)
        for t in range(2 + 2 * full, n):
            if t + 1 < n:
                self.act_stats(act, t + 1, (t + 1) % 2, (t + 1) // 2, False)
            self.act_hi(act, t, t % 2, t * P)

    def dve_group(self, dve, chain, n):
        self.dve_scale(dve, chain, 0, 0)
        full = (n - 1) // 2
        with chain.loop(full, 8) as i:
            for j in range(2):
                self.dve_scale(dve, chain, 2 * i + j + 1, (j + 1) % 2)
                self.dve_lo(dve, 2 * i + j, j, (2 * i + j) * P)
        for t in range(2 * full, n):
            if t + 1 < n:
                self.dve_scale(dve, chain, t + 1, (t + 1) % 2)
            self.dve_lo(dve, t, t % 2, t * P)

    def pe_group(self, pe, n, after=None):
        for t in range(n):
            self.pe_turn(pe, t, t % 2, t < 2)
            if after:
                after(t)


def split_products(nc, out, pairs, last_inc=None, before=None):
    n = len(pairs)
    for k, (ah, al, bh, bl) in enumerate(pairs):
        if before:
            before(k)
        nc.tensor.matmul(out, ah, bh, start=(k == 0), stop=False)
        nc.tensor.matmul(out, ah, bl, start=False, stop=False)
        ins = nc.tensor.matmul(out, al, bh, start=False, stop=(k == n - 1))
    if last_inc is not None:
        ins.then_inc(last_inc, 1)
    return ins


def project(K):
    nc, sem = K.nc, K.sem
    GT0, GN = (0, 8), (8, 9)
    SPLIT = 8 * P
    with ExitStack() as ctx:
        def sb(name, shape, dt=F32):
            return ctx.enter_context(nc.sbuf_tensor("p1_" + name, shape, dt))

        hT_hi = sb("hT_hi", [P, KC, 9 * P], F32R)
        hT_lo = sb("hT_lo", [P, KC, 9 * P], F32R)
        w_raw = sb("w_raw", [P, KC, 512])
        w_hi = [sb(f"w_hi{s}", [P, KC, 512], F32R) for s in range(2)]
        w_lo = [sb(f"w_lo{s}", [P, KC, 512], F32R) for s in range(2)]
        wq_hi = [w[:].rearrange("p k c -> p (k c)")[:, 0:KC * P].rearrange("p (k c) -> p k c", k=KC) for w in w_hi]
        wq_lo = [w[:].rearrange("p k c -> p (k c)")[:, 0:KC * P].rearrange("p (k c) -> p k c", k=KC) for w in w_lo]
        xb = sb("xb", [P, 2, D])
        wq_raw = xb[:, 1]
        xn = sb("xn", [P, 2, D])
        small = sb("small", [P, 2, 8])
        gain = sb("gain", [P, D])
        stage = sb("stage", [P, 3, AW])
        rot_a = sb("rot_a", [P, 2, H, ROT])
        rot_b = sb("rot_b", [P, 2, H, ROT])
        rot = sb("rot", [P, 2, TILES, 2 * ROT])
        wg_raw = sb("wg_raw", [P, KC, 8])
        wg_hi = sb("wg_hi", [P, KC, 8], F32R)
        wg_lo = sb("wg_lo", [P, KC, 8], F32R)
        bg = sb("bg", [8, 1])
        raw = sb("raw", [P, 2, 3 + SPLIT])
        sraw = sb("sraw", [P, 2, DEC_B, 3 + DEC_T])
        acc = sb("acc", [P, 2, SPLIT + NS])
        sig = xn[:].rearrange("p s d -> p (s d)")[:, 0:SPLIT + NS]
        wcv = sb("wcv", [P, 8, CONVW])
        bcv = sb("bcv", [P, 8])
        ksc = sb("ksc", [P, 8])
        ct = sb("ct", [P, 8, 27])
        stT = sb("stT", [P, 8, 24])
        st24, lastrows = acc[0:24, 0, 0:8 * P], sig[0:27, 0:8 * P]
        bank = [ctx.enter_context(nc.psum_tensor(f"p1_bank{i}", [P, 512], F32)) for i in range(8)]
        ident = K.ident

        wq_in, wt_in, hi_half, lo_half = sem("p1_wq_in"), sem("p1_wt_in"), sem("p1_hi_half"), sem("p1_lo_half")
        gain_in = sem("p1_gain_in")
        const_in, hi_ready, lo_ready = sem("p1_const_in"), sem("p1_w_hi"), sem("p1_w_lo")
        wg_hi_ready, wg_lo_ready = sem("p1_wg_hi"), sem("p1_wg_lo")
        qk_mm, qk_out = sem("p1_qk_mm"), sem("p1_qk_evac")
        tok_mm, tok_ready, gate_mm, gate_ready = sem("p1_tok_mm"), sem("p1_tok_ready"), sem("p1_gate_mm"), sem("p1_gate_ready")
        conv_done, sig_done, conv_out = sem("p1_conv_done"), sem("p1_sig_done"), sem("p1_conv_out")
        stage_out = [sem(f"p1_stage_out{s}") for s in range(3)]
        acc_out = [sem(f"p1_acc_out{s}") for s in range(2)]
        gate_out = sem("p1_gate_out")
        gated, dve_own, pe_state, act_state = sem("p1_gated"), sem("p1_dve_own"), sem("p1_pe_state"), sem("p1_act_state")
        tail_zero, tail_mm, tail_ev, tail_out = sem("p1_tail_zero"), sem("p1_tail_mm"), sem("p1_tail_ev"), sem("p1_tail_out")
        xv = K.x.rearrange("(t p) d -> t p d", p=P)

        norm = Norm(nc, sem, "p1", lambda T: xv[T], xb, xn, small, gain, hT_hi, hT_lo,
                    [bank[4], bank[5], bank[6], bank[7]], ident)

        GB = (2, 3, 6)
        GW = ((512, 512), (512, 512, NS))
        NPC = (2, 3)
        QB = (0, 16)

        block = ctx.enter_context(nc.Block(no_gpsimd_drain=True))

        @block.sync
        def _(sp):
            def constants():
                sp.dma_start(gain[:], K.norm1_g.partition_broadcast(P)).then_inc(gain_in, 16)
                for dst, src in ((wg_raw[:], K.w_gate), (bg[:], K.b_gate.rearrange("(g a) -> g a", a=1)),
                                 (st24, K.state_conv), (wcv[:], K.w_conv), (bcv[:], K.b_conv), (ksc[:], K.k_scale),
                                 (rot[:], K.rot)):
                    sp.dma_start(dst, src).then_inc(const_in, 16)

            for g in range(2):
                if g == 0:
                    norm.sync_group(sp, GN[0], constants)
                else:
                    for T in range(GT0[1], GT0[1] + GN[1]):
                        norm.load(sp, T, T % 2, False)
                base = 13 * g
                sp.wait_ge(norm.xn_ready, 8 + 8 * g)
                sp.dma_start(wq_raw, K.w_qk[0]).then_inc(wq_in, 16)
                if g:
                    sp.wait_ge(lo_ready, base)
                sp.dma_start(w_raw[:], K.w_tok[0]).then_inc(wt_in, 16)
                with sp.Fori(1, 8) as c:
                    sp.wait_ge(lo_ready, c + base)
                    sp.dma_start(wq_raw, K.w_qk[c]).then_inc(wq_in, 16)
                with sp.Fori(1, 5) as b:
                    sp.wait_ge(lo_ready, b + (base + 8))
                    sp.dma_start(w_raw[:], K.w_tok[b]).then_inc(wt_in, 16)

        @block.gpsimd
        def _(pool):
            nc.gpsimd.memset(ct[:], 0.0).then_inc(tail_zero, 1)
            pool.wait_ge(wg_hi_ready, 1)
            nc.gpsimd.tensor_tensor(wg_lo[:], wg_raw[:], wg_hi[:].bitcast(F32), ALU.subtract).then_inc(wg_lo_ready, 1)

            def lo(E, dst, hi, src):
                pool.wait_ge(hi_ready, E + 1)
                nc.gpsimd.tensor_tensor(dst, src, hi.bitcast(F32), ALU.subtract).then_inc(lo_ready, 1)

            def lo_token(g, b, j):
                for e, (before, after) in enumerate(((hi_half, lo_half), (hi_ready, lo_ready))):
                    pool.wait_ge(before, b + (5 * g + 1 if e == 0 else 13 * g + 9))
                    k = slice(4 * e, 4 * e + 4)
                    nc.gpsimd.tensor_tensor(w_lo[j][:, k], w_raw[:, k], w_hi[j][:, k].bitcast(F32), ALU.subtract).then_inc(after, 1)

            qr = wq_raw.rearrange("p (k c) -> p k c", k=KC)
            for g in range(2):
                base = 13 * g
                with pool.Fori(0, 4) as i:
                    for j in range(2):
                        lo(base + 2 * i + j, wq_lo[j], wq_hi[j], qr)
                with pool.Fori(0, 2) as i:
                    for j in range(2):
                        lo_token(g, 2 * i + j, j)
                lo_token(g, 4, 0)

        @block.scalar
        def _(act):
            def constants():
                act.wait_ge(const_in, 16 * 7)
                nc.scalar.activation(wg_hi[:], wg_raw[:], ACT.Copy).then_inc(wg_hi_ready, 1)
                act.wait_ge(pe_state, 1)
                nc.scalar.activation(stT[:], bank[0][:, 0:8 * 24].rearrange("p (k c) -> p k c", k=8),
                                     ACT.Copy).then_inc(act_state, 1)

            def round_chunk(g, c, j, free=None):
                act.wait_ge(wq_in, 16 * (c + (8 * g + 1)))
                if free:
                    act.wait_ge(*free)
                nc.scalar.activation(wq_hi[j], qr, ACT.Copy).then_inc(hi_ready, 1)

            def round_block(g, b, free):
                act.wait_ge(wt_in, 16 * (b + (5 * g + 1)))
                act.wait_ge(*free)
                for e, done in enumerate((hi_half, hi_ready)):
                    k = slice(4 * e, 4 * e + 4)
                    nc.scalar.activation(w_hi[b % 2][:, k], w_raw[:, k], ACT.Copy).then_inc(done, 1)

            qr = wq_raw.rearrange("p (k c) -> p k c", k=KC)

            def evac(g, c, j, slot_used=True):
                n, qb = NPC[g], QB[g]
                if slot_used:
                    act.wait_ge(conv_out, 8 * g + c - 1)
                nc.scalar.activation(raw[:, j, 0:3], ct[:, bass.ds(c, 1), 0:3].rearrange("p a b -> p (a b)"), ACT.Copy)
                if g == 1:
                    nc.scalar.activation(sraw[:, j, :, 0:3],
                                         stT[:, bass.ds(c, 1), :].rearrange("p a (b w) -> p (a b) w", w=3), ACT.Copy)
                for q in range(2):
                    act.wait_ge(qk_mm, qb + n * c + q + 1)
                    nc.scalar.activation(raw[:, j, 3 + 512 * q:3 + 512 * (q + 1)], bank[q][:], ACT.Copy).then_inc(qk_out, 1)
                if g == 1:
                    act.wait_ge(qk_mm, qb + n * c + 3)
                    nc.scalar.activation(sraw[:, j, :, 3:3 + DEC_T],
                                         bank[2][:, 0:NS].rearrange("p (b t) -> p b t", b=DEC_B), ACT.Copy).then_inc(qk_out, 1)

            def squash(g, c, j):
                w = SPLIT + (NS if g else 0)
                act.wait_ge(conv_done, 8 * g + c + 1)
                nc.scalar.activation(sig[:, 0:w], acc[:, j, 0:w], ACT.Sigmoid).then_inc(sig_done, 1)

            def store(g, c, j):
                w = SPLIT + (NS if g else 0)
                act.wait_ge(conv_out, 8 * g + c + 1)
                act.dma_start(K.qkt[c, :, SPLIT * g:SPLIT * g + w], acc[:, j, 0:w]).then_inc(acc_out[j], 16)

            def keep(g, b, t, slot):
                T = GT0[g] + t
                act.wait_ge(tok_ready, 40 * g + b * GN[g] + t + 1)
                if b == OB:
                    nc.scalar.activation(stage[:, slot], stage[:, slot], ACT.Sigmoid).then_inc(gated, 1)
                    act.wait_ge(gated, T + 1)
                act.dma_start(K.proj[b, T * P:(T + 1) * P, :], stage[:, slot]).then_inc(stage_out[slot], 16)

            def store_gates(g):
                for q, w in enumerate(GW[g]):
                    act.wait_ge(gate_ready, 2 * g + q + 1)
                    for kind in range(2):
                        src = stage[MH * kind:MH * (kind + 1), q, 0:w]
                        if w == 512:
                            dst = K.gate_rows[kind].rearrange("(c h) p -> h c p", h=MH)[:, 8 * g + 4 * q:8 * g + 4 * q + 4]
                            src = src.rearrange("h (c p) -> h c p", p=P)
                        else:
                            dst = K.gate_sample[kind].rearrange("(b h) t -> h b t", h=MH)
                            src = src.rearrange("h (b t) -> h b t", t=DEC_T)
                        act.dma_start(dst, src).then_inc(gate_out, 16)

            for g in range(2):
                n, nn = NPC[g], GN[g]
                if g == 0:
                    nc.scalar.preload_act_table_set(LN_EXP)
                    norm.act_group(act, nn, constants)
                    act.wait_ge(act_state, 1)
                    act.wait_ge(tail_zero, 1)
                round_chunk(g, 0, 0, (tok_mm, 40) if g else None)
                round_chunk(g, 1, 1, (tok_mm, 32) if g else None)
                store_gates(g)
                evac(g, 0, 0, g > 0)
                squash(g, 0, 0)
                round_chunk(g, 2, 0, (qk_mm, QB[g] + n))
                evac(g, 1, 1, g > 0)
                store(g, 0, 0)
                squash(g, 1, 1)
                with act.Fori(1, 3) as i:
                    for j in range(2):
                        round_chunk(g, 2 * i + j + 1, 1 - j, (qk_mm, QB[g] + n * (2 * i + j)))
                        evac(g, 2 * i + j, j)
                        store(g, 2 * i + j - 1, 1 - j)
                        squash(g, 2 * i + j, j)
                round_chunk(g, 7, 1, (qk_mm, QB[g] + n * 6))
                evac(g, 6, 0)
                round_block(g, 0, (qk_mm, QB[g] + n * 7))
                store(g, 5, 1)
                squash(g, 6, 0)
                evac(g, 7, 1)
                store(g, 6, 0)
                squash(g, 7, 1)
                store(g, 7, 1)
                R = 2 if g == 0 else 3
                round_block(g, 1, (qk_mm, QB[g] + n * 8))
                for t in range(nn):
                    keep(g, 0, t, t % R)
                round_block(g, 2, (tok_mm, 40 * g + nn))
                for t in range(nn):
                    keep(g, 1, t, t % R)
                round_block(g, 3, (tok_mm, 40 * g + 2 * nn))
                for t in range(nn):
                    keep(g, 2, t, t % R)
                round_block(g, 4, (tok_mm, 40 * g + 3 * nn))
                for t in range(nn):
                    keep(g, 3, t, t % R)
                if g == 0:
                    nc.scalar.preload_act_table_set(LN_EXP)
                    norm.act_stats(act, nn, 0, nn // 2, False)
                for t in range(nn):
                    keep(g, 4, t, t % R)
                    if g == 0:
                        T = nn + t
                        norm.act_stats(act, T + 1, (T + 1) % 2, (T + 1) // 2, False)
                        norm.act_hi(act, T, T % 2, t * P)
                if g == 0:
                    norm.act_hi(act, 2 * nn, 0, nn * P)
            act.wait_ge(tail_mm, 1)
            for half in range(2):
                nc.scalar.activation(lastrows[:, 512 * half:512 * half + 512], bank[half][0:27, :],
                                     ACT.Copy).then_inc(tail_ev, 1)
            act.wait_ge(tail_ev, 2)
            act.dma_start(K.new_conv_prompt, lastrows[0:3, :]).then_inc(tail_out, 16)
            act.dma_start(K.new_conv_sample, lastrows[3:27, :]).then_inc(tail_out, 16)
            act.wait_ge(tail_out, 32)
            for s in range(3):
                act.wait_ge(stage_out[s], 16 * (15 + (20 if s < 2 else 0)))
            for s in range(2):
                act.wait_ge(acc_out[s], 16 * 8)

        @block.vector
        def _(dve):
            chain = Chain(dve, dve_own)
            v = nc.vector
            dve.wait_ge(gain_in, 16)

            def conv(g, c, j, stored):
                dve.wait_ge(qk_out, QB[g] + NPC[g] * (c + 1))
                if stored is not None:
                    dve.wait_ge(acc_out[j], 16 * stored)
                views = [(raw[:, j, :], acc[:, j, 0:SPLIT], lambda a, w: a[:, w:w + SPLIT])]
                if g:
                    views.append((sraw[:, j], acc[:, j, SPLIT:SPLIT + NS].rearrange("p (b t) -> p b t", b=DEC_B),
                                  lambda a, w: a[:, :, w:w + DEC_T]))
                cw = [wcv[:, bass.ds(c, 1), w:w + 1].rearrange("p a b -> p (a b)") for w in range(CONVW)]
                cb = bcv[:, bass.ds(c, 1)]
                for src, dst, cut in views:
                    ins = v.tensor_scalar(dst, cut(src, 0), cw[0], cb, ALU.mult, ALU.add)
                chain.link(ins)
                for w in (1, 2, 3):
                    for src, dst, cut in views:
                        ins = v.scalar_tensor_tensor(dst, cut(src, w), cw[w], dst, ALU.mult, ALU.add)
                    if w < 3:
                        chain.link(ins)
                ins.then_inc(conv_done, 1)
                v.tensor_copy(ct[:, bass.ds(c, 1), 0:3].rearrange("p a b -> p (a b)"), raw[:, j, SPLIT:SPLIT + 3])
                if g:
                    v.tensor_copy(ct[:, bass.ds(c, 1), 3:27].rearrange("p a (b w) -> p (a b) w", w=3),
                                  sraw[:, j, :, DEC_T:DEC_T + 3])
                w = SPLIT + (NS if g else 0)
                dve.wait_ge(sig_done, 8 * g + c + 1)
                v.scalar_tensor_tensor(acc[:, j, 0:w], sig[:, 0:w], ksc[:, bass.ds(c, 1)], acc[:, j, 0:w],
                                       ALU.mult, ALU.mult).then_inc(conv_out, 1)

            def tile_out(g, b, j, t, kind):
                R = 2 if g == 0 else 3
                n = GN[g]
                slot, s, T = t % R, (n * j + t) % 2, GT0[g] + t
                ev = 40 * g + b * n + t
                dve.wait_ge(tok_mm, ev + 1)
                uses = (20 if g and slot < 2 else 0) + b * (n // R) + t // R
                if not (isinstance(uses, int) and uses == 0):
                    dve.wait_ge(stage_out[slot], 16 * uses)
                ps = bank[2 + s][:].rearrange("p (h d) -> p h d", h=H)
                st = stage[:, slot].rearrange("p (h d) -> p h d", h=H)
                half = ROT // 2

                def tab(lo, hi):
                    a = rot[:, bass.ds(kind, 1), T, lo:hi]
                    return a.broadcast_to([P, H, hi - lo])

                v.tensor_tensor(rot_a[:, s], ps[:, :, 0:ROT], tab(0, ROT), ALU.mult)
                v.tensor_tensor(rot_b[:, s, :, 0:half], ps[:, :, half:ROT], tab(ROT, ROT + half), ALU.mult)
                v.tensor_tensor(rot_b[:, s, :, half:ROT], ps[:, :, 0:half], tab(ROT + half, 2 * ROT), ALU.mult)
                chain.link(v.tensor_copy(stage[:, slot], bank[2 + s][:]))
                v.tensor_tensor(st[:, :, 0:ROT], rot_a[:, s], rot_b[:, s], ALU.add).then_inc(tok_ready, 1)

            for g in range(2):
                n = GN[g]
                if g == 0:
                    norm.dve_group(dve, chain, n)
                    dve.wait_ge(const_in, 16 * 7)
                    dve.wait_ge(pe_state, 1)
                if g:
                    for slot in range(2):
                        dve.wait_ge(stage_out[slot], 16 * 20)
                for q, w in enumerate(GW[g]):
                    dve.wait_ge(gate_mm, 2 * g + q + 1)
                    v.tensor_scalar(stage[0:8, q, 0:w], bank[GB[q]][0:8, 0:w], bg[:, 0:1], None, ALU.add).then_inc(gate_ready, 1)
                if g == 0:
                    dve.wait_ge(tail_zero, 1)
                for c in range(2):
                    conv(g, c, c, 4 if g else None)
                with chain.loop(3, 6) as i:
                    for j in range(2):
                        conv(g, 2 * i + 2 + j, j, i + (4 * g + 1))
                dve.wait_ge(gate_out, 64 if g == 0 else 64 + 96)
                with chain.loop(2, 2 * n) as i:
                    for j in range(2):
                        for t in range(n):
                            tile_out(g, 2 * i + j, j, t, i)
                if g == 0:
                    norm.dve_scale(dve, chain, n, 0)
                for t in range(n):
                    tile_out(g, 4, 0, t, 1)
                    if g == 0:
                        norm.dve_scale(dve, chain, n + t + 1, (n + t + 1) % 2)
                        norm.dve_lo(dve, n + t, t % 2, t * P)
                if g == 0:
                    norm.dve_lo(dve, 2 * n, 0, n * P)

        @block.tensor
        def _(pe):
            pe.wait_ge(K.ident_ready, K.ident_value)

            def gates(g, q):
                w = GW[g][q]
                split_products(nc, bank[GB[q]][0:8, 0:w],
                               [(wg_hi[:, k], wg_lo[:, k], hT_hi[:, k, 512 * q:512 * q + w],
                                 hT_lo[:, k, 512 * q:512 * q + w]) for k in range(KC)], gate_mm)

            def between(t):
                if t == 1:
                    pe.wait_ge(const_in, 16 * 7)
                    for k in range(8):
                        last = nc.tensor.transpose(bank[0][:, 24 * k:24 * k + 24], st24[:, k * P:(k + 1) * P], ident[0:24, 0:24])
                    last.then_inc(pe_state, 1)
                if t == 5:
                    pe.wait_ge(norm.lo_ready, 4)
                    pe.wait_ge(wg_lo_ready, 1)
                    gates(0, 0)

            def chunk(g, c, j, opening=False):
                n = NPC[g]
                pe.wait_ge(lo_ready, c + (13 * g + 1))
                for q in range(n):
                    w = 512 if q < 2 else NS
                    if not opening:
                        pe.wait_ge(qk_out, n * c + (QB[g] - n + q + 1))
                    elif g and q == 0:
                        pe.wait_ge(qk_out, QB[1])
                    elif g and q == 2:
                        pe.wait_ge(gate_ready, 5)
                    split_products(nc, bank[q][:, 0:w],
                                   [(wq_hi[j][:, k], wq_lo[j][:, k], hT_hi[:, k, 512 * q:512 * q + w],
                                     hT_lo[:, k, 512 * q:512 * q + w]) for k in range(KC)], qk_mm)

            def tokens(g, b, j, turn=False):
                n = GN[g]
                for t in range(n):
                    ev = n * b + (40 * g + t)
                    if g == 0 and j == 0 and t == 0 and not isinstance(b, int):
                        pe.wait_ge(tok_ready, ev)
                    else:
                        pe.wait_ge(tok_ready, ev - 1)

                    def split(k):
                        if t == 0 and k in (0, 4):
                            pe.wait_ge((lo_half, lo_ready)[k // 4], b + (5 * g + 1, 13 * g + 9)[k // 4])

                    split_products(nc, bank[2 + (n * j + t) % 2][:],
                                   [(hT_hi[:, k, t * P:(t + 1) * P], hT_lo[:, k, t * P:(t + 1) * P],
                                     w_hi[j][:, k], w_lo[j][:, k]) for k in range(KC)], tok_mm, split)
                    if turn:
                        norm.pe_turn(pe, n + t, t % 2, False)

            for g in range(2):
                n = GN[g]
                if g == 0:
                    norm.pe_group(pe, n, between)
                    pe.wait_ge(norm.lo_ready, n)
                    gates(0, 1)
                    pe.wait_ge(act_state, 1)
                else:
                    pe.wait_ge(norm.lo_ready, 2 * n - 2)
                    pe.wait_ge(tok_ready, 40)
                    gates(1, 0)
                    gates(1, 1)
                    norm.pe_turn(pe, 2 * n - 2, 0, False)
                    pe.wait_ge(norm.lo_ready, 2 * n - 1)
                    gates(1, 2)
                chunk(g, 0, 0, True)
                chunk(g, 1, 1)
                with pe.Fori(1, 4) as i:
                    for j in range(2):
                        chunk(g, 2 * i + j, j)
                pe.wait_ge(qk_out, QB[g] + 8 * NPC[g])
                pe.wait_ge(gate_ready, 2 + 3 * g)
                with pe.Fori(0, 2) as i:
                    for j in range(2):
                        tokens(g, 2 * i + j, j)
                if g == 0:
                    tokens(0, 4, 0, turn=True)
                else:
                    tokens(1, 4, 0)
            pe.wait_ge(conv_out, 16)
            pe.wait_ge(qk_out, 16 + 24)
            for k in range(8):
                last = nc.tensor.transpose(bank[k // 4][0:27, (k % 4) * P:(k % 4 + 1) * P], ct[:, k, :], ident[:])
            last.then_inc(tail_mm, 1)


class GateTables:

    RP, RS = NCH * MH, DEC_B * MH
    R = RP + RS
    SCAN, M_DONE, G_DONE, LAST = 4, 5, 9, 10
    TABLES = ("u", "w_in", "e_mt", "w_T")

    def __init__(self, K, sb, bank):
        self.K, self.bank = K, bank
        R = self.R
        self.t = {n: sb("gt_" + n, [R, P]) for n in ("ig", "fg", "mag", "soft", "lf", "b", "u", "U", "g", "ng", "mt",
                                                     "w_in", "e_mt", "w_T", "ones")}
        col = sb("gt_col", [R, 8])
        self.MP, self.NGT, self.WTI, self.MN = (col[:, k:k + 1] for k in range(4))
        self.ends = sb("gt_ends", [MH, 2, NCH])
        self.msc = sb("gt_msc", [MH, NCH + 1])
        names = ("own", "pad", "gates_in", "ends_out", "ends_in", "m_out", "m_in", "ng_out",
                 "tabs_out", "fin", "pe_tab", "tab_ready", "act_step", "wti_in")
        self.s = {n: K.sem("gt_" + n) for n in names}
        self.ends_dram = K.dram("gate_ends", (2, self.RP))
        self.mprev_dram = K.dram("gate_mprev", (self.RP,))
        self.tab_dram = K.dram("gate_tab", (4, self.RS, DEC_T))
        self.wti_dram = K.dram("gate_wti", (R,))

    def pool(self, pool):
        g, s = self.K.nc.gpsimd, self.s
        RP, R = self.RP, self.R
        g.memset(self.t["ones"][:], 1.0).then_inc(s["pad"], 1)
        g.memset(self.msc[:], 0.0).then_inc(s["pad"], 1)
        pool.wait_ge(s["pad"], 2)
        g.memset(self.t["ig"][RP:R, DEC_T:P], NEG).then_inc(s["pad"], 1)
        g.memset(self.t["fg"][RP:R, DEC_T:P], 1.0e30).then_inc(s["pad"], 1)
        pool.wait_ge(s["pad"], 4)

    def sync_load(self, sp):
        K, s, t = self.K, self.s, self.t
        RP, R = self.RP, self.R
        for kind, name in ((0, "ig"), (1, "fg")):
            sp.dma_start(t[name][0:RP, :], K.gate_rows[kind]).then_inc(s["gates_in"], 16)
            sp.dma_start(t[name][RP:R, 0:DEC_T], K.gate_sample[kind]).then_inc(s["gates_in"], 16)
        sp.dma_start(self.MP[RP:R, :], K.ins["state_m"]).then_inc(s["gates_in"], 16)

    def sync(self, sp):
        K, nc, s, t = self.K, self.K.nc, self.s, self.t
        RP = self.RP
        with nc.allow_non_contiguous_dma(reason="a few words"):
            sp.wait_ge(s["own"], self.SCAN)
            sp.dma_start(self.ends_dram[0].rearrange("(r a) -> r a", a=1), t["U"][0:RP, P - 1:P]).then_inc(s["ends_out"], 16)
            sp.dma_start(self.ends_dram[1].rearrange("(r a) -> r a", a=1), t["b"][0:RP, P - 1:P]).then_inc(s["ends_out"], 16)
            sp.wait_ge(s["ends_out"], 32)
            sp.dma_start(self.ends[:], self.ends_dram.rearrange("k (c h) -> h k c", h=MH)).then_inc(s["ends_in"], 16)
            sp.wait_ge(s["own"], self.M_DONE)
            sp.dma_start(self.mprev_dram.rearrange("(c h) -> h c", h=MH), self.msc[:, 0:NCH]).then_inc(s["m_out"], 16)
            sp.wait_ge(s["m_out"], 16)
            sp.dma_start(self.MP[0:RP, :], self.mprev_dram.rearrange("(r a) -> r a", a=1)).then_inc(s["m_in"], 16)
            sp.dma_start(K.o["m_prompt"].rearrange("a b (h c) -> (a b h) c", c=1), self.msc[:, NCH:NCH + 1]).then_inc(s["fin"], 16)
            sp.wait_ge(s["own"], self.G_DONE)
            sp.dma_start(K.ng_rows, t["ng"][0:RP, :]).then_inc(s["ng_out"], 16)
            sp.wait_ge(s["act_step"], 7)
            sp.dma_start(self.wti_dram.rearrange("(r a) -> r a", a=1), self.WTI).then_inc(s["tabs_out"], 16)
            sp.wait_ge(s["ng_out"], 16)
            sp.wait_ge(s["tabs_out"], 16)
            sp.dma_start(K.wti[:], self.wti_dram.partition_broadcast(P)).then_inc(s["wti_in"], 16)

    def sync_sample(self, sp):
        K, nc, s, t = self.K, self.K.nc, self.s, self.t
        RP, R = self.RP, self.R
        with nc.allow_non_contiguous_dma(reason="a few words"):
            sp.dma_start(K.ng_sample, t["ng"][RP:R, 0:DEC_T]).then_inc(s["fin"], 16)
            sp.wait_ge(s["own"], self.LAST)
            sp.dma_start(K.o["m_sample"].rearrange("a b (h c) -> (a b h) c", c=1), self.MN[RP:R, :]).then_inc(s["fin"], 16)
            for k, n in enumerate(self.TABLES):
                sp.dma_start(self.tab_dram[k], t[n][RP:R, 0:DEC_T]).then_inc(s["tabs_out"], 16)
            sp.wait_ge(s["tabs_out"], 80)
            for k in range(4):
                for b in range(DEC_B):
                    sp.dma_start(K.tab_s[DEC_T * b:DEC_T * (b + 1), k, :],
                                 self.tab_dram[k, MH * b:MH * (b + 1), :].rearrange("h t -> t h")).then_inc(s["fin"], 16)

    def sync_end(self, sp):
        sp.wait_ge(self.s["fin"], 16 * (3 + 4 * DEC_B))

    def act_log(self, act):
        A, s, t = self.K.nc.scalar.activation, self.s, self.t
        act.wait_ge(s["gates_in"], 16 * 5)
        act.wait_ge(s["pad"], 4)
        own = self.own = Chain(act, s["act_step"])
        own.link(A(t["mag"][:], t["fg"][:], ACT.Abs))
        own.link(A(t["soft"][:], t["mag"][:], ACT.Exp, scale=-1.0))
        own.link(A(t["lf"][:], t["soft"][:], ACT.Ln, bias=1.0))

    def act_weights(self, act):
        A, s, t, own = self.K.nc.scalar.activation, self.s, self.t, self.own
        act.wait_ge(s["own"], self.G_DONE)
        act.wait_ge(s["m_in"], 16)
        own.mark(A(t["w_in"][:], t["g"][:], ACT.Exp, bias=self.MP, scale=-1.0))
        own.mark(A(t["e_mt"][:], t["mt"][:], ACT.Exp, scale=-1.0))
        own.mark(A(t["w_T"][:], t["u"][:], ACT.Exp, bias=self.NGT))
        own.mark(A(self.WTI, self.MP, ACT.Exp, bias=self.NGT))

    def dve(self, dve):
        K, s, t = self.K, self.s, self.t
        v, RP, MP = K.nc.vector, self.RP, self.MP
        chain = Chain(dve, s["own"])
        dve.wait_ge(s["act_step"], 3)
        chain.link(v.scalar_tensor_tensor(t["lf"][:], t["fg"][:], 0.0, t["lf"][:], ALU.min, ALU.subtract))
        chain.link(v.tensor_tensor_scan(t["b"][:], t["ones"][:], t["lf"][:], 0.0, ALU.mult, ALU.add))
        chain.link(v.tensor_tensor(t["u"][:], t["ig"][:], t["b"][:], ALU.subtract))
        chain.link(v.tensor_tensor_scan(t["U"][:], t["u"][:], t["u"][:], -3.0e38, ALU.max, ALU.max))
        assert chain.n == self.SCAN
        dve.wait_ge(s["ends_in"], 16)
        chain.link(v.tensor_tensor_scan(self.msc[:, 1:NCH + 1], self.ends[:, 0, :], self.ends[:, 1, :], 0.0, ALU.max, ALU.add))
        assert chain.n == self.M_DONE
        dve.wait_ge(s["m_in"], 16)
        chain.link(v.tensor_scalar(t["g"][:], t["U"][:], MP, None, ALU.max))
        chain.mark(v.tensor_scalar(t["ng"][:], t["g"][:], -1.0, None, ALU.mult))
        chain.link(v.tensor_tensor(t["mt"][:], t["b"][:], t["g"][:], ALU.add))
        chain.link(v.tensor_copy(self.NGT, t["ng"][:, P - 1:P]))
        assert chain.n == self.G_DONE
        chain.link(v.tensor_copy(self.MN, t["mt"][:, P - 1:P]))
        assert chain.n == self.LAST
        dve.wait_ge(s["pe_tab"], 1)
        v.tensor_copy(K.tab_p[:], self.bank[:, 0:4 * RP].rearrange("p (k r) -> p k r", k=4)).then_inc(s["tab_ready"], 1)
        dve.wait_ge(s["tab_ready"], 1)
        dve.wait_ge(s["wti_in"], 16)

    def pe(self, pe):
        s, RP = self.s, self.RP
        pe.wait_ge(s["act_step"], 7)
        for k, n in enumerate(self.TABLES):
            last = self.K.nc.tensor.transpose(self.bank[:, RP * k:RP * (k + 1)], self.t[n][0:RP, :], self.K.ident[0:RP, 0:RP])
        last.then_inc(s["pe_tab"], 1)


def mix_prompt(K):
    nc, sem = K.nc, K.sem
    HW = HD + 2
    VW = MD + 1
    STEPS = 4
    NZ = 10
    ZERO = 8
    UNIT = [0] * 4 + [1] * 4 + [2] * 2
    FIRSTZ = (0, 4, 8)
    LASTZ = (3, 7, 9)
    with ExitStack() as ctx:
        def sb(name, shape, dt=F32):
            return ctx.enter_context(nc.sbuf_tensor("mx_" + name, shape, dt))

        q_in = [sb(f"q_in{a}", [P, AW]) for a in range(3)]
        k_in = [sb(f"k_in{a}", [P, AW]) for a in range(3)]
        v_in = [sb(f"v_in{a}", [P, 2, AW]) for a in range(3)]
        qz = [sb(f"qz{a}", [P, H, P]) for a in range(3)]
        kT = [sb(f"kT{a}", [P, 2, H // 2, P]) for a in range(3)]
        probs = sb("probs", [P, 2, 512])
        probsT = sb("probsT", [P, 2, 512])
        part = [sb(f"part{a}", [P, 2, H, HW]) for a in range(3)]
        mk = sb("mk", [P, 2, 2, P], BF16)
        mk1 = sb("mk1", [P, 4, 2, P], BF16)
        identb = sb("identb", [P, P], BF16)
        maskT = sb("maskT", [P, P])
        mq = sb("mq", [P, 2, MH, P])
        mkk = sb("mkk", [P, 2, MH, P])
        vx = sb("vx", [P, 2, MH, VW])
        gb = sb("gb", [P, 2, MH, P])
        ob = sb("ob", [P, 2, MW])
        mhg = sb("mhg", [P, MW])
        tb = sb("tb", [P, 2, 4, MH])
        wt = sb("wt", [P, 2, MH])
        arg = sb("arg", [P, MH, P])
        wm = sb("wm", [P, MH, P])
        scT = sb("scT", [P, MH, P])
        kw = sb("kw", [P, MH, P])
        num = sb("num", [P, MH, VW])
        C = sb("C", [P, MH, VW])
        hh = sb("hh", [P, MH, MD])
        sq = sb("sq", [P, MH, MD])
        hg = sb("hg", [P, MH, MD])
        gs = sb("gs", [P, MW])
        hb = sb("hb", [P, 2, MH, MD])
        sm = sb("sm", [P, 10, MH])
        bank = [ctx.enter_context(nc.psum_tensor(f"mx_bank{i}", [P, 512], F32)) for i in range(8)]

        s = {n: sem("mx_" + n) for n in (
            "turned", "scores", "probs_turned", "summed", "ml_scores", "ml_num", "ml_inter", "ml_dC",
            "turned_out", "exps", "ml_w", "ml_num_out", "ml_rms",
            "maxes", "probsT_out", "unit_out", "ml_arg", "ml_sc", "ml_kw", "ml_num_done", "ml_h", "ml_C", "ml_hb",
            "own", "pool_own", "gs", "sq", "hg", "consts", "zeros", "fin", "ml_ms", "gain_in")}
        unit_in = [sem(f"mx_unit_in{a}") for a in range(3)]
        ml_in = [sem(f"mx_ml_in{p}") for p in range(2)]
        part_out = [[sem(f"mx_part_out{a}{p}") for p in range(2)] for a in range(3)]
        hb_out = [sem(f"mx_hb_out{p}") for p in range(2)]

        gates = GateTables(K, sb, bank[5])
        qkt = K.qkt

        def view(t, a, i, j):
            if a == 0:
                return t[0:SEQ].rearrange("(n p) c -> n p c", p=P)[4 * i + j]
            if a == 1:
                return t[0:SEQ].rearrange("(b p r) c -> r b p c", p=P, r=4)[i, j]
            return t[0:SEQ].rearrange("(p r) c -> r p c", r=16)[4 * i + j]

        block = ctx.enter_context(nc.Block(no_gpsimd_drain=True))

        @block.sync
        def _(sp):
            def load_unit(a, i, j):
                sp.dma_start(q_in[a][:], view(K.proj[QK], a, i, j)).then_inc(unit_in[a], 16)
                sp.dma_start(k_in[a][:], view(K.proj[KK], a, i, j)).then_inc(unit_in[a], 16)
                sp.dma_start(v_in[a][:, j % 2 if a < 2 else 0], view(K.proj[VK], a, i, j)).then_inc(unit_in[a], 16)

            def load_ml(n, p):
                x = ml_in[p]
                sp.dma_start(mq[:, p], qkt[0:MH, :, bass.ds(n * P, P)].rearrange("h p t -> p h t")).then_inc(x, 16)
                sp.dma_start(mkk[:, p], qkt[MH:2 * MH, :, bass.ds(n * P, P)].rearrange("h p t -> p h t")).then_inc(x, 16)
                sp.dma_start(vx[:, p, :, 0:MD], K.proj[VB, bass.ds(n * P, P), :].rearrange("p (h d) -> p h d", h=MH)).then_inc(x, 16)
                sp.dma_start(gb[:, p], K.ng_rows[bass.ds(MH * n, MH), :].partition_broadcast(P)).then_inc(x, 16)
                sp.dma_start(ob[:, p], K.proj[OB, bass.ds(n * P, P), :]).then_inc(x, 16)

            def turn(i, j, more, more_ml):
                n = 4 * i + j
                for a in range(3):
                    sp.wait_ge(s["unit_out"], 3 * n + a + 1)
                    sp.dma_start(view(K.parts[a], a, i, j), part[a][:, j % 2].rearrange("p h c -> p (h c)"))\
                        .then_inc(part_out[a][j % 2], 16)
                    if more:
                        load_unit(a, i + (j + 1) // 4, (j + 1) % 4)
                sp.wait_ge(s["ml_C"], n + 1)
                sp.wait_ge(s["gs"], n + 1)
                if more_ml:
                    load_ml(n + 2, j % 2)
                sp.wait_ge(s["ml_hb"], n + 1)
                sp.dma_start(K.mix[bass.ds(n * P, P), AW:D], hb[:, j % 2].rearrange("p h d -> p (h d)"))\
                    .then_inc(hb_out[j % 2], 16)

            gates.sync_load(sp)
            sp.dma_start(mhg[:], K.ins["mh_norm_g"].partition_broadcast(P)).then_inc(s["gain_in"], 16)
            for a in range(3):
                load_unit(a, 0, 0)
            gates.sync(sp)
            load_ml(0, 0)
            load_ml(1, 1)
            gates.sync_sample(sp)
            with sp.Fori(0, 3) as i:
                for j in range(STEPS):
                    turn(i, j, True, True)
            for j in range(STEPS):
                turn(3, j, j < 3, j < 2)
            sp.dma_start(K.o["C_prompt"][0, 0].rearrange("h d e -> d h e"), C[:, :, 0:MD]).then_inc(s["fin"], 16)
            with nc.allow_non_contiguous_dma(reason="the normaliser column"):
                sp.dma_start(K.o["n_prompt"][0, 0].rearrange("h (d e) -> d h e", e=1), C[:, :, MD:VW]).then_inc(s["fin"], 16)
            sp.wait_ge(s["fin"], 32)
            gates.sync_end(sp)
            for a in range(3):
                for p in range(2):
                    sp.wait_ge(part_out[a][p], 16 * 8)
            for p in range(2):
                sp.wait_ge(hb_out[p], 16 * 8)

        @block.gpsimd
        def _(pool):
            g = nc.gpsimd
            own = Chain(pool, s["pool_own"])
            gates.pool(pool)
            own.mark(g.memset(mk[:], 0.0))
            own.mark(g.memset(mk1[:], 0.0))
            own.mark(g.memset(maskT[:], 0.0))
            own.mark(g.tensor_copy(identb[:], K.ident[:]))
            own.wait()

            def keep_where(t, step, mult):
                own.mark(g.affine_select(out=t, in_=t, compare_op=ALU.is_ge, fill=NEG, base=0,
                                         pattern=[[step, P]], channel_multiplier=mult))

            for p in range(2):
                keep_where(mk[:, p, p], -1, 1)
                keep_where(mk[:, p, 1 - p], 1, -1)
            for i in range(4):
                keep_where(mk1[:, i, 0], -1, 1)
                if i:
                    keep_where(mk1[:, i, 1], 1, -1)
            own.mark(g.memset(mk1[:, 0, 1], NEG))
            keep_where(maskT[:], 1, -1)
            own.wait()
            g.memset(sm[:, 9], 0.0).then_inc(s["consts"], 1)
            pool.wait_ge(s["gain_in"], 16)
            with pool.Fori(0, 4) as i:
                for j in range(STEPS):
                    n, p = 4 * i + j, j % 2
                    pool.wait_ge(ml_in[p], 80 * (2 * i + j // 2 + 1))
                    pool.wait_ge(s["hg"], n)
                    g.tensor_tensor(gs[:], ob[:, p], mhg[:], ALU.mult).then_inc(s["gs"], 1)
                    pool.wait_ge(s["ml_h"], n + 1)
                    g.tensor_tensor(sq[:], hh[:], hh[:], ALU.mult).then_inc(s["sq"], 1)
                    pool.wait_ge(s["gs"], n + 1)
                    g.tensor_tensor(hg[:].rearrange("p h d -> p (h d)"), hh[:].rearrange("p h d -> p (h d)"), gs[:],
                                    ALU.mult).then_inc(s["hg"], 1)

        @block.scalar
        def _(act):
            A = nc.scalar.activation
            nc.scalar.preload_act_table_set(LN_EXP)
            gates.act_log(act)
            act.wait_ge(s["zeros"], ZERO)

            def q_out(a, n):
                act.wait_ge(s["turned"], 6 * n + (2 * a + 1))
                t = bank[4][:].rearrange("p (h c) -> p h c", h=4)
                for e in range(2):
                    r = slice(64 * e, 64 * e + 64)
                    ins = A(qz[a][r].rearrange("p (h e) c -> p h e c", e=2)[:, :, e], t[r], ACT.Copy, scale=HD ** -0.5)
                ins.then_inc(s["turned_out"], 1)

            def k_out(a, n, p):
                act.wait_ge(s["turned"], 6 * n + (2 * a + 2))
                A(kT[a][:, p if a < 2 else 0], bank[4][:].rearrange("p (h c) -> p h c", h=4), ACT.Copy).then_inc(s["turned_out"], 1)

            def exps(z, n, p):
                a = UNIT[z]
                w = 256 if a < 2 else P
                h0 = 2 * (z - FIRSTZ[a]) if a < 2 else 4 * (z - 8)
                act.wait_ge(s["maxes"], NZ * n + (z + 1))
                act.wait_ge(s["probs_turned"], NZ * n + max(z - 1, 0))
                for k in range(512 // w):
                    ins = A(probs[:, z % 2, w * k:w * (k + 1)], bank[z % 2][:, w * k:w * (k + 1)], ACT.Exp,
                            bias=part[a][:, p, h0 + k, HD:HD + 1], accum_out=part[a][:, p, h0 + k, HD + 1:HW])
                ins.then_inc(s["exps"], 1)

            def step(i, j, more=True):
                n, p = 4 * i + j, j % 2
                act.wait_ge(s["ml_arg"], n + 1)
                for h in range(MH):
                    ins = A(wm[:, h], arg[:, h], ACT.Exp, bias=tb[:, p, 0, h:h + 1])
                ins.then_inc(s["ml_w"], 1)
                exps(0, n, p)
                exps(1, n, p)
                q_out(1, n)
                exps(2, n, p)
                k_out(1, n, p)
                exps(3, n, p)
                act.wait_ge(s["ml_num"], n + 1)
                for e in range(2):
                    ins = A(num[:, 2 * e:2 * e + 2], bank[6 + e][:, 0:2 * VW].rearrange("p (h c) -> p h c", h=2), ACT.Copy)
                ins.then_inc(s["ml_num_out"], 1)
                exps(4, n, p)
                q_out(2, n)
                exps(5, n, p)
                k_out(2, n, p)
                for z in (6, 7, 8, 9):
                    exps(z, n, p)
                if more:
                    q_out(0, n + 1)
                act.wait_ge(s["ml_ms"], n + 1)
                A(sm[:, 3], sm[:, 2], ACT.Ln).then_inc(s["ml_rms"], 1)
                act.wait_ge(s["ml_rms"], 2 * n + 1)
                A(sm[:, 4], sm[:, 3], ACT.Exp, scale=-0.5).then_inc(s["ml_rms"], 1)
                if more:
                    k_out(0, n + 1, 1 - p)

            q_out(0, 0)
            k_out(0, 0, 0)
            gates.act_weights(act)
            with act.Fori(0, 3) as i:
                for j in range(STEPS):
                    step(i, j)
            for j in range(STEPS):
                step(3, j, j < 3)

        @block.vector
        def _(dve):
            v = nc.vector
            chain = Chain(dve, s["own"])
            for a in range(3):
                v.memset(qz[a][:], 0.0).then_inc(s["zeros"], 1)
            for a in range(2):
                v.memset(kT[a][:, 1], 0.0).then_inc(s["zeros"], 1)
                v.memset(v_in[a][:, 1], 0.0).then_inc(s["zeros"], 1)
            v.memset(vx[:, :, :, MD:VW], 1.0)
            v.memset(C[:], 0.0).then_inc(s["zeros"], 1)
            gates.dve(dve)
            dve.wait_ge(s["zeros"], ZERO)
            dve.wait_ge(s["consts"], 1)

            def bc(ap, w):
                return ap.rearrange("p (h a) -> p h a", a=1).broadcast_to([P, MH, w])

            def maxes(z, n, p, i, j):
                a = UNIT[z]
                w = 256 if a < 2 else P
                h0 = 2 * (z - FIRSTZ[a]) if a < 2 else 4 * (z - 8)
                if z in FIRSTZ:
                    dve.wait_ge(part_out[a][p], 16 * (2 * i + j // 2))
                dve.wait_ge(s["scores"], NZ * n + (z + 1))
                v.reduce_max(part[a][:, p, h0:h0 + 512 // w, HD:HD + 1], bank[z % 2][:].rearrange("p (h k) -> p h k", k=w),
                             AX.X, negate=True).then_inc(s["maxes"], 1)

            def pt_out(z, n):
                dve.wait_ge(s["probs_turned"], NZ * n + (z + 1))
                dve.wait_ge(s["summed"], NZ * n + max(z - 1, 0))
                v.tensor_copy(probsT[:, z % 2], bank[2 + z % 2][:]).then_inc(s["probsT_out"], 1)

            def unit_out(a, n, p):
                dve.wait_ge(s["summed"], NZ * n + (LASTZ[a] + 1))
                v.tensor_copy(part[a][:, p, :, 0:HD], bank[5][:].rearrange("p (h d) -> p h d", h=H)).then_inc(s["unit_out"], 1)

            def finish(n, p, stored):
                dve.wait_ge(s["ml_rms"], 2 * n + 2)
                chain.link(v.tensor_tensor(sm[:, 5], sm[:, 4], sm[:, 4], ALU.mult))
                chain.link(v.tensor_tensor(sm[:, 6], sm[:, 5], sm[:, 2], ALU.mult))
                chain.link(v.tensor_scalar(sm[:, 7], sm[:, 6], -0.5, 1.5, ALU.mult, ALU.add))
                chain.link(v.tensor_tensor(sm[:, 8], sm[:, 7], sm[:, 4], ALU.mult))
                dve.wait_ge(s["hg"], n + 1)
                dve.wait_ge(hb_out[p], 16 * stored)
                v.tensor_tensor(hb[:, p], hg[:], bc(sm[:, 8], MD), ALU.mult).then_inc(s["ml_hb"], 1)

            def step(i, j, prev):
                n, p = 4 * i + j, j % 2
                v.tensor_copy(tb[:, p], K.tab_p[:, :, bass.ds(MH * n, MH)])
                v.tensor_copy(wt[:, p], K.wti[:, bass.ds(MH * n, MH)])
                dve.wait_ge(ml_in[p], 80 * (2 * i + j // 2 + 1))
                v.tensor_tensor(arg[:], gb[:, p], maskT[:].rearrange("p (a t) -> p a t", a=1).broadcast_to([P, MH, P]),
                                ALU.add).then_inc(s["ml_arg"], 1)
                dve.wait_ge(s["ml_arg"], n + 1)
                maxes(0, n, p, i, j)
                dve.wait_ge(s["ml_scores"], 2 * n + 2)
                v.tensor_tensor(kw[:], bank[7][:].rearrange("p (h d) -> p h d", h=MH), bc(tb[:, p, 3], MD), ALU.mult).then_inc(s["ml_kw"], 1)
                dve.wait_ge(s["ml_w"], n + 1)
                v.tensor_tensor(scT[:], bank[6][:].rearrange("p (h t) -> p h t", h=MH), wm[:], ALU.mult).then_inc(s["ml_sc"], 1)
                maxes(1, n, p, i, j)
                pt_out(0, n)
                maxes(2, n, p, i, j)
                pt_out(1, n)
                if prev is not None:
                    finish(n - 1, 1 - p, prev)
                maxes(3, n, p, i, j)
                pt_out(2, n)
                maxes(4, n, p, i, j)
                pt_out(3, n)
                maxes(5, n, p, i, j)
                pt_out(4, n)
                unit_out(0, n, p)
                maxes(6, n, p, i, j)
                pt_out(5, n)
                dve.wait_ge(s["ml_inter"], n + 1)
                dve.wait_ge(s["ml_num_out"], n + 1)
                for h in range(MH):
                    ins = v.scalar_tensor_tensor(num[:, h], bank[6 + h // 2][:, VW * (h % 2):VW * (h % 2 + 1)],
                                                 tb[:, p, 1, h:h + 1], num[:, h], ALU.mult, ALU.add)
                ins.then_inc(s["ml_num_done"], 1)
                maxes(7, n, p, i, j)
                pt_out(6, n)
                dve.wait_ge(s["ml_num_done"], n + 1)
                chain.link(v.tensor_scalar(sm[:, 5], num[:, :, MD:VW].rearrange("p h a -> p (h a)"), -1.0, None, ALU.mult))
                chain.link(v.tensor_tensor(sm[:, 6], sm[:, 5], num[:, :, MD:VW].rearrange("p h a -> p (h a)"), ALU.max))
                chain.link(v.tensor_tensor(sm[:, 0], sm[:, 6], tb[:, p, 2], ALU.max))
                chain.link(v.reciprocal(sm[:, 1], sm[:, 0]))
                v.tensor_tensor(hh[:], num[:, :, 0:MD], bc(sm[:, 1], MD), ALU.mult).then_inc(s["ml_h"], 1)
                maxes(8, n, p, i, j)
                pt_out(7, n)
                maxes(9, n, p, i, j)
                pt_out(8, n)
                unit_out(1, n, p)
                dve.wait_ge(s["sq"], n + 1)
                chain.link(v.reduce_sum(sm[:, 7], sq[:], AX.X))
                v.tensor_scalar(sm[:, 2], sm[:, 7], 1.0 / MD, EPS, ALU.mult, ALU.add).then_inc(s["ml_ms"], 1)
                pt_out(9, n)
                dve.wait_ge(s["ml_dC"], n + 1)
                for h in range(MH):
                    ins = v.scalar_tensor_tensor(C[:, h], C[:, h], wt[:, p, h:h + 1],
                                                 bank[6 + h // 2][:, VW * (h % 2):VW * (h % 2 + 1)], ALU.mult, ALU.add)
                ins.then_inc(s["ml_C"], 1)
                unit_out(2, n, p)

            def before(i, j):
                return 2 * i + (j - 1) // 2

            for j in range(STEPS):
                step(0, j, before(0, j) if j else None)
            with chain.loop(3, 4 * 9) as i:
                for j in range(STEPS):
                    step(i + 1, j, before(i + 1, j))
            finish(NCH - 1, 1, NCH // 2 - 1)

        @block.tensor
        def _(pe):
            mm, tp = nc.tensor.matmul, nc.tensor.transpose
            pe.wait_ge(s["zeros"], ZERO)
            pe.wait_ge(s["consts"], 1)

            def turn(a, which, n):
                k = 2 * a + which
                pe.wait_ge(unit_in[a], 48 * (n + 1))
                pe.wait_ge(s["turned_out"], 6 * n + k)
                src = (q_in, k_in)[which][a]
                for c in range(4):
                    ins = tp(bank[4][:, c * P:(c + 1) * P], src[:, c * P:(c + 1) * P], K.ident[:])
                ins.then_inc(s["turned"], 1)

            def scores(z, n, i, j):
                a, p = UNIT[z], j % 2
                out = bank[z % 2]
                pe.wait_ge(s["turned_out"], 6 * n + 2 * (a + 1))
                pe.wait_ge(s["exps"], NZ * n + max(z - 1, 0))
                if a < 2:
                    if j:
                        m = mk[:, p]
                    else:
                        m = mk1[:, bass.ds(i, 1)].rearrange("p a s k -> p (a s) k") if a == 0 else mk1[:, 0]
                    m = m.rearrange("p s k -> p (s k)").rearrange("p (a c) -> p a c", a=1).broadcast_to([P, 2, 256])
                    h0, w = 2 * (z - FIRSTZ[a]), 256
                    ks = lambda h: kT[a][:, :, h // 2, :]
                else:
                    m = mk[:, 0, 0].rearrange("p (a c) -> p a c", a=1).broadcast_to([P, 4, P])
                    h0, w = 4 * (z - 8), P
                    ks = lambda h: kT[a][:, 0, h // 2, :]
                mm(out[:], identb[:], m, start=True, stop=False, skip_group_check=True)
                for k in range(512 // w):
                    ins = mm(out[:, w * k:w * (k + 1)], qz[a][:, h0 + k], ks(h0 + k), start=False, stop=(k == 512 // w - 1),
                             skip_group_check=True)
                ins.then_inc(s["scores"], 1)

            def turn_probs(z, n):
                pe.wait_ge(s["exps"], NZ * n + (z + 1))
                pe.wait_ge(s["probsT_out"], NZ * n + max(z - 1, 0))
                for c in range(4):
                    ins = tp(bank[2 + z % 2][:, c * P:(c + 1) * P], probs[:, z % 2, c * P:(c + 1) * P], K.ident[:])
                ins.then_inc(s["probs_turned"], 1)

            def values(z, n):
                a = UNIT[z]
                pe.wait_ge(s["probsT_out"], NZ * n + (z + 1))
                if z in FIRSTZ:
                    pe.wait_ge(s["unit_out"], 3 * n + a)
                if a < 2:
                    for k in range(2):
                        h = 2 * (z - FIRSTZ[a]) + k
                        for b in range(2):
                            ins = mm(bank[5][:, HD * h:HD * (h + 1)], probsT[:, z % 2, (2 * k + b) * P:(2 * k + b + 1) * P],
                                     v_in[a][:, b, HD * h:HD * (h + 1)], start=(b == 0), stop=(b == 1))
                else:
                    for k in range(4):
                        h = 4 * (z - 8) + k
                        ins = mm(bank[5][:, HD * h:HD * (h + 1)], probsT[:, z % 2, k * P:(k + 1) * P],
                                 v_in[a][:, 0, HD * h:HD * (h + 1)], start=True, stop=True)
                ins.then_inc(s["summed"], 1)

            def pair(h):
                return bank[6 + h // 2][:, VW * (h % 2):VW * (h % 2 + 1)]

            def step(i, j, more=True):
                n, p = 4 * i + j, j % 2
                scores(0, n, i, j)
                pe.wait_ge(ml_in[p], 80 * (2 * i + j // 2 + 1))
                pe.wait_ge(s["ml_C"], n)
                for h in range(MH):
                    ins = mm(bank[6][:, P * h:P * (h + 1)], mkk[:, p, h], mq[:, p, h], start=True, stop=True)
                ins.then_inc(s["ml_scores"], 1)
                for h in range(MH):
                    ins = tp(bank[7][:, P * h:P * (h + 1)], mkk[:, p, h], K.ident[:])
                ins.then_inc(s["ml_scores"], 1)
                scores(1, n, i, j); turn_probs(0, n); turn(1, 0, n)
                scores(2, n, i, j); turn_probs(1, n); values(0, n); turn(1, 1, n)
                scores(3, n, i, j); turn_probs(2, n); values(1, n)
                pe.wait_ge(s["ml_sc"], n + 1)
                pe.wait_ge(s["ml_kw"], n + 1)
                for h in range(MH):
                    ins = mm(pair(h), scT[:, h], vx[:, p, h], start=True, stop=True)
                ins.then_inc(s["ml_num"], 1)
                scores(4, n, i, j); turn_probs(3, n); values(2, n); turn(2, 0, n)
                scores(5, n, i, j); turn_probs(4, n); values(3, n); turn(2, 1, n)
                scores(6, n, i, j); turn_probs(5, n); values(4, n)
                pe.wait_ge(s["ml_num_out"], n + 1)
                for h in range(MH):
                    ins = mm(pair(h), mq[:, p, h], C[:, h], start=True, stop=True)
                ins.then_inc(s["ml_inter"], 1)
                scores(7, n, i, j); turn_probs(6, n); values(5, n)
                scores(8, n, i, j); turn_probs(7, n); values(6, n)
                scores(9, n, i, j); turn_probs(8, n); values(7, n)
                if more:
                    turn(0, 0, n + 1)
                turn_probs(9, n); values(8, n)
                pe.wait_ge(s["ml_num_done"], n + 1)
                for h in range(MH):
                    ins = mm(pair(h), kw[:, h], vx[:, p, h], start=True, stop=True)
                ins.then_inc(s["ml_dC"], 1)
                if more:
                    turn(0, 1, n + 1)
                values(9, n)

            turn(0, 0, 0)
            turn(0, 1, 0)
            gates.pe(pe)
            pe.wait_ge(gates.s["tab_ready"], 1)
            with pe.Fori(0, 3) as i:
                for j in range(STEPS):
                    step(i, j)
            for j in range(STEPS):
                step(3, j, j < 3)


KT = 13
KEYS = 12 * P + DEC_T
RT = H * DEC_T


def sample_tables():
    t = np.arange(DEC_T)[:, None]
    p = np.arange(P)
    pos = np.concatenate([16 * p + r for r in range(8)] + [WB - 512 + 4 * p + c for c in range(4)]
                         + [WB + np.arange(DEC_T)])[None, :]
    back = WB + t - pos
    part16 = np.zeros(KEYS, bool)
    part16[0:8 * P] = True
    new = np.zeros(KEYS, bool)
    new[12 * P:] = True
    d16 = (back >= 0) & (back % 16 == 0) & (back <= 2048) & (part16 | new)
    d4 = (back >= 0) & (back % 4 == 0) & (back <= 512) & ~part16
    d1 = (back >= 0) & (back <= 128) & ~part16
    count = d16.astype(np.float32) + d4 + d1
    assert (d1.sum(1) == 129).all() and (d4.sum(1) == 129).all() and (d16.sum(1) == 129).all()
    mask = np.where(count > 0, 0.0, NEG).astype(np.float32)
    return np.tile(mask, (H, 1)), np.tile(count.astype(np.float32), (H, 1))


def sample_chunk_tables():
    tok = np.arange(NS)
    b = tok // DEC_T
    ok = (b[:, None] == b[None, :]) & (tok[:, None] <= tok[None, :])
    return np.where(ok, 0.0, NEG).astype(np.float32), (b[:, None] == np.arange(DEC_B)[None, :]).astype(np.float32)


def mix_sample(K):
    nc, sem = K.nc, K.sem
    VW = MD + 1
    BH = DEC_B * MH
    S0 = SEQ
    with ExitStack() as ctx:
        def sb(name, shape, dt=F32):
            return ctx.enter_context(nc.sbuf_tensor("sm_" + name, shape, dt))

        kin = sb("kin", [P, 2, 12, AW])
        vin = sb("vin", [P, 2, 12, AW])
        knew = sb("knew", [DEC_T, 2, AW])
        vnew = sb("vnew", [DEC_T, 2, AW])
        kT = sb("kT", [P, H // 2, KEYS])
        mask = sb("mask", [RT, KEYS])
        count = sb("count", [RT, KEYS])
        pr = sb("pr", [RT, 2, KEYS])
        pT = sb("pT", [P, KT, RT])
        qs = kT[0:NS, 0, 0:AW]
        qT = sb("qT", [P, H // 2, NS])
        qbd = sb("qbd", [P, 2, H // 2, RT])
        osb = sb("osb", [RT, 2, AW])
        st = sb("st", [RT, 2, 4])
        states = sb("states", [P, BH * VW + MH * DEC_B * MD + MD])
        free = {"rest": [vin[:].rearrange("p a b c -> p (a b c)"), 0, 24 * AW],
                "states": [states[:], 0, BH * VW + MH * DEC_B * MD + MD]}

        def carve(which, parts, cols):
            flat, at, size = free[which]
            free[which][1] = at + cols
            assert at + cols <= size
            return flat[0:parts, at:at + cols]

        Cs = carve("states", P, BH * VW).rearrange("p (e c) -> p e c", c=VW)
        mq = carve("rest", P, MH * NS).rearrange("p (h t) -> p h t", h=MH)
        mkk = carve("rest", P, MH * NS).rearrange("p (h t) -> p h t", h=MH)
        vx = carve("rest", NS, MH * VW).rearrange("p (h c) -> p h c", h=MH)
        ngs = carve("rest", NS, MH * NS).rearrange("p (h t) -> p h t", h=MH)
        arg = carve("rest", NS, MH * NS).rearrange("p (h t) -> p h t", h=MH)
        wm = carve("rest", NS, MH * NS).rearrange("p (h t) -> p h t", h=MH)
        scT = carve("rest", NS, MH * NS).rearrange("p (h t) -> p h t", h=MH)
        qm = carve("rest", P, MH * 576).rearrange("p (h x) -> p h x", h=MH)
        kwm = carve("states", NS, MH * DEC_B * MD).rearrange("p (h b d) -> p h b d", h=MH, b=DEC_B)
        kw = carve("rest", NS, MW).rearrange("p (h d) -> p h d", h=MH)
        num = carve("rest", NS, MH * VW).rearrange("p (h c) -> p h c", h=MH)
        obs = carve("rest", NS, MW)
        mhg = carve("rest", NS, MW)
        hh = carve("rest", NS, MW).rearrange("p (h d) -> p h d", h=MH)
        sq = carve("rest", NS, MW).rearrange("p (h d) -> p h d", h=MH)
        hb = osb[:, 0].rearrange("p (h d) -> p h d", h=MH)
        n32 = carve("states", BH, MD)
        maskS = carve("rest", NS, NS)
        seq1 = carve("rest", NS, DEC_B)
        sm = carve("rest", NS, 10 * MH).rearrange("p (k h) -> p k h", h=MH)
        bank = [ctx.enter_context(nc.psum_tensor(f"sm_bank{i}", [P, 512], F32)) for i in range(8)]

        s = {n: sem("sm_" + n) for n in (
            "first_in", "arg_in", "ml_in", "C_in", "tab_in", "clear", "pe_ml", "act_ml", "own", "pool_own", "dC", "C_new", "hb_ready", "fin",
            "rows_out", "k_turned", "k_out_a", "k_out_d", "scores", "masked", "maxed", "exps", "counted",
            "p_turned", "pT_out", "summed", "o_ready", "q_ready", "ml_done")}
        k_in = [sem(f"sm_k_in{p}") for p in range(2)]
        v_in = [sem(f"sm_v_in{p}") for p in range(2)]
        o_out = [sem(f"sm_o_out{p}") for p in range(2)]
        block = ctx.enter_context(nc.Block(no_gpsimd_drain=True))
        NML = 4

        @block.sync
        def _(sp):
            def load(t, new, cache, kind, b, p, x):
                sp.dma_start(t[:, p, 0:8], cache[b].rearrange("(i r) c -> i r c", r=16)[:, 0:8]).then_inc(x[p], 16)
                sp.dma_start(t[:, p, 8:12], cache[b, WB - 512:WB, :].rearrange("(i r) c -> i r c", r=4)).then_inc(x[p], 16)
                sp.dma_start(new[:, p], K.proj[kind, bass.ds(DEC_T * b + S0, DEC_T), :]).then_inc(x[p], 16)

            def load_k(b, p):
                load(kin, knew, K.ins["cache_k"], KK, b, p, k_in)

            def load_v(b, p):
                load(vin, vnew, K.ins["cache_v"], VK, b, p, v_in)

            x = s["ml_in"]
            first = s["first_in"]
            sp.dma_start(mkk, K.qkt[MH:2 * MH, :, SEQ:NT].rearrange("h p t -> p h t")).then_inc(first, 16)
            sp.dma_start(mq, K.qkt[0:MH, :, SEQ:NT].rearrange("h p t -> p h t")).then_inc(first, 16)
            sp.dma_start(qs, K.proj[QK, S0:S0 + NS, :]).then_inc(first, 16)
            sp.dma_start(n32, K.ins["state_n"].rearrange("b h d -> (b h) d")).then_inc(first, 16)
            for h in range(MH):
                sp.dma_start(ngs[:, h].rearrange("p (b t) -> p b t", b=DEC_B),
                             K.ng_sample.rearrange("(b h) t -> h b t", h=MH)[h].partition_broadcast(NS)).then_inc(s["arg_in"], 16)
            sp.dma_start(maskS, K.ins["chunk_mask"]).then_inc(s["arg_in"], 16)
            sp.dma_start(vx[:, :, 0:MD], K.proj[VB, S0:S0 + NS, :].rearrange("p (h d) -> p h d", h=MH)).then_inc(x, 16)
            sp.dma_start(seq1, K.ins["token_seq"]).then_inc(x, 16)
            sp.dma_start(obs, K.proj[OB, S0:S0 + NS, :]).then_inc(x, 16)
            sp.dma_start(mhg, K.ins["mh_norm_g"].partition_broadcast(NS)).then_inc(x, 16)
            for h in range(MH):
                sp.dma_start(Cs.rearrange("p (b h) c -> p b h c", h=MH)[:, :, h, 0:MD],
                             K.ins["state_C"][:, h].rearrange("b d e -> d b e")).then_inc(s["C_in"], 16)
            sp.dma_start(mask[:], K.ins["sample_mask"]).then_inc(s["tab_in"], 16)
            sp.dma_start(count[:], K.ins["sample_count"]).then_inc(s["tab_in"], 16)
            for b in range(2):
                load_k(b, b)
            sp.wait_ge(s["C_new"], BH)
            for h in range(MH):
                sp.dma_start(K.o["C_sample"][0, :, h].rearrange("b d e -> d b e"),
                             Cs.rearrange("p (b h) c -> p b h c", h=MH)[:, :, h, 0:MD]).then_inc(s["fin"], 16)
            with nc.allow_non_contiguous_dma(reason="the normaliser column"):
                for h in range(MH):
                    sp.dma_start(K.o["n_sample"][0, :, h].rearrange("b (d a) -> d b a", a=1),
                                 Cs.rearrange("p (b h) c -> p b h c", h=MH)[:, :, h, MD:VW]).then_inc(s["fin"], 16)
            sp.wait_ge(s["hb_ready"], 1)
            sp.dma_start(K.mix[S0:S0 + NS, AW:D], osb[:, 0]).then_inc(s["fin"], 16)
            sp.wait_ge(s["fin"], 16 * (2 * MH + 1))
            sp.wait_ge(s["ml_done"], 1)

            for b in range(2):
                load_v(b, b)
            for kind, name in ((KK, "k"), (VK, "v")):
                sp.dma_start(K.o[f"win_{name}_sample"][0].rearrange("b s h d -> b s (h d)")[:, WB - DEC_T:WB, :],
                             K.proj[kind, S0:S0 + NS, :].rearrange("(b t) c -> b t c", b=DEC_B)).then_inc(s["rows_out"], 16)
            RB = SEQ // DEC_B

            def turn(b, p, more):
                sp.wait_ge(s["k_turned"], KT * (b + 1))
                if more:
                    load_k(b + 2, p)
                sp.wait_ge(s["summed"], b + 1)
                if more:
                    load_v(b + 2, p)
                for kind, name in ((KK, "k"), (VK, "v")):
                    sp.dma_start(K.o[f"win_{name}_prompt"].rearrange("a z s h d -> (a z s) (h d)")[bass.ds(RB * b, RB), :],
                                 K.proj[kind, bass.ds(RB * b, RB), :]).then_inc(s["rows_out"], 16)
                sp.wait_ge(s["o_ready"], b + 1)
                for h in range(H):
                    sp.dma_start(K.mix[bass.ds(DEC_T * b + S0, DEC_T), HD * h:HD * (h + 1)],
                                 osb[DEC_T * h:DEC_T * (h + 1), p, HD * h:HD * (h + 1)]).then_inc(o_out[p], 16)

            with sp.Fori(0, 3) as i:
                for j in range(2):
                    turn(2 * i + j, j, True)
            turn(6, 0, False)
            turn(7, 1, False)
            for p in range(2):
                sp.wait_ge(o_out[p], 16 * H * 4)
            sp.wait_ge(s["rows_out"], 16 * 2 * (DEC_B + 1))

        @block.gpsimd
        def _(pool):
            g = nc.gpsimd
            own = Chain(pool, s["pool_own"])
            g.memset(vx[:, :, MD:VW], 1.0).then_inc(s["clear"], 1)
            g.memset(qm, 0.0).then_inc(s["clear"], 1)
            g.memset(qbd[:], 0.0).then_inc(s["clear"], 1)
            pool.wait_ge(s["arg_in"], 16 * (MH + 1))
            own.mark(g.tensor_tensor(arg, ngs, maskS.rearrange("p (a t) -> p a t", a=1).broadcast_to([NS, MH, NS]), ALU.add))
            pool.wait_ge(s["ml_in"], 16 * NML)
            own.mark(g.tensor_tensor(obs, obs, mhg, ALU.mult))
            pool.wait_ge(s["first_in"], 64)
            pool.wait_ge(s["clear"], 3)
            for h in range(MH):
                own.mark(g.tensor_copy(qm[:, h].rearrange("p (b x) -> p b x", x=72)[:, :, 0:DEC_T],
                                       mq[:, h].rearrange("p (b t) -> p b t", b=DEC_B)))

            def put(b, p):
                for h in range(H):
                    e = h % 2
                    ins = g.tensor_copy(qbd[64 * e:64 * e + 64, p, h // 2, DEC_T * h:DEC_T * (h + 1)],
                                        qT[64 * e:64 * e + 64, h // 2, bass.ds(DEC_T * b, DEC_T)])
                ins.then_inc(s["q_ready"], 1)

            own.wait()
            pool.wait_ge(s["act_ml"], 1)
            put(0, 0)
            put(1, 1)
            with pool.Fori(1, 4) as i:
                for j in range(2):
                    pool.wait_ge(s["scores"], 4 * (2 * i + j - 1))
                    put(2 * i + j, j)

        def kcols(x):
            return slice(x * P, x * P + (P if x < 12 else DEC_T))

        @block.scalar
        def _(act):
            A = nc.scalar.activation
            nc.scalar.preload_act_table_set(LN_EXP)
            own = Chain(act, s["act_ml"])
            act.wait_ge(s["pe_ml"], 1)
            act.wait_ge(s["first_in"], 64)
            own.mark(A(qT[:], bank[0][:, 0:4 * NS].rearrange("p (h t) -> p h t", h=4), ACT.Copy, scale=HD ** -0.5))
            act.wait_ge(s["pool_own"], 1)
            for h in range(MH):
                ins = A(wm[:, h], arg[:, h], ACT.Exp, bias=K.tab_s[:, 0, h:h + 1])
            own.mark(ins)
            act.wait_ge(s["C_in"], 16 * MH)
            own.mark(A(Cs[:, :, MD:VW].rearrange("p e a -> p (e a)"), bank[1][:, 0:BH], ACT.Copy))
            act.wait_ge(s["pe_ml"], 3)
            for e in range(2):
                ins = A(num[:, 2 * e:2 * e + 2], bank[4 + e][0:NS, 0:2 * VW].rearrange("p (h c) -> p h c", h=2), ACT.Copy)
            own.link(ins)
            act.wait_ge(s["own"], K.sm_own_ms)
            own.link(A(sm[:, 3], sm[:, 2], ACT.Ln))
            own.link(A(sm[:, 4], sm[:, 3], ACT.Exp, scale=-0.5))

            def keys(b, p, xs):
                for x in xs:
                    act.wait_ge(s["k_turned"], KT * b + x + 1)
                    w = P if x < 12 else DEC_T
                    A(kT[:, :, kcols(x)], bank[0][:, 0:4 * w].rearrange("p (h c) -> p h c", h=4), ACT.Copy).then_inc(s["k_out_a"], 1)

            def exps(b, p):
                act.wait_ge(s["maxed"], b + 1)
                A(pr[:, p], pr[:, p], ACT.Exp, bias=st[:, p, 0:1]).then_inc(s["exps"], 1)

            def turned(b, p):
                act.wait_ge(s["p_turned"], 2 * b + 1)
                act.wait_ge(s["summed"], b)
                A(pT[:, 0:8], bank[4][:].rearrange("p (x r) -> p x r", x=8), ACT.Copy)
                act.wait_ge(s["p_turned"], 2 * b + 2)
                A(pT[:, 8:12], bank[5][:, 0:4 * RT].rearrange("p (x r) -> p x r", x=4), ACT.Copy)
                A(pT[0:DEC_T, 12], bank[5][0:DEC_T, 4 * RT:5 * RT], ACT.Copy).then_inc(s["pT_out"], 1)

            keys(0, 0, range(0, 13, 2))

            def step(b, j):
                keys(b + 1, 1 - j, (0, 2, 4))
                exps(b, j)
                keys(b + 1, 1 - j, (6, 8, 10, 12))
                turned(b, j)

            with act.Fori(0, 3) as i:
                for j in range(2):
                    step(2 * i + j, j)
            step(6, 0)
            exps(7, 1)
            turned(7, 1)

        @block.vector
        def _(dve):
            v = nc.vector
            chain = Chain(dve, s["own"])

            def bc(ap, w):
                return ap.rearrange("p (h a) -> p h a", a=1).broadcast_to([NS, MH, w])

            dve.wait_ge(s["pe_ml"], 2)
            chain.link(v.tensor_tensor(kw, bank[6][0:NS, :].rearrange("p (h d) -> p h d", h=MH), bc(K.tab_s[:, 3], MD), ALU.mult))
            dve.wait_ge(s["act_ml"], 2)
            chain.mark(v.tensor_tensor(scT, bank[7][0:NS, 0:MH * NS].rearrange("p (h t) -> p h t", h=MH), wm, ALU.mult))
            dve.wait_ge(s["ml_in"], 16 * NML)
            for h in range(MH):
                chain.mark(v.tensor_tensor(kwm[:, h], kw[:, h].rearrange("p (b d) -> p b d", b=1).broadcast_to([NS, DEC_B, MD]),
                                           seq1.rearrange("p (b d) -> p b d", d=1).broadcast_to([NS, DEC_B, MD]), ALU.mult))
            assert chain.n == K.sm_own_kwm
            dve.wait_ge(s["pe_ml"], 4)
            dve.wait_ge(s["act_ml"], 4)
            for h in range(MH):
                ins = v.scalar_tensor_tensor(num[:, h], bank[2 + h // 2][0:NS, VW * (h % 2):VW * (h % 2 + 1)],
                                             K.tab_s[:, 1, h:h + 1], num[:, h], ALU.mult, ALU.add)
            chain.link(ins)
            den = num[:, :, MD:VW].rearrange("p h a -> p (h a)")
            chain.link(v.tensor_scalar(sm[:, 5], den, -1.0, None, ALU.mult))
            chain.link(v.tensor_tensor(sm[:, 6], sm[:, 5], den, ALU.max))
            chain.link(v.tensor_tensor(sm[:, 0], sm[:, 6], K.tab_s[:, 2], ALU.max))
            chain.link(v.reciprocal(sm[:, 1], sm[:, 0]))
            chain.link(v.tensor_tensor(hh, num[:, :, 0:MD], bc(sm[:, 1], MD), ALU.mult))
            chain.link(v.tensor_tensor(sq, hh, hh, ALU.mult))
            chain.link(v.reduce_sum(sm[:, 7], sq, AX.X))
            chain.link(v.tensor_scalar(sm[:, 2], sm[:, 7], 1.0 / MD, EPS, ALU.mult, ALU.add))
            assert chain.n == K.sm_own_ms
            dve.wait_ge(s["act_ml"], 6)
            chain.link(v.tensor_tensor(sm[:, 5], sm[:, 4], sm[:, 4], ALU.mult))
            chain.link(v.tensor_tensor(sm[:, 6], sm[:, 5], sm[:, 2], ALU.mult))
            chain.link(v.tensor_scalar(sm[:, 7], sm[:, 6], -0.5, 1.5, ALU.mult, ALU.add))
            chain.link(v.tensor_tensor(sm[:, 8], sm[:, 7], sm[:, 4], ALU.mult))
            chain.link(v.tensor_tensor(hh, hh, bc(sm[:, 8], MD), ALU.mult))
            dve.wait_ge(s["pool_own"], 2)
            v.tensor_tensor(osb[:, 0], hh.rearrange("p h d -> p (h d)"), obs, ALU.mult).then_inc(s["hb_ready"], 1)
            for e in range(BH):
                dve.wait_ge(s["dC"], e + 1)
                v.scalar_tensor_tensor(Cs[:, e], Cs[:, e], K.wti[:, NCH * MH + e:NCH * MH + e + 1], bank[e % 4][:, 0:VW],
                                       ALU.mult, ALU.add).then_inc(s["C_new"], 1)
            dve.wait_ge(s["tab_in"], 32)

            def keys(b, xs):
                for x in xs:
                    dve.wait_ge(s["k_turned"], KT * b + x + 1)
                    v.tensor_copy(kT[:, :, kcols(x)], bank[1][:].rearrange("p (h c) -> p h c", h=4)).then_inc(s["k_out_d"], 1)

            def masked(b, p, cs, first=False):
                for c in cs:
                    w = 512 if c < 3 else DEC_T
                    dve.wait_ge(s["scores"], 4 * b + c + 1)
                    if c == 0 and not first:
                        dve.wait_ge(s["p_turned"], 2 * b - 2)
                    v.tensor_tensor(pr[:, p, 512 * c:512 * c + w], bank[2 + c % 2][0:RT, 0:w], mask[:, 512 * c:512 * c + w],
                                    ALU.add).then_inc(s["masked"], 1)

            def maxed(b, p):
                dve.wait_ge(s["masked"], 4 * b + 4)
                v.reduce_max(st[:, p, 0:1], pr[:, p], AX.X, negate=True).then_inc(s["maxed"], 1)

            def counted(b, p):
                dve.wait_ge(s["exps"], b + 1)
                v.scalar_tensor_tensor(pr[:, p], pr[:, p], 1.0, count[:], ALU.mult, ALU.mult,
                                       accum_out=st[:, p, 1:2]).then_inc(s["counted"], 1)
                dve.wait_ge(s["counted"], b + 1)
                v.reciprocal(st[:, p, 2:3], st[:, p, 1:2]).then_inc(s["own"], 1)
                chain.n += 1

            def out(b, p, used):
                dve.wait_ge(s["summed"], b + 1)
                if used is not None:
                    dve.wait_ge(o_out[p], 16 * H * used)
                chain.wait()
                v.tensor_scalar(osb[:, p], bank[6][0:RT, :], st[:, p, 2:3], None, ALU.mult).then_inc(s["o_ready"], 1)

            keys(0, (1, 3, 5, 7))
            masked(0, 0, (0,), True)
            keys(0, (9, 11))
            masked(0, 0, (1, 2, 3))
            maxed(0, 0)

            def step(b, j, used, first=False):
                keys(b + 1, (1, 3, 5))
                counted(b, j)
                keys(b + 1, (7,))
                masked(b + 1, 1 - j, (0,), first)
                keys(b + 1, (9, 11))
                masked(b + 1, 1 - j, (1, 2, 3))
                maxed(b + 1, 1 - j)
                out(b, j, used)

            step(0, 0, None, True)
            step(1, 1, None)
            with chain.loop(2, 2) as i:
                for j in range(2):
                    step(2 * i + j + 2, j, i + 1)
            step(6, 0, 3)
            counted(7, 1)
            out(7, 1, 3)

        @block.tensor
        def _(pe):
            mm, tp = nc.tensor.matmul, nc.tensor.transpose
            ident = K.ident
            pe.wait_ge(s["first_in"], 64)
            for c in range(4):
                tp(bank[0][:, NS * c:NS * (c + 1)], qs[:, c * P:(c + 1) * P], ident[0:NS, 0:NS])
            tp(bank[1][:, 0:BH], n32, ident[0:BH, 0:BH]).then_inc(s["pe_ml"], 1)
            for h in range(MH):
                mm(bank[7][0:NS, NS * h:NS * (h + 1)], mkk[:, h], mq[:, h], start=True, stop=True)
            for h in range(MH):
                ins = tp(bank[6][0:NS, P * h:P * (h + 1)], mkk[:, h], ident[:])
            ins.then_inc(s["pe_ml"], 1)
            pe.wait_ge(s["clear"], 3)
            pe.wait_ge(s["ml_in"], 16 * NML)
            pe.wait_ge(s["own"], 2)
            for h in range(MH):
                ins = mm(bank[4 + h // 2][0:NS, VW * (h % 2):VW * (h % 2 + 1)], scT[:, h], vx[:, h], start=True, stop=True)
            ins.then_inc(s["pe_ml"], 1)
            pe.wait_ge(s["act_ml"], 3)
            pe.wait_ge(s["pool_own"], 6)
            for h in range(MH):
                for b in range(DEC_B):
                    ins = mm(bank[2 + h // 2][0:NS, VW * (h % 2):VW * (h % 2 + 1)], qm[:, h, NS * b:NS * (b + 1)],
                             Cs[:, MH * b + h], start=(b == 0), stop=(b == DEC_B - 1))
            ins.then_inc(s["pe_ml"], 1)
            pe.wait_ge(s["own"], K.sm_own_kwm + 1)
            for e in range(BH):
                if e >= 4:
                    pe.wait_ge(s["C_new"], e - 3)
                ins = mm(bank[e % 4][:, 0:VW], kwm[:, e % MH, e // MH], vx[:, e % MH], start=True, stop=True)
                ins.then_inc(s["dC"], 1)
            pe.wait_ge(s["C_new"], BH)
            nc.tensor.transpose(bank[7][0:1, 0:P], ident[:, 0:1], ident[:]).then_inc(s["ml_done"], 1)

            def turn(b, p, xs):
                for x in xs:
                    if x % 2 == 0:
                        pe.wait_ge(s["k_out_a"], 7 * b + x // 2)
                    else:
                        pe.wait_ge(s["k_out_d"], 6 * b + x // 2)
                    src = kin[:, p, x] if x < 12 else knew[:, p]
                    w = P if x < 12 else DEC_T
                    for c in range(4):
                        dst, rows = bank[x % 2][:, w * c:w * (c + 1)], src[:, c * P:(c + 1) * P]
                        if x < 12:
                            ins = tp(dst, rows, ident[:])
                        else:
                            ins = mm(dst, rows, ident[0:w, 0:w], start=True, stop=True)
                    ins.then_inc(s["k_turned"], 1)

            def scores(b, p, c):
                w = 512 if c < 3 else DEC_T
                pe.wait_ge(s["k_out_a"], 7 * b + (2 * c + 2 if c < 3 else 7))
                pe.wait_ge(s["k_out_d"], 6 * b + (2 * c + 2 if c < 3 else 6))
                if c < 2:
                    pe.wait_ge(s["masked"], 4 * b)
                else:
                    pe.wait_ge(s["masked"], 4 * b + c - 1)
                for h in range(4):
                    ins = mm(bank[2 + c % 2][0:RT, 0:w], qbd[:, p, h], kT[:, h, 512 * c:512 * c + w], start=(h == 0), stop=(h == 3))
                ins.then_inc(s["scores"], 1)

            def first_half(b, p, use):
                pe.wait_ge(k_in[p], 48 * (use + 1))
                pe.wait_ge(s["q_ready"], b + 1)
                turn(b, p, range(0, 8))
                scores(b, p, 0)
                turn(b, p, range(8, 12))
                scores(b, p, 1)
                turn(b, p, (12,))
                scores(b, p, 2)
                scores(b, p, 3)

            def second_half(b, p, use):
                pe.wait_ge(s["counted"], b + 1)
                pe.wait_ge(s["pT_out"], b)
                for x in range(KT):
                    w = P if x < 12 else DEC_T
                    dst = bank[4 + x // 8][0:w, RT * (x % 8):RT * (x % 8 + 1)]
                    if x:
                        ins = tp(dst, pr[:, p, kcols(x)], ident[0:RT, 0:RT])
                    else:
                        mm(dst, pr[:, p, kcols(x)], ident[0:RT, 0:RT], start=True, stop=True)
                    if x in (7, 12):
                        ins.then_inc(s["p_turned"], 1)
                pe.wait_ge(v_in[p], 48 * (use + 1))
                pe.wait_ge(s["pT_out"], b + 1)
                pe.wait_ge(s["o_ready"], b)
                for x in range(KT):
                    w = P if x < 12 else DEC_T
                    ins = mm(bank[6][0:RT, :], pT[0:w, x], vin[:, p, x] if x < 12 else vnew[:, p], start=(x == 0), stop=(x == KT - 1))
                ins.then_inc(s["summed"], 1)

            first_half(0, 0, 0)
            with pe.Fori(0, 3) as i:
                for j in range(2):
                    first_half(2 * i + j + 1, 1 - j, i + j)
                    second_half(2 * i + j, j, i)
            first_half(7, 1, 3)
            second_half(6, 0, 3)
            second_half(7, 1, 3)


def project_out(K):
    nc, sem = K.nc, K.sem
    HW = HD + 2
    NP = SEQ // P
    with ExitStack() as ctx:
        def sb(name, shape, dt=F32):
            return ctx.enter_context(nc.sbuf_tensor("out_" + name, shape, dt))

        w_raw = sb("w_raw", [P, 2, 2, D])
        w_hi = sb("w_hi", [P, KC, D], F32R)
        w_lo = sb("w_lo", [P, KC, D], F32R)
        xt = sb("xt", [P, 2, D])
        mt = sb("mt", [P, 2, D])
        pt = sb("pt", [P, 2, 3, H, HW])
        prod = sb("prod", [P, 3, H, HD])
        mT_hi = sb("mT_hi", [P, 2, KC, P], F32R)
        mT_lo = sb("mT_lo", [P, 2, KC, P], F32R)
        st = sb("st", [P, 2, 8, 3, H])
        bank = [ctx.enter_context(nc.psum_tensor(f"out_bank{i}", [P, 512], F32)) for i in range(8)]
        w_in = [sem(f"out_w_in{q}") for q in range(2)]
        w_hi_ready, w_lo_ready = sem("out_w_hi"), sem("out_w_lo")
        tile_in = [sem(f"out_tile_in{q}") for q in range(2)]
        x_in = [sem(f"out_x_in{q}") for q in range(2)]
        x2_out = [sem(f"out_x2_out{q}") for q in range(2)]
        shifted, exps, mixed, turned, hi_ready, lo_ready, prod_mm, added, own = (
            sem("out_" + n) for n in ("shifted", "exps", "mixed", "turned", "hi", "lo", "prod_mm", "added", "own"))
        block = ctx.enter_context(nc.Block(no_gpsimd_drain=True))
        IN = 16 * 2
        last_in = IN * (NP // 2) + 16

        xv = K.x.rearrange("(t p) d -> t p d", p=P)

        @block.sync
        def _(sp):
            def load(t, p):
                rows = bass.ds(t * P, P)
                sp.dma_start(pt[:, p], K.parts[:, rows, :].rearrange("a p (h c) -> p a h c", h=H)).then_inc(tile_in[p], 16)
                sp.dma_start(mt[:, p, AW:D], K.mix[rows, AW:D]).then_inc(tile_in[p], 16)

            def load_x(t, p):
                sp.dma_start(xt[:, p], xv[t]).then_inc(x_in[p], 16)

            def load_w(q):
                sp.dma_start(w_raw[:, q % 2], K.ins["w_out"][:, 2 * q:2 * q + 2, :]).then_inc(w_in[q % 2], 16)

            load(0, 0)
            load_w(0)
            load_w(1)
            load(1, 1)
            load_x(0, 0)
            load_x(1, 1)
            for q in (2, 3):
                sp.wait_ge(w_lo_ready, q - 1)
                load_w(q)
            for t in range(2):
                sp.wait_ge(turned, t + 1)
                load(t + 2, t)
            sp.wait_ge(x2_out[0], 16)
            load_x(2, 0)
            with sp.Fori(1, NP // 2 - 1) as i:
                for j in range(2):
                    sp.wait_ge(turned, 2 * i + j + 1)
                    load(2 * i + j + 2, j)
                    sp.wait_ge(x2_out[1 - j], 16 * i + 16 * j)
                    load_x(2 * i + j + 1, 1 - j)
            sp.wait_ge(turned, NP - 1)
            sp.dma_start(mt[0:NS, 0], K.mix[SEQ:NT, :]).then_inc(tile_in[0], 16)
            sp.wait_ge(x2_out[1], 16 * (NP // 2 - 1))
            load_x(NP - 1, 1)
            sp.wait_ge(x2_out[0], 16 * (NP // 2))
            load_x(NP, 0)

        @block.gpsimd
        def _(pool):
            for q in range(4):
                pool.wait_ge(w_hi_ready, q + 1)
                nc.gpsimd.tensor_tensor(w_lo[:, 2 * q:2 * q + 2], w_raw[:, q % 2], w_hi[:, 2 * q:2 * q + 2].bitcast(F32),
                                        ALU.subtract).then_inc(w_lo_ready, 1)

        @block.scalar
        def _(act):
            A = nc.scalar.activation
            nc.scalar.preload_act_table_set(LN_EXP)

            def exp(t, p):
                act.wait_ge(shifted, t + 1)
                A(st[:, p, 1], st[:, p, 1], ACT.Exp).then_inc(exps, 1)

            def hi(t, p, w=P, used=True):
                act.wait_ge(turned, t + 1)
                if used:
                    act.wait_ge(prod_mm, 2 * t - 2)
                for e in range(2):
                    ins = A(mT_hi[:, p, 4 * e:4 * e + 4, 0:w],
                            bank[2 * p + e][:].rearrange("p (k c) -> p k c", k=4)[:, :, 0:w], ACT.Copy)
                ins.then_inc(hi_ready, 1)

            def store(t, p):
                act.wait_ge(added, 2 * t + 2)
                act.dma_start(K.x2[bass.ds(t * P, P), :], xt[:, p]).then_inc(x2_out[p], 16)


            def w_round(q):
                act.wait_ge(w_in[q % 2], 16 * (q // 2 + 1))
                A(w_hi[:, 2 * q:2 * q + 2], w_raw[:, q % 2], ACT.Copy).then_inc(w_hi_ready, 1)

            w_round(0)
            exp(0, 0)
            w_round(1)
            hi(0, 0, used=False)
            exp(1, 1)
            w_round(2)
            w_round(3)
            hi(1, 1, used=False)
            exp(2, 0)
            store(0, 0)
            hi(2, 0)
            exp(3, 1)
            store(1, 1)
            with act.Fori(1, NP // 2 - 1) as i:
                for j in range(2):
                    hi(2 * i + j + 1, 1 - j)
                    exp(2 * i + j + 2, j)
                    store(2 * i + j, j)
            hi(NP - 1, 1)
            store(NP - 2, 0)
            hi(NP, 0, NS)
            store(NP - 1, 1)
            store(NP, 0)
            for p in range(2):
                act.wait_ge(x2_out[p], 16 * (NP // 2 + 1 - p))

        @block.vector
        def _(dve):
            v = nc.vector
            chain = Chain(dve, own)

            def wide(a):
                return a.rearrange("p h (d a) -> p h d a", a=1)

            def combine(t, i, p):
                q = pt[:, p]
                neg, den = q[:, :, :, HD], q[:, :, :, HD + 1]
                S = st[:, p]
                dve.wait_ge(tile_in[p], IN * i + IN)
                chain.link(v.tensor_tensor(S[:, 0, 0], neg[:, 0], neg[:, 1], ALU.min))
                chain.link(v.tensor_tensor(S[:, 0, 1], S[:, 0, 0], neg[:, 2], ALU.min))
                v.tensor_tensor(S[:, 1], S[:, 0, 1:2].broadcast_to([P, 3, H]), neg, ALU.subtract).then_inc(shifted, 1)
                dve.wait_ge(exps, t + 1)
                chain.link(v.tensor_tensor(S[:, 3], S[:, 1], den, ALU.mult))
                chain.link(v.tensor_tensor(S[:, 4, 0], S[:, 3, 0], S[:, 3, 1], ALU.add))
                chain.link(v.tensor_tensor(S[:, 4, 1], S[:, 4, 0], S[:, 3, 2], ALU.add))
                chain.link(v.reciprocal(S[:, 4, 2], S[:, 4, 1]))
                chain.link(v.tensor_tensor(S[:, 2], S[:, 1], S[:, 4, 2:3].broadcast_to([P, 3, H]), ALU.mult))
                for a in range(3):
                    ins = v.tensor_tensor(prod[:, a], q[:, a, :, 0:HD],
                                          S[:, 2, a].rearrange("p (h d) -> p h d", d=1).broadcast_to([P, H, HD]), ALU.mult)
                chain.link(ins)
                chain.link(v.tensor_tensor(prod[:, 0], prod[:, 0], prod[:, 1], ALU.add))
                v.tensor_tensor(mt[:, p, 0:AW].rearrange("p (h d) -> p h d", h=H), prod[:, 0], prod[:, 2],
                                ALU.add).then_inc(mixed, 1)
                dve.wait_ge(mixed, t + 1)

            def lo(t, p, w=P):
                dve.wait_ge(hi_ready, t + 1)
                for e in range(2):
                    ins = v.tensor_tensor(mT_lo[:, p, 4 * e:4 * e + 4, 0:w],
                                          bank[2 * p + e][:].rearrange("p (k c) -> p k c", k=4)[:, :, 0:w],
                                          mT_hi[:, p, 4 * e:4 * e + 4, 0:w].bitcast(F32), ALU.subtract)
                ins.then_inc(lo_ready, 1)

            def add(t, i, p, rows=P):
                dve.wait_ge(x_in[p], 16 * i + 16)
                for e in range(2):
                    dve.wait_ge(prod_mm, 2 * t + e + 1)
                    v.tensor_tensor(xt[0:rows, p, 512 * e:512 * e + 512], xt[0:rows, p, 512 * e:512 * e + 512],
                                    bank[4 + 2 * p + e][0:rows, :], ALU.add).then_inc(added, 1)

            combine(0, 0, 0)
            combine(1, 0, 1)
            lo(0, 0)
            with chain.loop(NP // 2 - 1, 18) as i:
                for j in range(2):
                    lo(2 * i + j + 1, 1 - j)
                    combine(2 * i + j + 2, i + 1, j)
                    add(2 * i + j, i, j)
            lo(NP - 1, 1)
            add(NP - 2, NP // 2 - 1, 0)
            lo(NP, 0, NS)
            add(NP - 1, NP // 2 - 1, 1)
            add(NP, NP // 2, 0, NS)

        @block.tensor
        def _(pe):
            def turn(t, p, used=True):
                pe.wait_ge(mixed, t + 1)
                if used:
                    pe.wait_ge(lo_ready, t - 1)
                for k in range(KC):
                    ins = nc.tensor.transpose(bank[2 * p + k // 4][:, (k % 4) * P:(k % 4 + 1) * P],
                                              mt[:, p, k * P:(k + 1) * P], K.ident[:])
                ins.then_inc(turned, 1)

            def products(t, p, w=P, used=True, before=None):
                pe.wait_ge(lo_ready, t + 1)
                for e in range(2):
                    if used:
                        pe.wait_ge(added, 2 * t + e - 3)
                    split_products(nc, bank[4 + 2 * p + e][0:w, :],
                                   [(mT_hi[:, p, k, 0:w], mT_lo[:, p, k, 0:w], w_hi[:, k, 512 * e:512 * e + 512],
                                     w_lo[:, k, 512 * e:512 * e + 512]) for k in range(KC)], prod_mm, before)

            pe.wait_ge(K.ident_ready, K.ident_value)
            turn(0, 0, False)
            turn(1, 1, False)
            products(0, 0, used=False, before=lambda k: pe.wait_ge(w_lo_ready, k // 2 + 1))
            turn(2, 0)
            products(1, 1, used=False)
            with pe.Fori(1, NP // 2 - 1) as i:
                for j in range(2):
                    turn(2 * i + j + 1, 1 - j)
                    products(2 * i + j, j)
            turn(NP - 1, 1)
            products(NP - 2, 0)
            pe.wait_ge(lo_ready, NP - 1)
            pe.wait_ge(tile_in[0], last_in)
            for k in range(KC):
                ins = nc.tensor.transpose(bank[k // 4][:, (k % 4) * P:(k % 4) * P + NS],
                                          mt[0:NS, 0, k * P:(k + 1) * P], K.ident[0:NS, 0:NS])
            ins.then_inc(turned, 1)
            products(NP - 1, 1)
            products(NP, 0, NS)


def mlp(K):
    nc, sem = K.nc, K.sem
    GT0, GN = (0, 6, 12), (6, 6, 5)
    PIECE = (3 * P, 3 * P, 2 * P + NS // 2)
    FB = DFF // 256
    G = len(GN)
    with ExitStack() as ctx:
        def sb(name, shape, dt=F32):
            return ctx.enter_context(nc.sbuf_tensor("mlp_" + name, shape, dt))

        hT_hi = sb("hT_hi", [P, KC, 6 * P], F32R)
        hT_lo = sb("hT_lo", [P, KC, 6 * P], F32R)
        xb = sb("xb", [P, 2, D])
        xn = sb("xn", [P, 2, D])
        small = sb("small", [P, 2, 8])
        gain2 = sb("gain2", [P, D])
        gain_f = sb("gain_f", [P, D])
        wu_raw = sb("wu_raw", [P, KC, 256])
        wd_raw = sb("wd_raw", [P, 2, D])
        wu_hi = [sb(f"wu_hi{s}", [P, KC, 256], F32R) for s in range(2)]
        wu_lo = [sb(f"wu_lo{s}", [P, KC, 256], F32R) for s in range(2)]
        wd_hi = [sb(f"wd_hi{s}", [P, 2, D], F32R) for s in range(2)]
        wd_lo = [sb(f"wd_lo{s}", [P, 2, D], F32R) for s in range(2)]
        u2 = xn[:].rearrange("p s d -> p (s d)")[:, 0:2 * 6 * P].rearrange("p (m c) -> p m c", m=2)
        u_hi = [sb(f"u_hi{s}", [P, 2, 6 * P], F32R) for s in range(2)]
        u_lo = [sb(f"u_lo{s}", [P, 2, 6 * P], F32R) for s in range(2)]
        acc = sb("acc", [P, 6, D])
        fin = sb("fin", [P, 8, 6])
        bank = [ctx.enter_context(nc.psum_tensor(f"mlp_bank{i}", [P, 512], F32)) for i in range(8)]

        const_in, acc_in, y_out, copied = sem("mlp_const_in"), sem("mlp_acc_in"), sem("mlp_y_out"), sem("mlp_copied")
        wu_in, wu_hi_ready, wu_lo_ready = sem("mlp_wu_in"), sem("mlp_wu_hi"), sem("mlp_wu_lo")
        wd_in, wd_hi_ready, wd_lo_ready = sem("mlp_wd_in"), sem("mlp_wd_hi"), sem("mlp_wd_lo")
        up_mm, u2_ready, u_hi_ready, u_lo_ready = sem("mlp_up_mm"), sem("mlp_u2"), sem("mlp_u_hi"), sem("mlp_u_lo")
        relu_done, gain_f_in = sem("mlp_relu"), sem("mlp_gain_f_in")
        down_mm, summed, own = sem("mlp_down_mm"), sem("mlp_summed"), sem("mlp_own")
        f_ssq, f_var, f_root, y_ready = sem("mlp_f_ssq"), sem("mlp_f_var"), sem("mlp_f_root"), sem("mlp_y_ready")
        DB = tuple(FB * GT0[g] for g in range(G))
        xv = K.x2.rearrange("(t p) d -> t p d", p=P)

        norm = Norm(nc, sem, "mlp", lambda T: xv[T], xb, xn, small, gain2, hT_hi, hT_lo,
                    bank[0:4], K.ident)
        block = ctx.enter_context(nc.Block(no_gpsimd_drain=True))
        @block.sync
        def _(sp):
            CB = (WB - DEC_T) // 6

            def load_up(E, f):
                sp.dma_start(wu_raw[:], K.ins["w_up"][f]).then_inc(wu_in, 16)

            def load_down(E, f):
                sp.dma_start(wd_raw[:], K.ins["w_down"][f]).then_inc(wd_in, 16)

            def opening():
                sp.dma_start(gain2[:], K.ins["norm2_g"].partition_broadcast(P)).then_inc(const_in, 16)
                load_up(0, 0)

            for g in range(G):
                if g == 0:
                    norm.sync_group(sp, GN[0], opening)
                    sp.dma_start(gain_f[:], K.ins["norm_f_g"].partition_broadcast(P)).then_inc(gain_f_in, 16)
                else:
                    for T in range(GT0[g] + 2, GT0[g] + GN[g]):
                        norm.load(sp, T, T % 2, False)
                    sp.wait_ge(y_out, 16 * GT0[g])
                sp.dma_start(acc[:, 0:GN[g]], K.x2[GT0[g] * P:(GT0[g] + GN[g]) * P, :].rearrange("(t p) d -> p t d", p=P))\
                    .then_inc(acc_in, 16)
                if g == 0:
                    load_down(0, 0)
                    sp.wait_ge(wu_lo_ready, 1)
                    load_up(1, 1)
                    sp.wait_ge(wu_lo_ready, 2)
                    load_up(2, 2)
                    sp.wait_ge(wd_lo_ready, 1)
                    load_down(1, 1)

                def copy(i, j):
                    for name in ("k", "v"):
                        sp.dma_start(K.o[f"win_{name}_sample"][0].rearrange("b s h d -> b s (h d)")[i, CB * (2 * g + j):CB * (2 * g + j + 1), :],
                                     K.ins["cache_" + name][i, DEC_T + CB * (2 * g + j):DEC_T + CB * (2 * g + j + 1), :])\
                            .then_inc(copied, 16)

                def step(i, j, up=None, down=None):
                    f = 2 * i + j
                    copy(i, j)
                    if up is not None:
                        sp.wait_ge(wu_lo_ready, f + (FB * g + 3))
                        load_up(0, up)
                    if down is not None:
                        sp.wait_ge(wd_lo_ready, f + (FB * g + 2))
                        load_down(0, down)

                if g < G - 1:
                    for T in (GT0[g + 1], GT0[g + 1] + 1):
                        norm.load(sp, T, T % 2, False)
                with sp.Fori(0, 6) as i:
                    for j in range(2):
                        step(i, j, 2 * i + j + 3, 2 * i + j + 2)
                for f in range(12, FB):
                    more = g < G - 1
                    step(f // 2, f % 2, (f + 3) % FB if more or f + 3 < FB else None,
                         (f + 2) % FB if more or f + 2 < FB else None)
            sp.wait_ge(copied, 16 * 2 * G * FB)

        @block.gpsimd
        def _(pool):
            g_ = nc.gpsimd

            def split_up(E, s):
                pool.wait_ge(wu_hi_ready, E + 1)
                g_.tensor_tensor(wu_lo[s][:], wu_raw[:], wu_hi[s][:].bitcast(F32), ALU.subtract).then_inc(wu_lo_ready, 1)

            def split_down(E, s):
                pool.wait_ge(wd_hi_ready, E + 1)
                g_.tensor_tensor(wd_lo[s][:], wd_raw[:], wd_hi[s][:].bitcast(F32), ALU.subtract).then_inc(wd_lo_ready, 1)

            def split_u(g, E, s):
                w = PIECE[g]
                for k in range(4):
                    m, q = k // 2, k % 2
                    pool.wait_ge(u_hi_ready, 4 * E + k + 1)
                    cols = slice(w * q, w * q + w)
                    g_.tensor_tensor(u_lo[s][:, m, cols], u2[:, m, cols], u_hi[s][:, m, cols].bitcast(F32),
                                     ALU.subtract).then_inc(u_lo_ready, 1)

            split_up(0, 0)
            split_down(0, 0)
            split_up(1, 1)
            for g in range(G):
                split_u(g, FB * g, 0)

                def step(f, j, up=True, down=True, u=True):
                    E = f + FB * g
                    if up:
                        split_up(E + 2, j)
                    if down:
                        split_down(E + 1, 1 - j)
                    if u:
                        split_u(g, E + 1, 1 - j)

                with pool.Fori(0, 7) as i:
                    for j in range(2):
                        step(2 * i + j, j)
                more = g < G - 1
                step(14, 0, up=more)
                step(15, 1, up=more, down=more, u=False)

        @block.scalar
        def _(act):
            A = nc.scalar.activation
            nc.scalar.preload_act_table_set(LN_EXP)

            def round_up(E, s, used=True):
                act.wait_ge(wu_in, 16 * E + 16)
                if used:
                    act.wait_ge(up_mm, 4 * E - 4)
                A(wu_hi[s][:], wu_raw[:], ACT.Copy).then_inc(wu_hi_ready, 1)

            def round_down(E, s, used=None):
                act.wait_ge(wd_in, 16 * E + 16)
                if used is not None:
                    act.wait_ge(down_mm, used)
                A(wd_hi[s][:], wd_raw[:], ACT.Copy).then_inc(wd_hi_ready, 1)

            def round_u(g, E, s, used=None):
                w = PIECE[g]
                if used is not None:
                    act.wait_ge(down_mm, used)

                def relu(k):
                    m, q = k // 2, k % 2
                    act.wait_ge(up_mm, 4 * E + k + 1)
                    if not (isinstance(E, int) and E == 0):
                        act.wait_ge(u_lo_ready, 4 * E + (k - 3))
                    A(u2[:, m, w * q:w * q + w], bank[k][:, 0:w], ACT.Relu).then_inc(relu_done, 1)

                relu(0)
                for k in range(4):
                    if k < 3:
                        relu(k + 1)
                    m, q = k // 2, k % 2
                    act.wait_ge(u2_ready, 4 * E + k + 1)
                    cols = slice(w * q, w * q + w)
                    A(u_hi[s][:, m, cols], u2[:, m, cols], ACT.Copy).then_inc(u_hi_ready, 1)

            def final(g):
                n = GN[g]
                for t in range(n):
                    act.wait_ge(summed, DB[g] + (FB - 1) * n + t + 1)
                    if t >= 2:
                        act.wait_ge(f_ssq, GT0[g] + t - 1)
                    A(xn[:, t % 2], acc[:, t], ACT.Square, accum_out=fin[:, 0, t:t + 1]).then_inc(f_ssq, 1)
                act.wait_ge(f_var, g + 1)
                A(fin[:, 2, 0:n], fin[:, 1, 0:n], ACT.Ln).then_inc(f_root, 1)
                act.wait_ge(f_root, 2 * g + 1)
                A(fin[:, 3, 0:n], fin[:, 2, 0:n], ACT.Exp, scale=-0.5).then_inc(f_root, 1)
                for t in range(n):
                    T = GT0[g] + t
                    act.wait_ge(y_ready, T + 1)
                    dst = K.o["y_prompt"][0, T * P:(T + 1) * P, :] if T < TILES - 1 else K.o["y_sample"].rearrange("b t d -> (b t) d")
                    act.dma_start(dst, acc[0:(P if T < TILES - 1 else NS), t]).then_inc(y_out, 16)

            for g in range(G):
                if g == 0:
                    norm.act_group(act, GN[0], lambda: round_up(0, 0, False))
                    round_down(0, 0)
                    round_up(1, 1, False)
                else:
                    final(g - 1)
                    act.wait_ge(f_ssq, GT0[g])
                round_u(g, FB * g, 0)

                def step(f, j, up=True, down=True, u=True):
                    E = f + FB * g
                    past = GN[g] * f + DB[g]
                    if up:
                        round_up(E + 2, j)
                    if down:
                        round_down(E + 1, 1 - j, past)
                    if u:
                        round_u(g, E + 1, 1 - j, past)

                with act.Fori(0, 7) as i:
                    for j in range(2):
                        step(2 * i + j, j)
                more = g < G - 1
                step(14, 0, up=more)
                step(15, 1, up=more, down=more, u=False)
                if more:
                    T0, n = GT0[g + 1], GN[g + 1]
                    act.wait_ge(u_lo_ready, 4 * FB * (g + 1))
                    norm.act_stats(act, T0, T0 % 2, T0 // 2, False)
                    for T in range(T0, T0 + n):
                        if T + 1 < T0 + n:
                            norm.act_stats(act, T + 1, (T + 1) % 2, (T + 1) // 2, False)
                        norm.act_hi(act, T, T % 2, (T - T0) * P)
            act.wait_ge(u_lo_ready, 4 * FB * G)
            final(G - 1)
            act.wait_ge(y_out, 16 * TILES)

        @block.vector
        def _(dve):
            v = nc.vector
            chain = Chain(dve, own)
            dve.wait_ge(const_in, 16)

            def square(g, E):
                w = PIECE[g]
                for k in range(4):
                    m, q = k // 2, k % 2
                    dve.wait_ge(relu_done, 4 * E + k + 1)
                    v.tensor_tensor(u2[:, m, w * q:w * q + w], u2[:, m, w * q:w * q + w], u2[:, m, w * q:w * q + w],
                                    ALU.mult).then_inc(u2_ready, 1)

            def add(g, f, tiles=None):
                n = GN[g]
                for t in tiles or range(n):
                    rows = P if GT0[g] + t < TILES - 1 else NS
                    done = n * f + (DB[g] + t)
                    dve.wait_ge(down_mm, done + 1)
                    if not (isinstance(f, int) and f == 0):
                        dve.wait_ge(summed, n * f + DB[g])
                    for e in range(2):
                        ins = v.tensor_tensor(acc[0:rows, t, 512 * e:512 * e + 512], acc[0:rows, t, 512 * e:512 * e + 512],
                                              bank[4 + 2 * (t % 2) + e][0:rows, :], ALU.add)
                    ins.then_inc(summed, 1)

            def final(g):
                n = GN[g]
                q = fin[:, :, 0:n]
                dve.wait_ge(gain_f_in, 16)
                dve.wait_ge(f_ssq, GT0[g] + n)
                v.tensor_scalar(q[:, 1], q[:, 0], 1.0 / D, EPS, ALU.mult, ALU.add).then_inc(f_var, 1)
                dve.wait_ge(f_root, 2 * g + 2)
                chain.link(v.tensor_tensor(q[:, 4], q[:, 3], q[:, 3], ALU.mult))
                chain.link(v.tensor_tensor(q[:, 5], q[:, 4], q[:, 1], ALU.mult))
                chain.link(v.tensor_scalar(q[:, 6], q[:, 5], -0.5, 1.5, ALU.mult, ALU.add))
                chain.link(v.tensor_tensor(q[:, 7], q[:, 6], q[:, 3], ALU.mult))
                for t in range(n):
                    v.scalar_tensor_tensor(acc[:, t], acc[:, t], q[:, 7, t:t + 1], gain_f[:], ALU.mult, ALU.mult).then_inc(y_ready, 1)

            for g in range(G):
                if g == 0:
                    norm.dve_group(dve, chain, GN[0])
                if g:
                    final(g - 1)
                square(g, FB * g)
                dve.wait_ge(acc_in, 16 * g + 16)
                square(g, FB * g + 1)
                add(g, 0)
                square(g, FB * g + 2)
                add(g, 1)
                with dve.Fori(1, 7) as i:
                    for j in range(2):
                        square(g, 2 * i + j + (FB * g + 1))
                        add(g, 2 * i + j)
                square(g, FB * g + 15)
                add(g, 14)
                if g == G - 1:
                    add(g, 15)
                else:
                    T0, n = GT0[g + 1], GN[g + 1]
                    norm.dve_scale(dve, chain, T0, T0 % 2)
                    for t in range(GN[g]):
                        add(g, 15, (t,))
                        if t + 1 < n:
                            norm.dve_scale(dve, chain, T0 + t + 1, (T0 + t + 1) % 2)
                        if t < n:
                            norm.dve_lo(dve, T0 + t, (T0 + t) % 2, t * P)
            final(G - 1)

        @block.tensor
        def _(pe):
            pe.wait_ge(K.ident_ready, K.ident_value)

            def up(g, E, s):
                w = PIECE[g]
                pe.wait_ge(wu_lo_ready, E + 1)
                for k in range(4):
                    m, q = k // 2, k % 2
                    if not (isinstance(E, int) and E == 0):
                        pe.wait_ge(relu_done, 4 * E + (k - 3))
                    split_products(nc, bank[k][:, 0:w],
                                   [(wu_hi[s][:, c, m * P:(m + 1) * P], wu_lo[s][:, c, m * P:(m + 1) * P],
                                     hT_hi[:, c, w * q:w * q + w], hT_lo[:, c, w * q:w * q + w]) for c in range(KC)], up_mm)

            def down(g, f, s, turn=False):
                n = GN[g]
                pe.wait_ge(wd_lo_ready, f + (FB * g + 1))
                pe.wait_ge(u_lo_ready, 4 * f + (4 * FB * g + 4))
                for t in range(n):
                    w = P if GT0[g] + t < TILES - 1 else NS
                    done = n * f + (DB[g] + t)
                    if not (isinstance(f, int) and f == 0 and t < 2):
                        pe.wait_ge(summed, done - 1 if t else done)
                    for e in range(2):
                        split_products(nc, bank[4 + 2 * (t % 2) + e][0:w, :],
                                       [(u_hi[s][:, m, t * P:t * P + w], u_lo[s][:, m, t * P:t * P + w],
                                         wd_hi[s][:, m, 512 * e:512 * e + 512], wd_lo[s][:, m, 512 * e:512 * e + 512])
                                        for m in range(2)], down_mm if e else None)
                    if turn and t < GN[g + 1]:
                        T = GT0[g + 1] + t
                        norm.pe_turn(pe, T, T % 2, False)

            for g in range(G):
                if g == 0:
                    norm.pe_group(pe, GN[0])
                pe.wait_ge(norm.lo_ready, GT0[g] + GN[g])
                up(g, FB * g, 0)
                up(g, FB * g + 1, 1)
                down(g, 0, 0)
                with pe.Fori(0, 7) as i:
                    for j in range(2):
                        up(g, 2 * i + j + (FB * g + 2), j)
                        down(g, 2 * i + j + 1, 1 - j)
                pe.wait_ge(relu_done, 4 * FB * (g + 1))
                down(g, 15, 1, turn=g < G - 1)


class Kernel:
    pass


STAGES = (project, mix_prompt, mix_sample, project_out, mlp)
INPUTS = [
    ("x", (ROWS, D)), ("norm1_g", (D,)), ("rot", (P, 2, TILES, 2 * ROT)), ("w_gate", (P, KC, 8)), ("b_gate", (8,)),
    ("w_conv", (P, 8, CONVW)), ("b_conv", (P, 8)), ("k_scale", (P, 8)), ("state_conv", (24, 2 * MW)),
    ("w_qk", (8, P, KC * P)), ("w_tok", (5, P, KC, 512)),
    ("cache_k", (DEC_B, WB, AW)), ("cache_v", (DEC_B, WB, AW)),
    ("state_C", (DEC_B, MH, MD, MD)), ("state_n", (DEC_B, MH, MD)), ("state_m", (DEC_B * MH, 1)),
    ("sample_mask", (RT, KEYS)), ("sample_count", (RT, KEYS)), ("chunk_mask", (NS, NS)), ("token_seq", (NS, DEC_B)),
    ("mh_norm_g", (MW,)), ("w_out", (P, KC, D)), ("norm2_g", (D,)),
    ("w_up", (16, P, KC, 256)), ("w_down", (16, P, 2, D)), ("norm_f_g", (D,)),
]
OUTPUTS = [
    ("y_prompt", (1, SEQ, D)), ("y_sample", (DEC_B, DEC_T, D)),
    ("win_k_prompt", (1, 1, WB, H, HD)), ("win_v_prompt", (1, 1, WB, H, HD)),
    ("conv_prompt", (1, 1, CONVW - 1, 2 * MW)), ("C_prompt", (1, 1, MH, MD, MD)),
    ("n_prompt", (1, 1, MH, MD)), ("m_prompt", (1, 1, MH)),
    ("win_k_sample", (1, DEC_B, WB, H, HD)), ("win_v_sample", (1, DEC_B, WB, H, HD)),
    ("conv_sample", (1, DEC_B, CONVW - 1, 2 * MW)), ("C_sample", (1, DEC_B, MH, MD, MD)),
    ("n_sample", (1, DEC_B, MH, MD)), ("m_sample", (1, DEC_B, MH)),
]


def hybrid_step(nc, ins, outs, debug=None):
    K = Kernel()
    K.nc, K.o = nc, outs
    K.x, K.norm1_g, K.rot, K.w_gate, K.b_gate = (ins[n] for n in ("x", "norm1_g", "rot", "w_gate", "b_gate"))
    K.w_conv, K.b_conv, K.k_scale, K.state_conv = (ins[n] for n in ("w_conv", "b_conv", "k_scale", "state_conv"))
    K.w_qk, K.w_tok, K.ins = ins["w_qk"], ins["w_tok"], ins
    K.new_conv_prompt = outs["conv_prompt"].rearrange("a b w c -> (a b w) c")
    K.new_conv_sample = outs["conv_sample"].rearrange("a b w c -> (a b w) c")

    def dram(name, shape):
        kind = "ExternalOutput" if debug and name in debug else "Internal"
        return nc.dram_tensor(name, shape, F32, kind=kind).ap()

    K.proj = dram("proj", (5, ROWS, AW))
    K.qkt = dram("qkt", (8, P, NT))
    K.dram = dram
    K.parts = dram("parts", (3, SEQ, H * (HD + 2)))
    K.mix = dram("mix", (ROWS, D))
    K.x2 = dram("x2", (ROWS, D))
    K.gate_rows = dram("gate_rows", (2, NCH * MH, P))
    K.gate_sample = dram("gate_sample", (2, DEC_B * MH, DEC_T))
    K.ng_rows = dram("ng_rows", (NCH * MH, P))
    K.ng_sample = dram("ng_sample", (DEC_B * MH, DEC_T))
    K.sm_own_kwm, K.sm_own_ms = 6, 15
    with ExitStack() as ctx:
        stage_sems = []

        def sem(name):
            stage_sems.append(nc.alloc_semaphore(name=name))
            return stage_sems[-1]

        K.sem = sem
        K.ident = ctx.enter_context(nc.sbuf_tensor("ident", [P, P], F32))
        K.tab_p = ctx.enter_context(nc.sbuf_tensor("tab_p", [P, 4, NCH * MH], F32))
        K.tab_s = ctx.enter_context(nc.sbuf_tensor("tab_s", [NS, 4, MH], F32))
        K.wti = ctx.enter_context(nc.sbuf_tensor("wti", [P, (NCH + DEC_B) * MH], F32))
        K.ident_ready, K.ident_value = ctx.enter_context(nc.semaphore("ident_ready")), 2
        with nc.Block(no_gpsimd_drain=True) as block:
            @block.gpsimd
            def _(pool):
                nc.gpsimd.memset(K.ident[:], 0.0).then_inc(K.ident_ready, 1)
                pool.wait_ge(K.ident_ready, 1)
                nc.gpsimd.affine_select(out=K.ident[:], in_=K.ident[:], compare_op=ALU.not_equal, fill=1.0, base=0,
                                        pattern=[[-1, P]], channel_multiplier=1).then_inc(K.ident_ready, 1)
        for stage in STAGES:
            stage(K)
            nc.clear_and_free_semaphores(stage_sems)
            stage_sems.clear()
            nc.all_engine_barrier()


def lay_out(i):
    c = np.ascontiguousarray
    w_in = np.asarray(i["w_in"])[0]
    cols = lambda a, n: w_in[:, a:a + n].reshape(KC, P, n).transpose(1, 0, 2)
    qk0 = 3 * AW
    x = np.zeros((ROWS, D), np.float32)
    x[0:SEQ] = np.asarray(i["x_prompt"])[0]
    x[SEQ:NT] = np.asarray(i["x_sample"]).reshape(NS, D)
    half = ROT // 2
    freq = (np.float32(500000.0) ** (-np.arange(half, dtype=np.float32) / half)).astype(np.float32)
    pos = np.zeros(ROWS, np.float32)
    pos[0:SEQ] = np.arange(SEQ)
    pos[SEQ:NT] = np.tile(4096 + np.arange(DEC_T), DEC_B)
    ang = (pos[:, None] * freq[None, :]).astype(np.float32)
    cos, sin = np.cos(ang).astype(np.float32), np.sin(ang).astype(np.float32)
    rot = np.zeros((2, ROWS, 2 * ROT), np.float32)
    rot[0] = np.concatenate([cos, cos, -sin, sin], 1)
    rot[1, :, 0:ROT] = 1.0
    ksc = np.ones((P, 8), np.float32)
    ksc[:, 4:8] = np.float32(MD ** -0.5)
    mask, count = sample_tables()
    chunk_mask, token_seq = sample_chunk_tables()
    return {
        "sample_mask": mask, "sample_count": count, "chunk_mask": chunk_mask, "token_seq": token_seq,
        "x": x, "norm1_g": c(np.asarray(i["norm1_g"])[0]),
        "rot": c(rot.reshape(2, TILES, P, 2 * ROT).transpose(2, 0, 1, 3)),
        "w_gate": c(cols(qk0 + 4 * MW, 8)), "b_gate": c(np.asarray(i["b_gate"])[0]),
        "w_conv": c(np.asarray(i["w_conv"])[0].reshape(CONVW, 8, P).transpose(2, 1, 0)),
        "b_conv": c(np.asarray(i["b_conv"])[0].reshape(8, P).T), "k_scale": ksc,
        "state_conv": c(np.asarray(i["state_conv"]).reshape(24, 2 * MW)),
        "w_qk": c(np.stack([cols(qk0 + P * k, P) for k in range(8)]).reshape(8, P, KC * P)),
        "w_tok": c(np.stack([cols(a, 512) for a in (0, AW, 2 * AW, qk0 + 3 * MW, qk0 + 2 * MW)])),
        "cache_k": c(np.asarray(i["cache_win_k"]).reshape(DEC_B, WB, AW)),
        "cache_v": c(np.asarray(i["cache_win_v"]).reshape(DEC_B, WB, AW)),
        "state_C": c(np.asarray(i["state_C"])[0]), "state_n": c(np.asarray(i["state_n"])[0]),
        "state_m": c(np.asarray(i["state_m"]).reshape(DEC_B * MH, 1)),
        "mh_norm_g": c(np.asarray(i["mh_norm_g"])[0]),
        "w_out": c(np.asarray(i["w_out"])[0].reshape(KC, P, D).transpose(1, 0, 2)),
        "norm2_g": c(np.asarray(i["norm2_g"])[0]),
        "w_up": c(np.asarray(i["w_up"])[0].reshape(KC, P, 16, 256).transpose(2, 1, 0, 3)),
        "w_down": c(np.asarray(i["w_down"])[0].reshape(16, 2, P, D).transpose(0, 2, 1, 3)),
        "norm_f_g": c(np.asarray(i["norm_f_g"])),
    }


def kernel(**inputs):
    import concourse.bacc as _bacc
    from concourse.bass_utils import run_bass_kernel_spmd as _run

    nc = _bacc.Bacc("TRN2", target_bir_lowering=False, num_devices=1)
    arrays = {"in_" + n: a for n, a in lay_out(inputs).items()}
    ins = {n: nc.dram_tensor("in_" + n, s, F32, kind="ExternalInput").ap() for n, s in INPUTS}
    outs = {n: nc.dram_tensor("out_" + n, s, F32, kind="ExternalOutput").ap() for n, s in OUTPUTS}
    hybrid_step(nc, ins, outs)
    r = _run(nc, [arrays], core_ids=[0])
    return tuple(r.results[0]["out_" + n] for n, _ in OUTPUTS)
```
